# Optimizing a Trainium2 kernel written in Bass

```python
import math
import jax, jax.numpy as jnp
from jax import lax
import numpy as np

D_MODEL = 1024
BATCH = 1
SEQ = 512
DEPTH = 2
DEC_BATCH = 8
DEC_SEQ = 8
PAST_LEN = 2048
PAGE_SIZE = 128

N_MIXERS = 2
N_MLA_LAYERS = (DEPTH + N_MIXERS - 1) // N_MIXERS
N_SSM_LAYERS = DEPTH // N_MIXERS
N_HEADS = 16
D_NOPE = 64
D_ROPE = 32
D_V = 64
Q_LORA = 512
KV_LORA = 256
ROPE_THETA = 10000.0
Q_BLOCK = 128
D_IN_MLA = Q_LORA + KV_LORA + D_ROPE
GROUP_SIZE = 16
N_GROUPS = D_MODEL // GROUP_SIZE
STATE_DIM = 64
DT_MIN = 1e-3
DT_MAX = 1e-1
D_FF = 4 * D_MODEL
EPS = 1e-6

kernel_name = "hybrid_mla_s5_decoder_step"

def _rmsnorm(x, g):
    xf = x.astype(jnp.float32)
    y = xf * lax.rsqrt(jnp.mean(xf * xf, axis=-1, keepdims=True) + EPS)
    return (y * g.astype(jnp.float32)).astype(x.dtype)

def _rope_tables(pos):
    half = D_ROPE // 2
    inv = ROPE_THETA ** (-jnp.arange(half, dtype=jnp.float32) / half)
    ang = pos.astype(jnp.float32)[:, None] * inv[None, :]
    return jnp.cos(ang), jnp.sin(ang)

def _apply_rope(x, cos, sin):
    half = D_ROPE // 2
    xf = x.astype(jnp.float32)
    x1, x2 = xf[..., :half], xf[..., half:]
    return jnp.concatenate([x1 * cos - x2 * sin, x2 * cos + x1 * sin], axis=-1).astype(x.dtype)

def _mla_project(h, pos, w_in, g_q, g_kv, w_q_up):
    B, L, _ = h.shape
    proj = h @ w_in
    c_q = _rmsnorm(proj[..., :Q_LORA], g_q)
    c_kv = _rmsnorm(proj[..., Q_LORA:Q_LORA + KV_LORA], g_kv)
    k_pe = proj[..., Q_LORA + KV_LORA:]
    q = (c_q @ w_q_up).reshape(B, L, N_HEADS, D_NOPE + D_ROPE)
    cos, sin = _rope_tables(pos)
    q_nope = q[..., :D_NOPE]
    q_pe = _apply_rope(q[..., D_NOPE:], cos[:, None, :], sin[:, None, :])
    k_pe = _apply_rope(k_pe, cos, sin)
    return q_nope, q_pe, c_kv, k_pe

def _mla_prompt(h, w_in, g_q, g_kv, w_q_up, w_kv_up, w_o):
    B, L, _ = h.shape
    pos = jnp.arange(L, dtype=jnp.int32)
    q_nope, q_pe, c_kv, k_pe = _mla_project(h, pos, w_in, g_q, g_kv, w_q_up)
    kv = (c_kv @ w_kv_up).reshape(B, L, N_HEADS, D_NOPE + D_V)
    k_nope, v = kv[..., :D_NOPE], kv[..., D_NOPE:]
    scale = (D_NOPE + D_ROPE) ** -0.5
    outs = []
    for blk in range(L // Q_BLOCK):
        q0, q1 = blk * Q_BLOCK, (blk + 1) * Q_BLOCK
        s = (jnp.einsum('bqhn,bkhn->bhqk', q_nope[:, q0:q1], k_nope[:, :q1])
             + jnp.einsum('bqhd,bkd->bhqk', q_pe[:, q0:q1], k_pe[:, :q1])).astype(jnp.float32) * scale
        mask = pos[q0:q1, None] >= pos[None, :q1]
        p = jax.nn.softmax(jnp.where(mask, s, -jnp.inf), axis=-1).astype(v.dtype)
        outs.append(jnp.einsum('bhqk,bkhv->bqhv', p, v[:, :q1]))
    o = jnp.concatenate(outs, axis=1).reshape(B, L, N_HEADS * D_V)
    return o @ w_o, c_kv, k_pe

def _mla_sample(h, ckv_pool, kpe_pool, page_table, w_in, g_q, g_kv, w_q_up, w_kv_up, w_o):
    B, L, _ = h.shape
    past = page_table.shape[1] * PAGE_SIZE
    pos = past + jnp.arange(L, dtype=jnp.int32)
    q_nope, q_pe, c_kv, k_pe = _mla_project(h, pos, w_in, g_q, g_kv, w_q_up)
    w_kv = w_kv_up.reshape(KV_LORA, N_HEADS, D_NOPE + D_V)
    w_uk, w_uv = w_kv[..., :D_NOPE], w_kv[..., D_NOPE:]
    q_lat = jnp.einsum('bqhn,rhn->bqhr', q_nope, w_uk)
    ckv_past = ckv_pool[page_table].reshape(B, past, KV_LORA)
    kpe_past = kpe_pool[page_table].reshape(B, past, D_ROPE)
    scale = (D_NOPE + D_ROPE) ** -0.5
    s_past = (jnp.einsum('bqhr,bkr->bhqk', q_lat, ckv_past)
              + jnp.einsum('bqhd,bkd->bhqk', q_pe, kpe_past)).astype(jnp.float32) * scale
    s_new = (jnp.einsum('bqhr,bkr->bhqk', q_lat, c_kv)
             + jnp.einsum('bqhd,bkd->bhqk', q_pe, k_pe)).astype(jnp.float32) * scale
    causal = jnp.tril(jnp.ones((L, L), dtype=bool))
    s = jnp.concatenate([s_past, jnp.where(causal, s_new, -jnp.inf)], axis=-1)
    p = jax.nn.softmax(s, axis=-1).astype(c_kv.dtype)
    o_lat = (jnp.einsum('bhqk,bkr->bqhr', p[..., :past], ckv_past)
             + jnp.einsum('bhqk,bkr->bqhr', p[..., past:], c_kv))
    o = jnp.einsum('bqhr,rhv->bqhv', o_lat, w_uv).reshape(B, L, N_HEADS * D_V)
    return o @ w_o, c_kv, k_pe

def _s5(h, h0_re, h0_im, a_re, a_im, log_dt, b_re, b_im, c_re, c_im, d, w_glu):
    B, L, D = h.shape
    a = lax.complex(a_re.astype(jnp.float32), a_im.astype(jnp.float32))
    dta = jnp.exp(log_dt.astype(jnp.float32))[:, None] * a
    a_bar = jnp.exp(dta)
    b = lax.complex(b_re.astype(jnp.float32), b_im.astype(jnp.float32))
    b_bar = ((a_bar - 1.0) / a)[..., None] * b
    u = h.astype(jnp.float32).reshape(B, L, N_GROUPS, GROUP_SIZE)
    bu = jnp.einsum('blgs,gps->blgp', u.astype(jnp.complex64), b_bar)
    a_seq = jnp.broadcast_to(a_bar, bu.shape)

    def combine(e1, e2):
        a1, x1 = e1
        a2, x2 = e2
        return a2 * a1, a2 * x1 + x2

    _, states = lax.associative_scan(combine, (a_seq, bu), axis=1)
    if h0_re is not None:
        h0 = lax.complex(h0_re.astype(jnp.float32), h0_im.astype(jnp.float32))
        t = jnp.arange(1, L + 1, dtype=jnp.float32)
        decay = jnp.exp(t[:, None, None] * dta)
        states = states + decay[None] * h0[:, None]
    c = lax.complex(c_re.astype(jnp.float32), c_im.astype(jnp.float32))
    y = jnp.real(jnp.einsum('gsp,blgp->blgs', c, states)).reshape(B, L, D)
    y = (y + d.astype(jnp.float32) * h.astype(jnp.float32)).astype(h.dtype)
    g = jax.nn.gelu(y)
    ab = g @ w_glu
    out = ab[..., :D] * jax.nn.sigmoid(ab[..., D:])
    final = states[:, -1]
    return out, jnp.real(final), jnp.imag(final)

def _mlp(h, w1, w2):
    z = jax.nn.relu(h @ w1)
    return (z * z) @ w2

def setup_inputs(seed: int = 0) -> dict:
    key = jax.random.key(seed)
    ks = jax.random.split(key, 32)
    f32 = jnp.float32
    n_pages = PAST_LEN // PAGE_SIZE
    n_used = DEC_BATCH * n_pages
    n_phys = n_used + n_used // 4
    nrm = lambda k, shape, s: jax.random.normal(k, shape, f32) * s
    perm = jax.random.permutation(ks[0], n_phys)
    page_table = perm[:n_used].reshape(DEC_BATCH, n_pages).astype(jnp.int32)
    n_idx = jnp.arange(STATE_DIM, dtype=f32)
    return {
        "x_prompt": nrm(ks[1], (BATCH, SEQ, D_MODEL), 1.0),
        "x_sample": nrm(ks[2], (DEC_BATCH, DEC_SEQ, D_MODEL), 1.0),
        "cache_ckv": nrm(ks[3], (N_MLA_LAYERS, n_phys, PAGE_SIZE, KV_LORA), 1.0),
        "cache_kpe": nrm(ks[4], (N_MLA_LAYERS, n_phys, PAGE_SIZE, D_ROPE), 1.0),
        "state_ssm_re": nrm(ks[5], (N_SSM_LAYERS, DEC_BATCH, N_GROUPS, STATE_DIM), 0.5),
        "state_ssm_im": nrm(ks[6], (N_SSM_LAYERS, DEC_BATCH, N_GROUPS, STATE_DIM), 0.5),
        "page_table": page_table,
        "norm_mix": 1.0 + nrm(ks[7], (DEPTH, D_MODEL), 0.02),
        "norm_mlp": 1.0 + nrm(ks[8], (DEPTH, D_MODEL), 0.02),
        "norm_final": 1.0 + nrm(ks[9], (D_MODEL,), 0.02),
        "mla_w_in": nrm(ks[10], (N_MLA_LAYERS, D_MODEL, D_IN_MLA), D_MODEL ** -0.5),
        "mla_q_norm": 1.0 + nrm(ks[11], (N_MLA_LAYERS, Q_LORA), 0.02),
        "mla_kv_norm": 1.0 + nrm(ks[12], (N_MLA_LAYERS, KV_LORA), 0.02),
        "mla_w_q_up": nrm(ks[13], (N_MLA_LAYERS, Q_LORA, N_HEADS * (D_NOPE + D_ROPE)), Q_LORA ** -0.5),
        "mla_w_kv_up": nrm(ks[14], (N_MLA_LAYERS, KV_LORA, N_HEADS * (D_NOPE + D_V)), KV_LORA ** -0.5),
        "mla_w_o": nrm(ks[15], (N_MLA_LAYERS, N_HEADS * D_V, D_MODEL), (N_HEADS * D_V) ** -0.5),
        "ssm_a_re": -0.5 + nrm(ks[16], (N_SSM_LAYERS, N_GROUPS, STATE_DIM), 0.01),
        "ssm_a_im": math.pi * n_idx + nrm(ks[17], (N_SSM_LAYERS, N_GROUPS, STATE_DIM), 0.01),
        "ssm_log_dt": jax.random.uniform(ks[18], (N_SSM_LAYERS, N_GROUPS), f32, math.log(DT_MIN), math.log(DT_MAX)),
        "ssm_b_re": nrm(ks[19], (N_SSM_LAYERS, N_GROUPS, STATE_DIM, GROUP_SIZE), (2 * GROUP_SIZE) ** -0.5),
        "ssm_b_im": nrm(ks[20], (N_SSM_LAYERS, N_GROUPS, STATE_DIM, GROUP_SIZE), (2 * GROUP_SIZE) ** -0.5),
        "ssm_c_re": nrm(ks[21], (N_SSM_LAYERS, N_GROUPS, GROUP_SIZE, STATE_DIM), (2 * STATE_DIM) ** -0.5),
        "ssm_c_im": nrm(ks[22], (N_SSM_LAYERS, N_GROUPS, GROUP_SIZE, STATE_DIM), (2 * STATE_DIM) ** -0.5),
        "ssm_d": nrm(ks[23], (N_SSM_LAYERS, D_MODEL), 1.0),
        "ssm_w_glu": nrm(ks[24], (N_SSM_LAYERS, D_MODEL, 2 * D_MODEL), D_MODEL ** -0.5),
        "mlp_w1": nrm(ks[25], (DEPTH, D_MODEL, D_FF), D_MODEL ** -0.5),
        "mlp_w2": nrm(ks[26], (DEPTH, D_FF, D_MODEL), D_FF ** -0.5),
    }

def reference(x_prompt, x_sample, cache_ckv, cache_kpe, state_ssm_re, state_ssm_im, page_table,
              norm_mix, norm_mlp, norm_final, mla_w_in, mla_q_norm, mla_kv_norm, mla_w_q_up,
              mla_w_kv_up, mla_w_o, ssm_a_re, ssm_a_im, ssm_log_dt, ssm_b_re, ssm_b_im, ssm_c_re,
              ssm_c_im, ssm_d, ssm_w_glu, mlp_w1, mlp_w2):
    xp, xs = x_prompt, x_sample
    p_ckv, p_kpe, p_re, p_im = [], [], [], []
    s_ckv, s_kpe, s_re, s_im = [], [], [], []
    for i in range(DEPTH):
        j = i // N_MIXERS
        hp = _rmsnorm(xp, norm_mix[i])
        hs = _rmsnorm(xs, norm_mix[i])
        if i % N_MIXERS == 0:
            w = (mla_w_in[j], mla_q_norm[j], mla_kv_norm[j], mla_w_q_up[j], mla_w_kv_up[j], mla_w_o[j])
            op, ckv_p, kpe_p = _mla_prompt(hp, *w)
            osm, ckv_s, kpe_s = _mla_sample(hs, cache_ckv[j], cache_kpe[j], page_table, *w)
            p_ckv.append(ckv_p); p_kpe.append(kpe_p)
            s_ckv.append(ckv_s); s_kpe.append(kpe_s)
        else:
            w = (ssm_a_re[j], ssm_a_im[j], ssm_log_dt[j], ssm_b_re[j], ssm_b_im[j],
                 ssm_c_re[j], ssm_c_im[j], ssm_d[j], ssm_w_glu[j])
            op, re_p, im_p = _s5(hp, None, None, *w)
            osm, re_s, im_s = _s5(hs, state_ssm_re[j], state_ssm_im[j], *w)
            p_re.append(re_p); p_im.append(im_p)
            s_re.append(re_s); s_im.append(im_s)
        xp = xp + op
        xs = xs + osm
        xp = xp + _mlp(_rmsnorm(xp, norm_mlp[i]), mlp_w1[i], mlp_w2[i])
        xs = xs + _mlp(_rmsnorm(xs, norm_mlp[i]), mlp_w1[i], mlp_w2[i])
    y_prompt = _rmsnorm(xp, norm_final)
    y_sample = _rmsnorm(xs, norm_final)
    return (y_prompt, y_sample,
            jnp.stack(p_ckv), jnp.stack(p_kpe), jnp.stack(p_re), jnp.stack(p_im),
            jnp.stack(s_ckv), jnp.stack(s_kpe), jnp.stack(s_re), jnp.stack(s_im))


_drawn_inputs = setup_inputs


def setup_inputs(seed=0):
    import zlib

    import numpy as np

    out = dict(_drawn_inputs(seed))
    spreads = {}
    factors = {'norm_final': 22.813,
     'mla_q_norm': 8.0,
     'mla_kv_norm': 2.991,
     'ssm_a_re': 45.904,
     'norm_mlp': 3.376,
     'ssm_c_re': 8.0,
     'ssm_c_im': 8.0}
    for name, (base, spread) in spreads.items():
        noise = np.random.default_rng([zlib.crc32(name.encode()), seed]).standard_normal(out[name].shape)
        drawn = base * np.exp(spread * noise) if base else spread * noise
        out[name] = __import__('jax').numpy.asarray(drawn.astype(out[name].dtype))
    for name, factor in factors.items():
        out[name] = (out[name] * factor).astype(out[name].dtype)
    return out
```

```python
from contextlib import ExitStack
import math

import concourse.bass as bass
from concourse import mybir
from concourse.alu_op_type import AluOpType as ALU

F32 = mybir.dt.float32
F32R = mybir.dt.float32r
I32 = mybir.dt.int32
ACT = mybir.ActivationFunctionType
AX = mybir.AxisListType
ds = bass.ds

P = 128
D = 1024
KT = D // P
SEQ, DEC_B, DEC_Q = 512, 8, 8
NS = DEC_B * DEC_Q
N = SEQ + NS
HALF = N // 2
HEADS, NOPE, ROPE, DV = 16, 64, 32, 64
QL_D, KV_D = 512, 256
HD = NOPE + ROPE
SCALE = HD ** -0.5
PAIRS = HEADS // 2
BLK = SEQ // P
PAGES, PAGE = 16, 128
PAST = PAGES * PAGE
FF = 4 * D
EPS = 1e-6
NEG = -1e30

GROUPS, GS, ST = 64, 16, 64
GP = GROUPS // 2
T = 8
NC = N // T
PC = SEQ // T
QC = 4

RAW = 4
CUT = 2
HI, LO = 0, 1
PASSES = ((HI, (HI, LO)), (LO, (HI,)))

V_MIX, V_MLP, V_FIN, V_Q, V_KV, V_D = 0, 16, 32, 40, 44, 46
VROWS = 54


CREDIT = 1


class Tally:

    def __init__(self, sem):
        self.sem, self.n, self.i, self.stride, self.k = sem, 0, None, 0, 0

    def add(self, k=1):
        if self.i is None:
            self.n += k
        else:
            self.k += k

    def now(self, back=0):
        if self.i is None:
            return self.n - back
        return self.i * self.stride + (self.n + self.k - back)

    def enter(self, i, stride):
        self.i, self.stride, self.k = i, stride, 0

    def leave(self, count):
        assert self.k == self.stride, (self.k, self.stride)
        self.n += count * self.stride
        self.i = None


def build(nc, I, O):
    ctx = ExitStack()
    with ctx:
        def sb(name, shape, dt=F32):
            return ctx.enter_context(nc.sbuf_tensor(name, shape, dt))

        def sem(name):
            return ctx.enter_context(nc.semaphore(name))

        def sb_with_parts(name, shape, parts_shape, parts_dt):
            base = (nc.sbuf_base + 31) // 32 * 32
            whole = sb(name, shape)
            return whole, nc.alloc_sbuf_tensor_at(name + "_parts", parts_shape, parts_dt, offset=base)

        arena, zR = sb_with_parts("arena", [P, 18432], [P, FF // P // 2, 2, N], F32R)
        side, hR = sb_with_parts("side", [P, 2 * KT * N], [P, KT, 2, N], F32R)
        xT = sb("xT", [P, KT, N])
        hT = sb("hT", [P, KT, N])
        wraw = sb("wraw", [P, RAW, 8, P])
        wR = sb("wR", [P, CUT, 2, 8, P], F32R)
        yblk = sb("yblk", [P, 2, T, P])
        ident = sb("ident", [P, P])
        ones = sb("ones", [P, P])
        ropeq = sb("ropeq", [P, N])
        ropek = sb("ropek", [P, N])
        cmask = sb("cmask", [P, P])
        nmask = sb("nmask", [P, DEC_Q])
        vecs = sb("vecs", [P, VROWS])
        sq = sb("sq", [P, 2, N])
        kpR = sb("kpR", [P, N])
        acc = sb("acc", [P, N])
        rstd = sb("rstd", [P, N])
        tmpa = sb("tmpa", [P, 2, N])
        a8 = sb("a8", [P, 3, GP])
        stat = sb("stat", [P, 32])
        ptab = sb("ptab", [1, DEC_B * PAGES], I32)

        offset = [0]

        def view(n):
            offset[0] += n
            assert offset[0] <= 18432, offset[0]
            return arena[:, offset[0] - n:offset[0]]

        in_arena = view
        ckvT = view(2 * N).rearrange("p (r n) -> p r n", r=2)
        QL = view(2 * 1024).rearrange("p (r n) -> p r n", r=2)
        QPE = view(1024)
        OLT = view(2 * 1024).rearrange("p (r b n) -> p r b n", r=2, b=DEC_B)
        CN = view(2048).rearrange("p (b n) -> p b n", b=DEC_B)
        KP = view(2 * PAGES * ROPE).rearrange("p (a g n) -> p a g n", a=2, g=PAGES)
        mark = offset[0]
        cqT = view(4 * N).rearrange("p (r n) -> p r n", r=4)
        qT = view(2 * N).rearrange("p (h n) -> p h n", h=2)
        kT = view(2 * SEQ).rearrange("p (h n) -> p h n", h=2)
        V = view(BLK * P).rearrange("p (t n) -> p t n", t=BLK)
        wq = view(4 * 2 * P).rearrange("p (k h n) -> p k h n", k=4, h=2)
        wkv = view(2 * 2 * P).rearrange("p (r c h n) -> p r c h n", r=2, c=2, h=2)
        ukT = view(4 * P).rearrange("p (a n) -> p a n", a=4)
        prob = view(2 * SEQ).rearrange("p (a n) -> p a n", a=2)
        probT = view(2 * SEQ).rearrange("p (a t n) -> p a t n", a=2, t=BLK)
        offset[0] = mark
        SW = PAST + DEC_Q
        S = view(2 * SW).rearrange("p (a n) -> p a n", a=2)
        PT = view(PAST).rearrange("p (g n) -> p g n", g=PAGES)
        PTN = view(P)
        cT = view(2 * 2 * 256).rearrange("p (a r n) -> p a r n", a=2, r=2)
        kpT = view(2 * 256).rearrange("p (a n) -> p a n", a=2)
        QLb = view(2 * 256).rearrange("p (a r n) -> p a r n", a=2, r=2)
        QPb = view(2 * P).rearrange("p (a n) -> p a n", a=2)
        OLn = view(256)
        pages = side[:, 0:8192].rearrange("p (a g n) -> p a g n", a=2, g=PAGES)
        kpeN = sq[:, 0, 0:NS]
        kpeNat = sq[:, 1, 0:(BLK + 1) * ROPE].rearrange("p (t n) -> p t n", n=ROPE)
        ckvNat = tmpa[:, :, 0:512].rearrange("p a (t n) -> p a t n", t=2)
        wkvf = wraw[:, 0:4, :, :].rearrange("p a k n -> p (a k n)").rearrange("p (r n) -> p r n", r=2)
        hid = sq
        offset[0] = 0
        xnat = view((BLK + 1) * D).rearrange("p (t n) -> p t n", n=D)
        nat = view(30 * P).rearrange("p (a n) -> p a n", a=30)
        PW = view(20 * GP).rearrange("p (a q) -> p a q", a=20)
        Bn = view(2 * GP * GS).rearrange("p (a q i) -> p a q i", a=2, q=GP)
        Cn = view(2 * 8 * ST).rearrange("p (a t n) -> p a t n", a=2, t=8)
        Cp = view(2 * GP * GS).rearrange("p (a q i) -> p a q i", a=2, q=GP)
        bb = view(2 * QC * GS).rearrange("p (a q i) -> p a q i", a=2, q=QC)
        Y = view(2 * QC * P).rearrange("p (a q n) -> p a q n", a=2, q=QC)
        CA = view(2 * QC * 9 * GS).rearrange("p (a q k o) -> p a q k o", a=2, q=QC, k=9)
        tm = view(4 * QC * 9 * GS).rearrange("p (a n) -> p a n", a=4)
        offset[0] = 0
        view = lambda n: (offset.__setitem__(0, offset[0] + n), side[:, offset[0] - n:offset[0]])[1]
        bstc = view(2 * QC * P).rearrange("p (a q n) -> p a q n", a=2, q=QC)
        kdc = view(2 * QC * P).rearrange("p (q a n) -> p q a n", a=2, q=QC)
        vrow = view(P)
        offset[0] = 0
        view = in_arena
        U = view(GROUPS * NC).rearrange("p (g c) -> p g c", g=GROUPS)
        Z = view(NC * 2 * GP).rearrange("p (c a q) -> p c a q", a=2, q=GP)
        XF = view((DEC_B + 1) * 2 * GP).rearrange("p (c a q) -> p c a q", a=2, q=GP)
        BC = view(2 * GP * P).rearrange("p (a q n) -> p a q n", a=2, q=GP)
        MI = side[:, 0:8192].rearrange("p (g n) -> p g n", g=GROUPS)
        h0n = yblk[:, 0, 0:4, :]
        XG = tmpa[:, 0, :].rearrange("p (a c q) -> p a c q", a=2, q=GP)

        bank01 = ctx.enter_context(nc.psum_tensor("bank01", [P, 2, 512], F32))
        bank23 = ctx.enter_context(nc.psum_tensor("bank23", [P, 2, 512], F32))
        bank45 = ctx.enter_context(nc.psum_tensor("bank45", [P, 2, 512], F32))
        bank6 = ctx.enter_context(nc.psum_tensor("bank6", [P, 512], F32))
        bank7 = ctx.enter_context(nc.psum_tensor("bank7", [P, 512], F32))
        pair = [bank01, bank23]

        BSTD = nc.dram_tensor("s5_in_to_state", (P, 2, GP, P), F32, kind="Internal").ap()
        CSD = nc.dram_tensor("s5_state_to_out", (P, 2, GP, P), F32, kind="Internal").ap()
        KD = nc.dram_tensor("s5_lag_kernels", (GROUPS, GS, P), F32, kind="Internal").ap()
        HDR = nc.dram_tensor("s5_input", (D, T, NC), F32, kind="Internal").ap()

        ones_set = sem("ones_set")
        waited = sem("waited")
        const_in = sem("const_in")
        x_in = sem("x_in")
        s5_in = sem("s5_in")
        vec_done = sem("vec_done")
        vec_sb = sem("vec_sb")
        w_loaded = [sem(f"w_loaded{s}") for s in range(RAW)]
        w_hi = sem("w_hi")
        w_lo = sem("w_lo")
        blk_done = sem("blk_done")
        h_hi, h_lo = sem("h_hi"), sem("h_lo")
        z_hi, z_lo = sem("z_hi"), sem("z_lo")
        tile_done = sem("tile_done")
        tile_free = sem("tile_free")
        sq_ready = sem("sq_ready")
        sq_used = sem("sq_used")
        ss_done = sem("ss_done")
        var_ready = sem("var_ready")
        rstd_ready = sem("rstd_ready")
        h_ready = sem("h_ready")
        z_ready = sem("z_ready")
        sig_ready = sem("sig_ready")
        x_new = sem("x_new")
        dstep = sem("dstep")
        dprep = sem("dprep")
        astep = sem("astep")
        kpe_raw = sem("kpe_raw")
        nat_done, nat_sb, nat_out = sem("nat_done"), sem("nat_sb"), sem("nat_out")
        hw_in, hw_swap = sem("hw_in"), sem("hw_swap")
        q_done, qn_sb, qr_sb = sem("q_done"), sem("qn_sb"), sem("qr_sb")
        k_done, k_sb, v_done, v_sb = sem("k_done"), sem("k_sb"), sem("v_done"), sem("v_sb")
        uk_done, uk_sb, ql_done, ql_sb = sem("uk_done"), sem("uk_sb"), sem("ql_done"), sem("ql_sb")
        s_done, nm_ready, p_exp, p_sb = sem("s_done"), sem("nm_ready"), sem("p_exp"), sem("p_sb")
        t_done, pt_sb, pv_done, o_sb = sem("t_done"), sem("pt_sb"), sem("pv_done"), sem("o_sb")
        tab_in = sem("tab_in")
        page_in = [sem("page_in0"), sem("page_in1")]
        qb_ready = sem("qb_ready")
        ct_done, ct_sb, kp_sb = sem("ct_done"), sem("ct_sb"), sem("kp_sb")
        sc_done, sc_sb, gm_done, dm_ready, d_exp = (sem("sc_done"), sem("sc_sb"), sem("gm_done"),
                                                    sem("dm_ready"), sem("d_exp"))
        dt_done, dt_sb, ov_done, ol_sb, olt_done, olt_sb = (
            sem("dt_done"), sem("dt_sb"), sem("ov_done"), sem("ol_sb"), sem("olt_done"), sem("olt_sb"))
        wkvf_in, os_done, os_sb = sem("wkvf_in"), sem("os_done"), sem("os_sb")
        pw_done, pw_sb, c_done, c_sb = sem("pw_done"), sem("pw_sb"), sem("c_done"), sem("c_sb")
        y_ready, yt_done, yt_sb, kd_done, kd_sb = (sem("y_ready"), sem("yt_done"), sem("yt_sb"),
                                                   sem("kd_done"), sem("kd_sb"))
        ca_ready, prep_out, prep_left = sem("ca_ready"), sem("prep_out"), sem("prep_left")
        hd_out, u_in, mi_zero, mi_in, bst_in, cs_in, h0_in = (
            sem("hd_out"), sem("u_in"), sem("mi_zero"), sem("mi_in"), sem("bst_in"), sem("cs_in"),
            sem("h0_in"))
        xs_done, xs_sb, h0_done, z_state = sem("xs_done"), sem("xs_sb"), sem("h0_done"), sem("z_state")
        h0_sb = sem("h0_sb")
        yc_done, yc_sb, yb_done, yb_sb, g_sb = (sem("yc_done"), sem("yc_sb"), sem("yb_done"),
                                                sem("yb_sb"), sem("g_sb"))
        f_ready, f_done, f_sb = sem("f_ready"), sem("f_done"), sem("f_sb")
        out_sem, aprep = sem("out_sem"), sem("aprep")
        y_out = [sem("y_out0"), sem("y_out1")]

        B_A = 0
        B_B = B_A + 7
        B_MLP = [B_B + 8, B_B + 8 + 64 + 16]
        B_GLU = B_MLP[0] + 64
        B_END = B_MLP[1] + 64
        T_X, T_A = 0, 8
        T_B = T_A + 7
        T_MLP = [T_B + 8, T_B + 8 + 48 + 16]
        T_GLU = T_MLP[0] + 48
        T_OUT = T_MLP[1] + 48
        R_A, R_B, R_MLP, R_GLU, R_END = 0, 8, [16, 32], 24, 40
        Q_MIX0, Q_CQ, Q_CKV, Q_MLP0, Q_MIX1, Q_MLP1, Q_FIN, Q_END = 0, 8, 12, 14, 22, 30, 38, 46
        H_MIX0, H_CQ, H_CKV, H_MLP0, H_MIX1, H_MLP1, H_FIN = 0, 8, 12, 14, 22, 30, 38

        def loads(n, raw):
            extra = 32 if raw == 6 % RAW else 0
            if isinstance(n, int):
                return 16 * (n // RAW + 1) + (extra if n >= 6 else 0)
            return n * (16 // RAW) + (16 - (16 // RAW) * raw + extra)

        def halves(t):
            return t.rearrange("p (a n) -> p a n", a=2)

        def row(t, m):
            if isinstance(m, int):
                return t[:, m, :]
            return t[:, ds(m, 1), :].rearrange("p o n -> p (o n)")

        def part_of(t, m, which):
            if isinstance(m, int):
                return t[:, m, which, :]
            return t[:, ds(m, 1), which, :].rearrange("p o n -> p (o n)")

        w_in = I["mla_w_in"][0].rearrange("(k p) n -> p k n", p=P)
        w_qup = I["mla_w_q_up"][0].rearrange("(k p) n -> p k n", p=P)
        w_kvup = I["mla_w_kv_up"][0].rearrange("(r p) n -> p r n", p=P)
        w_o = I["mla_w_o"][0].rearrange("(k p) n -> p k n", p=P)
        w_glu = I["ssm_w_glu"][0].rearrange("(k p) n -> p k n", p=P)
        w_up = [I["mlp_w1"][i].rearrange("(k p) n -> p k n", p=P) for i in range(2)]
        w_down = [I["mlp_w2"][i].rearrange("(k p) n -> p k n", p=P) for i in range(2)]

        def col(w, k0, m):
            return w[:, k0:k0 + 8, m * P:(m + 1) * P] if isinstance(m, int) else w[:, k0:k0 + 8, ds(m * P, P)]

        def apart(eng):
            eng.sem_inc(waited, 1)

        block = ctx.enter_context(nc.Block())

        @block.sync
        def _(sp):
            def load_block(n, src, slot=None):
                slot = n % RAW if slot is None else slot
                sp.wait_ge(w_hi, n - RAW + 1)
                sp.wait_ge(w_lo, n - RAW + 1)
                sp.dma_start(wraw[:, slot, :, :], src).then_inc(w_loaded[slot], 16)

            sp.dma_start(ident[:, :], I["c_ident"]).then_inc(const_in, 16)
            sp.dma_start(ropeq[64:128, :], I["c_ropeq"]).then_inc(const_in, 16)
            sp.dma_start(ropek[64:128, :], I["c_ropek"]).then_inc(const_in, 16)
            sp.dma_start(cmask[:, :], I["c_cmask"]).then_inc(const_in, 16)
            sp.dma_start(nmask[:, :], I["c_nmask"]).then_inc(const_in, 16)
            at = 0
            for name, k in (("norm_mix", 16), ("norm_mlp", 16), ("norm_final", 8), ("mla_q_norm", 4),
                            ("mla_kv_norm", 2), ("ssm_d", 8)):
                a = I[name]
                if len(a.shape) == 2:
                    a = a.rearrange("a b -> (a b)")
                sp.dma_start(vrow[at:at + k, :], a.rearrange("(k p) -> k p", p=P)).then_inc(const_in, 16)
                at += k
            sp.dma_start(ptab[:, :], I["page_table"].rearrange("a b -> (a b)").rearrange("(o n) -> o n", o=1))\
                .then_inc(tab_in, 16)
            sp.dma_start(xnat[:, 0:BLK, :], I["x_prompt"][0].rearrange("(t p) n -> p t n", p=P)).then_inc(x_in, 16)
            sp.dma_start(xnat[0:NS, BLK, :], I["x_sample"].rearrange("b q n -> (b q) n")).then_inc(x_in, 16)
            for m in range(4):
                sp.dma_start(wraw[:, m, :, :], col(w_in, 0, m)).then_inc(w_loaded[m], 16)
            flat = lambda a: a[0].rearrange("g p -> (g p)").rearrange("(q n) -> q n", n=P)
            sp.dma_start(nat[0:GP, 0, :], flat(I["ssm_a_re"])).then_inc(s5_in, 16)
            sp.dma_start(nat[0:GP, 1, :], flat(I["ssm_a_im"])).then_inc(s5_in, 16)
            sp.dma_start(nat[0:GP, 2, 0:2], I["ssm_log_dt"][0].rearrange("(q a) -> q a", a=2)).then_inc(s5_in, 16)
            for a, part in enumerate(("re", "im")):
                sp.dma_start(Bn[:, a, :, :], I[f"ssm_b_{part}"][0].rearrange("g p i -> (g p) i")
                             .rearrange("(q n) i -> n q i", n=P)).then_inc(s5_in, 16)
                sp.dma_start(Cn[:, a, :, :], I[f"ssm_c_{part}"][0].rearrange("g o p -> (g o) p")
                             .rearrange("(t m) p -> m t p", m=P)).then_inc(s5_in, 16)
            for m in (4, 5):
                load_block(m, col(w_in, 0, m))
            sp.wait_ge(w_hi, 3)
            sp.wait_ge(w_lo, 3)
            c0 = QL_D + KV_D
            sp.dma_start(wraw[:, 2, :, 64:96], w_in[:, :, c0:c0 + 32]).then_inc(w_loaded[2], 16)
            sp.dma_start(wraw[:, 2, :, 96:112], w_in[:, :, c0 + 16:c0 + 32]).then_inc(w_loaded[2], 16)
            sp.dma_start(wraw[:, 2, :, 112:128], w_in[:, :, c0:c0 + 16]).then_inc(w_loaded[2], 16)
            sp.wait_ge(prep_left, GP // QC + CREDIT)
            sp.wait_ge(tile_free, T_X + 8)

            def pair_weights(p):
                for h in range(2):
                    sp.dma_start(wq[:, :, h, 0:HD], w_qup[:, :, ds(p * (2 * HD) + h * HD, HD)]).then_inc(hw_in, 16)
                for r in range(2):
                    for c in range(2):
                        sp.dma_start(wkv[:, r, c, :, :],
                                     w_kvup[:, r, ds(p * (2 * P), 2 * P)].rearrange("p (h c n) -> p c h n", h=2, c=2)
                                     [:, c]).then_inc(hw_in, 16)

            with sp.Fori(0, PAIRS) as p:
                sp.wait_ge(uk_done, p + CREDIT)
                pair_weights(p)
            sp.wait_ge(tab_in, 16)
            sp.wait_ge(blk_done, B_B)

            with sp.Fori(0, DEC_B // 2) as i:
                for par in range(2):
                    sp.wait_ge(ov_done, i * 2 + CREDIT)
                    for g in range(PAGES):
                        r = sp.value_load(ptab[0:1, ds(i * (2 * PAGES) + (par * PAGES + g), 1)],
                                          min_val=0, max_val=I["cache_ckv"].shape[1] - 1)
                        sp.dma_start(pages[:, par, g, :], I["cache_ckv"][0][ds(r, 1)].rearrange("o p n -> (o p) n"))\
                            .then_inc(page_in[par], 16)
                        sp.dma_start(KP[:, par, g, :], I["cache_kpe"][0][ds(r, 1)].rearrange("o p n -> (o p) n"))\
                            .then_inc(page_in[par], 16)
            sp.wait_ge(w_hi, B_B)
            sp.wait_ge(w_lo, B_B)
            sp.dma_start(wkvf[:, :, :], w_kvup).then_inc(wkvf_in, 16)
            sp.wait_ge(os_done, 1)
            for m in range(RAW):
                sp.dma_start(wraw[:, (B_B + m) % RAW, :, :], col(w_o, 0, m)).then_inc(w_loaded[(B_B + m) % RAW], 16)
            for m in range(RAW, 8):
                load_block(B_B + m, col(w_o, 0, m))

            def load_mlp(i):
                for half in range(2):
                    n0 = B_MLP[i] + 32 * half
                    with sp.Fori(0, 4) as it:
                        for s in range(4):
                            load_block(it * 4 + (n0 + s), w_up[i][:, :, ds(it * (4 * P) + (16 * half + s) * P, P)],
                                       (n0 + s) % RAW)
                    n0 += 16
                    with sp.Fori(0, 4) as it:
                        for s in range(4):
                            k0 = 16 * half + 8 * (s % 2)
                            load_block(it * 4 + (n0 + s), w_down[i][:, k0:k0 + 8, ds(it * (2 * P) + (s // 2) * P, P)],
                                       (n0 + s) % RAW)

            load_mlp(0)
            for s in range(4):
                load_block(B_GLU + s, w_glu[:, :, (s // 2) * P + (s % 2) * D:(s // 2 + 1) * P + (s % 2) * D])
            sp.wait_ge(blk_done, B_GLU)
            sp.wait_ge(prep_left, GP // QC + CREDIT)
            sp.dma_start(BC[:, :, :, :], BSTD[:, :, :, :]).then_inc(bst_in, 16)
            for a, part in enumerate(("re", "im")):
                sp.dma_start(h0n[:, 2 * a:2 * a + 2, :],
                             I[f"state_ssm_{part}"][0].rearrange("b g p -> (b g p)")
                             .rearrange("(t m n) -> m t n", m=P, n=P)).then_inc(h0_in, 16)
            sp.wait_ge(hd_out, 16 * 8)
            for r in range(T):
                sp.dma_start(U[GS * r:GS * r + GS, :, :],
                             HDR[:, T - 1 - r, :].rearrange("(g i) c -> i g c", i=GS)).then_inc(u_in, 16)
            sp.wait_ge(xs_done, 11)
            sp.dma_start(BC[:, :, :, :], CSD[:, :, :, :]).then_inc(cs_in, 16)
            with sp.Fori(1, 4) as it:
                for s in range(4):
                    load_block(it * 4 + (B_GLU + s), w_glu[:, :, ds(it * (2 * P) + (s // 2) * P + (s % 2) * D, P)],
                               (B_GLU + s) % RAW)
            load_mlp(1)

        @block.gpsimd
        def _(pool):
            pool.sem_inc(prep_left, CREDIT)
            pool.sem_inc(z_lo, CREDIT)
            pool.memset(ones[:, :], 1.0).then_inc(ones_set, 1)
            with pool.Fori(0, GP // QC) as c:
                pool.wait_ge(yt_sb, c + 1 + CREDIT)
                apart(pool)
                pool.dma_start(BSTD[:, :, ds(c * QC, QC), :], bstc[:, :, :, :]).then_inc(prep_out, 16)
                pool.wait_ge(ca_ready, c + 1 + CREDIT)
                apart(pool)
                for a in range(2):
                    pool.dma_start(CSD[:, a, ds(c * QC, QC), :],
                                   CA[:, a, :, 1:9, :].rearrange("p q k o -> p q (k o)")).then_inc(prep_out, 16)
                pool.wait_ge(kd_sb, c + 1 + CREDIT)
                apart(pool)
                pool.dma_start(KD.rearrange("g i n -> i g n")[:, ds(c * (2 * QC), 2 * QC), :],
                               kdc[0:GS].rearrange("p q a n -> p (q a) n")).then_inc(prep_out, 16)
                pool.wait_ge(prep_out, c * 64 + 64)
                pool.sem_inc(prep_left, 1)
            def rest_of(n0, mask=None):
                for k in range(KT):
                    pool.wait_ge(h_hi, n0 + k + 1)
                    pool.tensor_tensor(hR[:, k, LO, :], hT[:, k, :], hR[:, k, HI, :].bitcast(F32), ALU.subtract)\
                        .then_inc(h_lo, 1)

            rest_of(R_A)
            pool.wait_ge(nat_sb, 5)
            pool.dma_start(O["sample_kpe"].rearrange("a b q n -> (a b q) n"), kpeNat[0:NS, BLK, :]).then_inc(out_sem, 16)
            pool.dma_start(O["prompt_kpe"][0, 0].rearrange("(t p) n -> p t n", p=P), kpeNat[:, 0:BLK, :])\
                .then_inc(out_sem, 16)
            pool.dma_start(O["prompt_ckv"][0, 0].rearrange("(a t p) n -> p a t n", a=2, p=P)[:, 0],
                           ckvNat[:, 0, :, :]).then_inc(out_sem, 16)
            pool.dma_start(O["prompt_ckv"][0, 0].rearrange("(a t p) n -> p a t n", a=2, p=P)[:, 1],
                           ckvNat[:, 1, :, :]).then_inc(out_sem, 16)
            pool.wait_ge(nat_sb, 9)
            pool.dma_start(O["sample_ckv"][0].rearrange("b q n -> q b n"), CN[0:DEC_Q, :, :]).then_inc(out_sem, 16)
            pool.wait_ge(out_sem, 16 * 5)
            with pool.Fori(0, PAIRS) as p:
                pool.wait_ge(hw_in, p * 96 + 96)
                apart(pool)
                pool.tensor_copy(wq[:, :, :, 96:112], wq[:, :, :, 80:96]).then_inc(hw_swap, 1)
                pool.tensor_copy(wq[:, :, :, 112:128], wq[:, :, :, 64:80]).then_inc(hw_swap, 1)
            pool.wait_ge(ql_sb, 4 * PAIRS + CREDIT)
            pool.wait_ge(o_sb, 2 * PAIRS + CREDIT)
            with pool.Fori(0, DEC_B // 2) as i:
                for par in range(2):
                    pool.wait_ge(sc_done, i * 18 + CREDIT)
                    apart(pool)
                    pool.tensor_copy(QLb[:, par, :, :], QL[:, :, ds(i * (2 * P) + par * P, P)]).then_inc(qb_ready, 1)
                    pool.tensor_copy(QPb[0:ROPE, par, :], QPE[0:ROPE, ds(i * (2 * P) + par * P, P)])\
                        .then_inc(qb_ready, 1)
            rest_of(R_B)

            def rest_of_hidden(i):
                for half in range(2):
                    z0 = 32 * i + 16 * half
                    with pool.Fori(0, 8) as it:
                        for s in range(2):
                            pool.wait_ge(z_hi, it * 2 + (z0 + s + 1))
                            apart(pool)
                            m = it * 2 + s
                            pool.tensor_tensor(part_of(zR, m, LO), hid[:, s, :], part_of(zR, m, HI).bitcast(F32),
                                               ALU.subtract).then_inc(z_lo, 1)

            rest_of(R_MLP[0])
            rest_of_hidden(0)
            pool.wait_ge(blk_done, B_MLP[0] + 48)
            pool.memset(MI[:, :, :], 0.0).then_inc(mi_zero, 1)
            pool.wait_ge(mi_zero, 1)
            for r in range(T):
                s = T - 1 - r
                pool.dma_start(MI[GS * r:GS * r + GS, :, GS * s:P],
                               KD.rearrange("g i n -> i g n")[:, :, 0:P - GS * s]).then_inc(mi_in, 16)
            for k in range(KT):
                pool.wait_ge(h_ready, H_MIX1 + k + 1)
                pool.dma_start(HDR[k * P:(k + 1) * P].rearrange("p s c -> p (s c)"), hT[:, k, :]).then_inc(hd_out, 16)
            pool.wait_ge(f_sb, 2)
            for a, part in enumerate(("re", "im")):
                pool.dma_start(O[f"sample_ssm_{part}"][0].rearrange("b g p -> (b g p)")
                               .rearrange("(t m n) -> m t n", m=P, n=P),
                               tmpa[:, 1, a * 256:a * 256 + 256].rearrange("p (t n) -> p t n", t=2)).then_inc(out_sem, 16)
                pool.dma_start(O[f"prompt_ssm_{part}"][0, 0].rearrange("g p -> (g p)").rearrange("(q n) -> q n", n=P),
                               sq[0:GP, 0, a * P:a * P + P]).then_inc(out_sem, 16)
            rest_of(R_GLU)
            rest_of(R_MLP[1])
            rest_of_hidden(1)
            for j in range(BLK + 1):
                pool.wait_ge(tile_free, T_OUT + j + 1)
                dst = O["y_prompt"][0, j * P:(j + 1) * P, :] if j < BLK else O["y_sample"].rearrange("b q n -> (b q) n")
                rows = P if j < BLK else NS
                pool.dma_start(dst, arena[0:rows, (j % 2) * D:(j % 2) * D + D]).then_inc(y_out[j % 2], 16)
            pool.wait_ge(out_sem, 16 * (5 + 4))
            pool.wait_ge(y_out[0], 16 * 3)
            pool.wait_ge(y_out[1], 16 * 2)

        @block.tensor
        def _(pe):
            for s in (t_done, pv_done, sc_done, dt_done, ov_done, olt_done, uk_done, kd_done):
                pe.sem_inc(s, CREDIT)
            def transpose(out, in_, rows=None):
                k = in_.shape[0]
                b = in_.base_partition()
                return pe.transpose(out, in_, ident[b:b + k, b:b + k])

            pe.wait_ge(const_in, 16 * 11)
            pe.wait_ge(ones_set, 1)
            transpose(bank6[:, 0:VROWS], vrow[0:VROWS, :]).then_inc(vec_done, 1)
            pe.wait_ge(x_in, 32)
            for k in range(KT):
                if k >= 2:
                    pe.wait_ge(tile_free, k - 1)
                for j in range(BLK):
                    transpose(pair[k % 2][:, 0, j * P:(j + 1) * P], xnat[:, j, k * P:(k + 1) * P])
                transpose(pair[k % 2][:, 1, 0:NS], xnat[0:NS, BLK, k * P:(k + 1) * P]).then_inc(tile_done, 1)

            pe.wait_ge(tile_free, 8)
            pe.wait_ge(y_ready, 1)
            for a in range(20):
                ins = transpose(pair[0][:, a // 16, (a % 16) * GP:(a % 16) * GP + GP], nat[0:GP, 3 + a, :])
            ins.then_inc(pw_done, 1)
            pe.wait_ge(s5_in, 16 * 7)
            for a in range(2):
                for t in range(8):
                    ins = transpose([bank23, bank45][a][0:ST, t // 4, (t % 4) * P:(t % 4 + 1) * P], Cn[:, a, t, :])
            ins.then_inc(c_done, 1)
            pe.wait_ge(pw_sb, 1)
            pe.wait_ge(c_sb, 1)
            with pe.Fori(0, GP // QC) as c:
                pe.wait_ge(y_ready, c + 2)
                pe.wait_ge(yt_sb, c + CREDIT)
                for a in range(2):
                    for q in range(QC):
                        ins = transpose(bank01[:, a, q * P:(q + 1) * P], Y[:, a, q, :])
                ins.then_inc(yt_done, 1)
                pe.wait_ge(ca_ready, c + 1 + CREDIT)
                pe.wait_ge(kd_sb, c + CREDIT)
                apart(pe)
                for half in range(2):
                    for q in range(QC):
                        for a in range(2):
                            rows = slice(64 * half, 64 * half + 64)
                            ins = pe.matmul(bank23[0:GS, half, q * P:(q + 1) * P], bb[rows, a, q, :],
                                            CA[rows, a, q, 0:8, :].rearrange("p k o -> p (k o)"),
                                            start=(a == 0), stop=(a == 1))
                ins.then_inc(kd_done, 1)

            def sum_squares(n, q_end):
                pe.wait_ge(sq_used, q_end)
                for a in range(2):
                    ins = pe.matmul(bank45[:, a, 0:HALF], ones[:, :], acc[:, a * HALF:(a + 1) * HALF],
                                    start=True, stop=True)
                ins.then_inc(ss_done, 1)

            def block_mm(n, bank, tokens, first, last, s=None, m=slice(0, P)):
                s = n % CUT if s is None else s
                pe.wait_ge(w_hi, n + 1)
                pe.wait_ge(w_lo, n + 1)
                for k in range(8):
                    for wp, parts in PASSES:
                        for xp in parts:
                            for a in range(2):
                                ins = pe.matmul(bank[:, a, 0:HALF], wR[:, s, wp, k, :],
                                                tokens(k, xp)[:, a * HALF:(a + 1) * HALF],
                                                start=(first and k == 0 and (wp, xp) == (HI, HI)),
                                                stop=(last and k == 7 and wp == LO))
                ins.then_inc(blk_done, 1)

            from_h = lambda k, xp: hR[:, k, xp, :]

            sum_squares(0, Q_CQ)
            for m in range(7):
                if m == 5:
                    sum_squares(1, Q_CKV)
                pe.wait_ge(tile_free, T_A + m - 1)
                if m == 0:
                    pe.wait_ge(h_hi, R_A + 8)
                    pe.wait_ge(h_lo, R_A + 8)
                block_mm(B_A + m, pair[(T_A + m) % 2], from_h, True, True)
            pe.wait_ge(var_ready, 2)
            sum_squares(2, Q_MLP0)
            pe.wait_ge(tile_free, T_B)

            pe.wait_ge(h_ready, H_CKV + 2)
            pe.wait_ge(kpe_raw, 1)
            for j in range(BLK):
                if j >= 2:
                    pe.wait_ge(nat_sb, j - 1)
                for r in range(2):
                    transpose(pair[j % 2][:, 0, r * P:(r + 1) * P], ckvT[:, r, j * P:(j + 1) * P])
                transpose(pair[j % 2][:, 0, 256:256 + ROPE], kpR[64:96, j * P:(j + 1) * P]).then_inc(nat_done, 1)
            pe.wait_ge(nat_sb, 4)
            transpose(pair[0][0:NS, 0, 0:ROPE], kpR[64:96, SEQ:N]).then_inc(nat_done, 1)
            for j in range(4):
                for b in (2 * j, 2 * j + 1):
                    for r in range(2):
                        dst = [bank45[:, 0, :], bank45[:, 1, :], bank6[:, :], bank7[:, :]][j]
                        ins = transpose(dst[0:DEC_Q, (b % 2) * 256 + r * P:(b % 2) * 256 + (r + 1) * P],
                                        ckvT[:, r, SEQ + b * DEC_Q:SEQ + (b + 1) * DEC_Q])
                ins.then_inc(nat_done, 1)
            pe.wait_ge(nat_sb, 9)

            pe.wait_ge(h_ready, H_CQ + 4)

            def unit_scores(U_, h, blk):
                pe.wait_ge(p_exp, (U_ if blk == 0 else U_ - 1) + CREDIT)
                n = (blk + 1) * P
                bank = bank01[:, blk % 2, :]
                pe.matmul(bank[:, 0:n], qT[0:HD, h, blk * P:(blk + 1) * P], kT[0:HD, h, 0:n],
                          start=True, stop=False)
                pe.matmul(bank[:, blk * P:n], ident[:, :], cmask[:, :], start=False, stop=True).then_inc(s_done, 1)

            def unit_turn(U_, blk):
                pe.wait_ge(p_sb, U_ + 1)
                for t in range(blk + 1):
                    ins = transpose(bank23[:, blk % 2, t * P:(t + 1) * P], prob[:, blk % 2, t * P:(t + 1) * P])
                ins.then_inc(t_done, 1)

            def unit_values(U_, h, blk):
                pe.wait_ge(pt_sb, U_ + 1)
                for t in range(blk + 1):
                    ins = pe.matmul(bank45[64 * h:64 * h + 64, 0, blk * P:(blk + 1) * P],
                                    V[:, t, 64 * h:64 * h + 64], probT[:, blk % 2, t, :],
                                    start=(t == 0), stop=(t == blk))
                ins.then_inc(pv_done, 1)

            with pe.Fori(0, PAIRS) as p:
                pe.wait_ge(hw_in, p * 96 + 96)
                pe.wait_ge(hw_swap, p * 2 + 2)
                for h in range(2):
                    for a in range(2):
                        for k in range(4):
                            ins = pe.matmul(pair[h][:, a, 0:HALF], wq[:, k, h, :], cqT[:, k, a * HALF:(a + 1) * HALF],
                                            start=(k == 0), stop=(k == 3))
                    ins.then_inc(q_done, 1)
                pe.wait_ge(o_sb, p * 2 + CREDIT)
                for r in range(2):
                    ins = pe.matmul(bank45[:, 0, :], wkv[:, r, 0, :, :].rearrange("p h n -> p (h n)"), ckvT[:, r, 0:SEQ],
                                    start=(r == 0), stop=(r == 1))
                ins.then_inc(k_done, 1)
                for t in range(BLK):
                    for r in range(2):
                        ins = pe.matmul(bank45[:, 1, t * P:(t + 1) * P], ckvT[:, r, t * P:(t + 1) * P],
                                        wkv[:, r, 1, :, :].rearrange("p h n -> p (h n)"), start=(r == 0), stop=(r == 1))
                ins.then_inc(v_done, 1)
                for h in range(2):
                    for r in range(2):
                        ins = transpose(bank6[0:NOPE, (2 * h + r) * P:(2 * h + r + 1) * P], wkv[:, r, 0, h, :])
                ins.then_inc(uk_done, 1)
                pe.wait_ge(uk_sb, p + 1)
                pe.wait_ge(qn_sb, p * 2 + 2)
                pe.wait_ge(ql_sb, p * 4 + CREDIT)
                for h in range(2):
                    for r in range(2):
                        ins = pe.matmul(bank7[:, (2 * h + r) * NS:(2 * h + r + 1) * NS], ukT[0:NOPE, 2 * h + r, :],
                                        qT[0:NOPE, h, SEQ:N], start=True, stop=True)
                ins.then_inc(ql_done, 1)
                pe.wait_ge(qr_sb, p * 2 + 2)
                pe.wait_ge(k_sb, p * 2 + 2)
                units = [(h, blk) for h in range(2) for blk in range(BLK)]
                unit_scores(p * 8, 0, 0)
                for u, (h, blk) in enumerate(units):
                    if u + 1 < 8:
                        unit_scores(p * 8 + (u + 1), *units[u + 1])
                    unit_turn(p * 8 + u, blk)
                    if u == 0:
                        pe.wait_ge(v_sb, p + 1)
                    if u >= 1:
                        unit_values(p * 8 + (u - 1), *units[u - 1])
                unit_values(p * 8 + 7, *units[7])

            def turn_pages(i, par, g):
                for j in range(2):
                    for r in range(2):
                        transpose(bank01[:, g % 2, r * 256 + j * P:r * 256 + (j + 1) * P],
                                  pages[:, par, 2 * g + j, r * P:(r + 1) * P])
                for j in range(2):
                    ins = transpose(bank23[0:ROPE, g % 2, j * P:(j + 1) * P], KP[:, par, 2 * g + j, :])
                ins.then_inc(ct_done, 1)

            def group_scores(i, par, g):
                n = DEC_Q if g == 8 else 256
                bank = bank45[:, g % 2, 0:n]
                if g < 8:
                    pe.wait_ge(ct_sb, i * 16 + (par * 8 + g + 1))
                    pe.wait_ge(kp_sb, i * 16 + (par * 8 + g + 1))
                back = i * 18 + (par * 9 + g - 1) if g >= 2 else i * 18 + par * 9
                pe.wait_ge(sc_sb, back + CREDIT)
                for r in range(2):
                    rhs = cT[:, g % 2, r, :] if g < 8 else ckvT[:, r, ds(i * (2 * DEC_Q) + (SEQ + par * DEC_Q), DEC_Q)]
                    pe.matmul(bank, QLb[:, par, r, :], rhs, start=(r == 0), stop=False)
                rhs = kpT[0:ROPE, g % 2, :] if g < 8 else kpeN[0:ROPE, ds(i * (2 * DEC_Q) + par * DEC_Q, DEC_Q)]
                ins = pe.matmul(bank, QPb[0:ROPE, par, :], rhs, start=False, stop=(g < 8))
                if g == 8:
                    ins = pe.matmul(bank, ident[:, :], nmask[:, :], start=False, stop=True)
                ins.then_inc(sc_done, 1)

            pe.wait_ge(o_sb, 2 * PAIRS + CREDIT)
            pe.wait_ge(ql_sb, 4 * PAIRS + CREDIT)
            with pe.Fori(0, DEC_B // 2) as i:
                pe.wait_ge(olt_sb, i * 2 + CREDIT)
                for par in range(2):
                    pe.wait_ge(page_in[par], i * (32 * PAGES) + 32 * PAGES)
                    pe.wait_ge(qb_ready, i * 4 + (2 * par + 2))
                    turn_pages(i, par, 0)
                    for g in range(9):
                        if g + 1 < 8:
                            if g + 1 >= 2:
                                pe.wait_ge(ct_sb, i * 16 + (par * 8 + g))
                                pe.wait_ge(kp_sb, i * 16 + (par * 8 + g))
                            turn_pages(i, par, g + 1)
                        group_scores(i, par, g)
                for par in range(2):
                    pe.wait_ge(d_exp, i * 2 + (par + 1))
                    for j in range(5):
                        bank = [bank6, bank7][j % 2]
                        J = i * 10 + (par * 5 + j)
                        pe.wait_ge(dt_sb, i * 10 + (par * 5 + max(j - 1, 0)) + CREDIT)
                        if j < 4:
                            for t in range(4):
                                c0 = (4 * j + t) * P
                                ins = transpose(bank[:, t * P:(t + 1) * P], S[:, par, c0:c0 + P])
                        else:
                            ins = transpose(bank[0:DEC_Q, 0:P], S[:, par, PAST:PAST + DEC_Q])
                        ins.then_inc(dt_done, 1)
                    pe.wait_ge(olt_sb, i * 2 + par + CREDIT)
                    for g in range(PAGES):
                        if g % 4 == 0:
                            pe.wait_ge(dt_sb, i * 10 + (par * 5 + g // 4 + 1) + CREDIT)
                        pe.matmul(bank23[:, 0, 0:256], PT[:, g, :], pages[:, par, g, :], start=(g == 0), stop=False)
                    pe.wait_ge(dt_sb, i * 10 + (par * 5 + 5) + CREDIT)
                    pe.matmul(bank23[:, 0, 0:256], PTN[0:DEC_Q, :],
                              CN[0:DEC_Q, ds(i * 2 + par, 1), :].rearrange("p o n -> p (o n)"),
                              start=False, stop=True).then_inc(ov_done, 1)
                    pe.wait_ge(ol_sb, i * 2 + (par + 1))
                    for r in range(2):
                        ins = transpose(bank23[:, 1, r * P:(r + 1) * P], OLn[:, r * P:(r + 1) * P])
                    ins.then_inc(olt_done, 1)
            pe.wait_ge(olt_sb, DEC_B + CREDIT)
            pe.wait_ge(wkvf_in, 16)
            for h in range(HEADS):
                for r in range(2):
                    ins = pe.matmul(bank01[64 * (h % 2):64 * (h % 2) + 64, 0, (h // 2) * NS:(h // 2 + 1) * NS],
                                    wkvf[:, r, h * P + NOPE:(h + 1) * P],
                                    OLT[:, r, :, :].rearrange("p b (q h) -> p b q h", h=HEADS)[:, :, :, h],
                                    start=(r == 0), stop=(r == 1))
            ins.then_inc(os_done, 1)

            pe.wait_ge(h_hi, R_B + 8)
            pe.wait_ge(h_lo, R_B + 8)
            for m in range(8):
                pe.wait_ge(tile_free, T_B + m - 1)
                block_mm(B_B + m, pair[(T_B + m) % 2], from_h, True, True)

            def mlp(i):
                pe.wait_ge(h_hi, R_MLP[i] + 8)
                pe.wait_ge(h_lo, R_MLP[i] + 8)
                for half in range(2):
                    n0, t0, z0 = B_MLP[i] + 32 * half, T_MLP[i] + 24 * half, 32 * i + 16 * half
                    with pe.Fori(0, 4) as it:
                        for s in range(4):
                            pe.wait_ge(tile_free, it * 4 + (t0 + s - 1))
                            block_mm(it * 4 + (n0 + s), pair[(t0 + s) % 2], from_h, True, True, (n0 + s) % CUT)
                    pe.wait_ge(z_lo, z0 + 16 + CREDIT)
                    pe.wait_ge(z_hi, z0 + 16)
                    n0, t0 = n0 + 16, t0 + 16
                    with pe.Fori(0, 4) as it:
                        for s in range(4):
                            if s % 2 == 0:
                                pe.wait_ge(tile_free, it * 2 + (t0 + s // 2 - 1))
                            block_mm(it * 4 + (n0 + s), pair[(t0 + s // 2) % 2],
                                     lambda k, xp, c=s % 2: zR[:, 8 * c + k, xp, :],
                                     s % 2 == 0, s % 2 == 1, (n0 + s) % CUT)

            sum_squares(3, Q_MIX1)
            mlp(0)
            sum_squares(4, Q_MLP1)

            pe.wait_ge(h0_in, 32)
            pe.wait_ge(tile_free, T_GLU)
            for a in range(2):
                for t in range(2):
                    ins = transpose(bank6[:, (2 * a + t) * P:(2 * a + t + 1) * P], h0n[:, 2 * a + t, :])
            ins.then_inc(h0_done, 1)
            pe.wait_ge(bst_in, 16)
            pe.wait_ge(u_in, 16 * T)
            for j in range(11):
                qs = range(3 * j, min(3 * j + 3, GP))
                if j >= 2:
                    pe.wait_ge(xs_sb, j - 1)
                for q in qs:
                    for half in range(2):
                        for a in range(2):
                            ins = pe.matmul(bank01[64 * half:64 * half + 64, j % 2,
                                                   ((q % 3) * 2 + a) * NC:((q % 3) * 2 + a + 1) * NC],
                                            BC[:, a, q, 64 * half:64 * half + 64], U[:, 2 * q + half, :],
                                            start=True, stop=True)
                ins.then_inc(xs_done, 1)
            pe.wait_ge(cs_in, 16)
            pe.wait_ge(mi_in, 16 * T)
            pe.wait_ge(z_state, 1)

            def chunk_outputs(k):
                banks = pair[k % 2]
                if k >= 2:
                    pe.wait_ge(yc_sb, k - 1)
                for q4 in range(4):
                    for half in range(2):
                        q = 4 * k + q4
                        rows = slice(64 * half, 64 * half + 64)
                        out = banks[0:NC, half, q4 * P:(q4 + 1) * P]
                        pe.matmul(out, U[:, 2 * q + half, :], MI[:, 2 * q + half, :], start=True, stop=False)
                        for a in range(2):
                            ins = pe.matmul(out, Z[rows, :, a, q], BC[rows, a, q, :], start=False, stop=(a == 1))
                ins.then_inc(yc_done, 1)

            def outputs_by_channel(k):
                pe.wait_ge(yc_sb, k + 1)
                if k >= 1:
                    pe.wait_ge(yb_sb, k)
                for t in range(T):
                    ins = transpose(bank45[:, t // 4, (t % 4) * NC:(t % 4 + 1) * NC], yblk[0:NC, k % 2, t, :])
                ins.then_inc(yb_done, 1)

            chunk_outputs(0)
            pe.wait_ge(f_ready, 1)
            pe.wait_ge(h0_sb, 1)
            for a in range(2):
                for t in range(2):
                    transpose(bank7[:, (2 * a + t) * P:(2 * a + t + 1) * P],
                              XG[:, a, 1 + 4 * t:5 + 4 * t, :].rearrange("p c q -> p (c q)"))
                ins = transpose(bank6[0:GP, a * P:(a + 1) * P], XG[:, a, 0, :])
            ins.then_inc(f_done, 1)
            for k in range(KT):
                if k + 1 < KT:
                    chunk_outputs(k + 1)
                outputs_by_channel(k)

            pe.wait_ge(h_hi, R_GLU + 8)
            pe.wait_ge(h_lo, R_GLU + 8)
            with pe.Fori(0, 4) as it:
                for s in range(4):
                    pe.wait_ge(tile_free, it * 4 + (T_GLU + s - 1))
                    block_mm(it * 4 + (B_GLU + s), pair[(T_GLU + s) % 2], from_h, True, True, (B_GLU + s) % CUT)
            sum_squares(5, Q_FIN)
            mlp(1)
            sum_squares(6, Q_END)
            for j in range(BLK + 1):
                pe.wait_ge(tile_free, T_OUT + j - 1)
                rows = P if j < BLK else NS
                for k in range(KT):
                    if j == 0:
                        pe.wait_ge(h_ready, H_FIN + k + 1)
                    ins = transpose(pair[j % 2][0:rows, k // 4, (k % 4) * P:(k % 4 + 1) * P],
                                    hT[:, k, j * P:j * P + rows])
                ins.then_inc(tile_done, 1)


        @block.scalar
        def _(act):
            for s in (yt_sb, kd_sb, o_sb, p_exp, sc_sb, dt_sb):
                act.sem_inc(s, CREDIT)
            def copy(out, in_, scale=1.0):
                return act.activation(out, in_, ACT.Copy, scale=scale)

            def square(n, src):
                act.wait_ge(sq_used, n - 1)
                return act.activation(sq[:, square_place[0], :], src, ACT.Square)

            square_place = [0]

            def root(n):
                act.wait_ge(var_ready, n + 1)
                act.activation(rstd[:, :], rstd[:, :], ACT.Sqrt).then_inc(rstd_ready, 1)

            act.wait_ge(vec_done, 1)
            copy(vecs[:, :], bank6[:, 0:VROWS]).then_inc(vec_sb, 1)
            for k in range(KT):
                act.wait_ge(tile_done, k + 1)
                copy(xT[:, k, 0:SEQ], pair[k % 2][:, 0, :])
                copy(xT[:, k, SEQ:N], pair[k % 2][:, 1, 0:NS]).then_inc(tile_free, 1)
                act.wait_ge(tile_free, k + 1)
                if k >= 2:
                    act.wait_ge(sq_used, k - 1)
                act.activation(sq[:, k % 2, :], xT[:, k, :], ACT.Square).then_inc(sq_ready, 1)

            act.wait_ge(s5_in, 16 * 7)
            act.activation(nat[0:GP, 2, 2:4], nat[0:GP, 2, 0:2], ACT.Exp).then_inc(aprep, 1)
            act.wait_ge(dprep, 1)
            act.activation(nat[0:GP, 25, :], nat[0:GP, 23, :], ACT.Exp)
            act.activation(nat[0:GP, 26, :], nat[0:GP, 24, :], ACT.Sin)
            act.activation(nat[0:GP, 27, :], nat[0:GP, 24, :], ACT.Sin, scale=0.5).then_inc(aprep, 1)
            act.wait_ge(pw_done, 1)
            copy(PW[:, 0:16, :].rearrange("p a q -> p (a q)"), bank01[:, 0, :])
            copy(PW[:, 16:20, :].rearrange("p a q -> p (a q)"), bank01[:, 1, 0:4 * GP]).then_inc(pw_sb, 1)
            act.wait_ge(c_done, 1)
            for a in range(2):
                for half in range(2):
                    ins = copy(Cp[64 * half:64 * half + 64, a, :, :].rearrange("p (b q) o -> p b q o", b=2),
                               [bank23, bank45][a][0:ST, :, :].rearrange("p b (q h o) -> p h b q o", h=2, o=GS)[:, half])
            ins.then_inc(c_sb, 1)
            with act.Fori(0, GP // QC) as c:
                act.wait_ge(yt_done, c + 1)
                act.wait_ge(prep_left, c + CREDIT)
                copy(bstc.rearrange("p a q n -> p a (q n)"), bank01[:, :, :]).then_inc(yt_sb, 1)
                act.wait_ge(kd_done, c + 1 + CREDIT)
                copy(kdc[0:GS, :, 0, :], bank23[0:GS, 0, :].rearrange("p (q n) -> p q n", q=QC))
                copy(kdc[0:GS, :, 1, :], bank23[0:GS, 1, :].rearrange("p (q n) -> p q n", q=QC)).then_inc(kd_sb, 1)

            def cut_block(n, raw=None, place=None):
                raw = n % RAW if raw is None else raw
                place = n % CUT if place is None else place
                q = n // RAW if isinstance(n, int) else None
                act.wait_ge(w_loaded[raw], loads(n, raw))
                if not (isinstance(n, int) and n < CUT):
                    act.wait_ge(blk_done, n - CUT + 1)
                act.activation(wR[:, place, HI, :, :], wraw[:, raw, :, :], ACT.Copy).then_inc(w_hi, 1)

            def cut_tokens(n0, ready, r0):
                for k in range(KT):
                    act.wait_ge(ready, r0 + k + 1 if r0 is not None else 1)
                    act.activation(hR[:, k, HI, :], hT[:, k, :], ACT.Copy).then_inc(h_hi, 1)

            root(0)
            act.wait_ge(prep_left, GP // QC + CREDIT)
            cut_tokens(R_A, h_ready, H_MIX0)
            cut_block(0)
            for m in range(6):
                n = Q_CQ + m
                cut_block(m + 1)
                act.wait_ge(blk_done, B_A + m + 1)
                act.wait_ge(sq_used, n - 1)
                src = pair[(T_A + m) % 2][:, :, 0:HALF]
                act.activation(halves(sq[:, n % 2, :]), src, ACT.Square).then_inc(sq_ready, 1)
                copy(halves(cqT[:, m, :] if m < 4 else ckvT[:, m - 4, :]), src).then_inc(tile_free, 1)
            root(1)
            root(2)
            for j in range(BLK):
                act.wait_ge(nat_done, j + 1)
                copy(ckvNat[:, j // 2, j % 2, :], pair[j % 2][:, 0, 0:KV_D])
                copy(kpeNat[:, j, :], pair[j % 2][:, 0, KV_D:KV_D + ROPE]).then_inc(nat_sb, 1)
            act.wait_ge(nat_done, 5)
            copy(kpeNat[0:NS, BLK, :], pair[0][0:NS, 0, 0:ROPE]).then_inc(nat_sb, 1)
            for j, src in enumerate((bank45[:, 0, :], bank45[:, 1, :], bank6[:, :], bank7[:, :])):
                act.wait_ge(nat_done, 6 + j)
                copy(CN[0:DEC_Q, 2 * j:2 * j + 2, :].rearrange("p b n -> p (b n)"), src[0:DEC_Q]).then_inc(nat_sb, 1)

            def unit_exp(U_, blk):
                n = (blk + 1) * P
                act.wait_ge(nm_ready, U_ + 1)
                act.wait_ge(t_done, (U_ if blk == 0 else U_ - 1) + CREDIT)
                act.activation(prob[:, blk % 2, 0:n], bank01[:, blk % 2, 0:n], ACT.Exp,
                               bias=stat[:, blk % 2:blk % 2 + 1],
                               accum_out=stat[:, 2 + blk % 2:3 + blk % 2]).then_inc(p_exp, 1)

            def unit_turned(U_, blk):
                n = (blk + 1) * P
                act.wait_ge(t_done, U_ + 1 + CREDIT)
                act.wait_ge(pv_done, (U_ if blk == 0 else U_ - 1) + CREDIT)
                copy(probT[:, blk % 2, 0:blk + 1, :].rearrange("p t n -> p (t n)"), bank23[:, blk % 2, 0:n])\
                    .then_inc(pt_sb, 1)

            def head_out(p, h):
                act.wait_ge(pv_done, p * 8 + (4 * h + 4) + CREDIT)
                copy(hT[64 * h:64 * h + 64, ds(p, 1), 0:SEQ].rearrange("p o n -> p (o n)"),
                     bank45[64 * h:64 * h + 64, 0, :]).then_inc(o_sb, 1)

            with act.Fori(0, PAIRS) as p:
                for h in range(2):
                    act.wait_ge(q_done, p * 2 + (h + 1))
                    copy(halves(qT[0:NOPE, h, :]), pair[h][0:NOPE, :, 0:HALF], SCALE).then_inc(qn_sb, 1)
                act.wait_ge(k_done, p + 1)
                copy(kT[0:NOPE, 0, :], bank45[0:NOPE, 0, :]).then_inc(k_sb, 1)
                copy(kT[0:NOPE, 1, :], bank45[NOPE:P, 0, :]).then_inc(k_sb, 1)
                act.wait_ge(uk_done, p + 1 + CREDIT)
                copy(ukT[0:NOPE, :, :].rearrange("p a n -> p (a n)"), bank6[0:NOPE, :]).then_inc(uk_sb, 1)
                unit_exp(p * 8, 0)
                for u in range(8):
                    if u + 1 < 8:
                        unit_exp(p * 8 + (u + 1), (u + 1) % 4)
                    unit_turned(p * 8 + u, u % 4)
                    if u == 5:
                        head_out(p, 0)
                head_out(p, 1)

            def pages_turned(i, par, g):
                act.wait_ge(ct_done, i * 16 + (par * 8 + g + 1))
                act.wait_ge(sc_done, i * 18 + (par * 9 + max(g - 1, 0)) + CREDIT)
                copy(cT[:, g % 2, :, :].rearrange("p r n -> p (r n)"), bank01[:, g % 2, :]).then_inc(ct_sb, 1)

            with act.Fori(0, DEC_B // 2) as i:
                act.wait_ge(dt_done, i * 10 + CREDIT)
                for par in range(2):
                    pages_turned(i, par, 0)
                    for g in range(9):
                        if g + 1 < 8:
                            pages_turned(i, par, g + 1)
                        n = DEC_Q if g == 8 else 256
                        act.wait_ge(sc_done, i * 18 + (par * 9 + g + 1) + CREDIT)
                        copy(S[:, par, g * 256:g * 256 + n], bank45[:, g % 2, 0:n]).then_inc(sc_sb, 1)
                    act.wait_ge(dm_ready, i * 2 + (par + 1))
                    act.activation(S[:, par, :], S[:, par, :], ACT.Exp, bias=stat[:, 24 + par:25 + par],
                                   accum_out=stat[:, 26 + par:27 + par]).then_inc(d_exp, 1)
                for par in range(2):
                    act.wait_ge(ov_done, i * 2 + par + CREDIT)
                    for j in range(5):
                        act.wait_ge(dt_done, i * 10 + (par * 5 + j + 1) + CREDIT)
                        bank = [bank6, bank7][j % 2]
                        if j < 4:
                            copy(PT[:, 4 * j:4 * j + 4, :].rearrange("p g n -> p (g n)"), bank[:, :]).then_inc(dt_sb, 1)
                        else:
                            copy(PTN[0:DEC_Q, :], bank[0:DEC_Q, 0:P]).then_inc(dt_sb, 1)
            act.wait_ge(os_done, 1)
            copy(hT[:, :, SEQ:N], bank01[:, 0, :].rearrange("p (k n) -> p k n", k=KT)).then_inc(os_sb, 1)

            def mlp(i):
                for half in range(2):
                    n0, t0, z0 = B_MLP[i] + 32 * half, T_MLP[i] + 24 * half, 32 * i + 16 * half
                    act.wait_ge(tile_free, t0)
                    with act.Fori(0, 4) as it:
                        for s in range(4):
                            n = it * 4 + (n0 + s)
                            cut_block(n + 1, (n0 + s + 1) % RAW, (n0 + s + 1) % CUT)
                            act.wait_ge(blk_done, n + 1)
                            act.wait_ge(z_ready, it * 4 + max(z0 + s - 1, 0) + CREDIT)
                            act.activation(halves(tmpa[:, s % 2, :]), pair[(t0 + s) % 2][:, :, 0:HALF], ACT.Relu)\
                                .then_inc(tile_free, 1)
                            act.wait_ge(z_ready, it * 4 + (z0 + s + 1 + CREDIT))
                            act.activation(part_of(zR, it * 4 + s, HI), hid[:, s % 2, :], ACT.Copy).then_inc(z_hi, 1)
                    n0, t0 = n0 + 16, t0 + 16
                    q0 = (Q_MIX1, Q_FIN)[i]

                    def down(it):
                        for j in range(2):
                            for c in range(2):
                                n = it * 4 + (n0 + 2 * j + c)
                                if isinstance(n, int) and n + 1 == B_END:
                                    continue
                                cut_block(n + 1, (n0 + 2 * j + c + 1) % RAW, (n0 + 2 * j + c + 1) % CUT)
                            if half == 1:
                                act.wait_ge(tile_free, it * 2 + (t0 + j + 1))
                                act.wait_ge(sq_used, it * 2 + (q0 + j - 1))
                                act.activation(sq[:, j, :], row(xT, it * 2 + j), ACT.Square).then_inc(sq_ready, 1)

                    final = (i, half) == (1, 1)
                    with act.Fori(0, 4 - final) as it:
                        down(it)
                    if final:
                        down(3)

            cut_tokens(R_B, os_sb, None)
            cut_block(B_B)
            for m in range(KT):
                cut_block(B_B + m + 1)
                act.wait_ge(tile_free, T_B + m + 1)
                act.wait_ge(sq_used, Q_MLP0 + m - 1)
                act.activation(sq[:, m % 2, :], xT[:, m, :], ACT.Square).then_inc(sq_ready, 1)
            root(3)
            cut_tokens(R_MLP[0], h_ready, H_MLP0)
            mlp(0)
            root(4)

            for j in range(11):
                n = min(3, GP - 3 * j)
                act.wait_ge(xs_done, j + 1)
                src = bank01[:, j % 2, 0:n * 2 * NC].rearrange("p (q a c) -> p q a c", q=n, a=2)
                copy(Z[:, 1:PC, :, 3 * j:3 * j + n].rearrange("p c a q -> p q a c"), src[:, :, :, 0:PC - 1])
                copy(XF[:, :, :, 3 * j:3 * j + n].rearrange("p c a q -> p q a c"), src[:, :, :, PC - 1:NC])\
                    .then_inc(xs_sb, 1)

            def chunk_outputs(k):
                act.wait_ge(yc_done, k + 1)
                if k >= 2:
                    act.wait_ge(yb_done, k - 1)
                for half in range(2):
                    ins = copy(yblk[0:NC, k % 2, :, :].rearrange("p t (q a o) -> p a q t o", a=2, o=GS)[:, half],
                               pair[k % 2][0:NC, half, :].rearrange("p (q t o) -> p q t o", q=4, o=GS))
                ins.then_inc(yc_sb, 1)

            chunk_outputs(0)
            act.wait_ge(f_done, 1)
            copy(tmpa[:, 1, 0:512], bank7[:, :]).then_inc(f_sb, 1)
            copy(sq[0:GP, 0, 0:2 * P], bank6[0:GP, 0:2 * P]).then_inc(f_sb, 1)
            for k in range(KT):
                if k + 1 < KT:
                    chunk_outputs(k + 1)
                act.wait_ge(yb_sb, k + 1)
                act.activation(hT[:, k, :], hT[:, k, :], ACT.Gelu_apprx_tanh).then_inc(g_sb, 1)
            act.wait_ge(yc_done, KT)
            cut_tokens(R_GLU, g_sb, 0)
            act.wait_ge(out_sem, 16 * 9)
            for m in range(KT):
                cut_block(B_GLU + 2 * m + 1)
                cut_block(B_GLU + 2 * m + 2)
                act.wait_ge(blk_done, B_GLU + 2 * m + 2)
                if m >= 2:
                    act.wait_ge(x_new, m - 1)
                act.activation(halves(tmpa[:, m % 2, :]), pair[(T_GLU + 1) % 2][:, :, 0:HALF], ACT.Sigmoid)\
                    .then_inc(sig_ready, 1)
                act.wait_ge(x_new, m + 1)
                act.wait_ge(sq_used, Q_MLP1 + m - 1)
                act.activation(sq[:, m % 2, :], xT[:, m, :], ACT.Square).then_inc(sq_ready, 1)
            root(5)
            cut_tokens(R_MLP[1], h_ready, H_MLP1)
            mlp(1)
            root(6)
            for j in range(BLK + 1):
                rows = P if j < BLK else NS
                act.wait_ge(tile_done, 8 + j + 1)
                if j >= 2:
                    act.wait_ge(y_out[j % 2], 16 * (j // 2))
                copy(arena[0:rows, (j % 2) * D:(j % 2 + 1) * D].rearrange("p (a n) -> p a n", a=2), pair[j % 2][0:rows, :, :])\
                    .then_inc(tile_free, 1)

        @block.vector
        def _(dve):
            for s in (ql_sb, olt_sb, ca_ready, z_ready):
                dve.sem_inc(s, CREDIT)
            step = Tally(dstep)

            def own(ins):
                step.add()
                return ins.then_inc(dstep, 1)

            def settle():
                dve.wait_ge(dstep, step.now())

            tt = dve.tensor_tensor

            def clear_acc():
                own(dve.memset(acc[:, :], 0.0))
                settle()

            def add_square(n, place):
                dve.wait_ge(sq_ready, n + 1)
                dve.wait_ge(sq_used, n)
                tt(acc[:, :], acc[:, :], sq[:, place, :], ALU.add).then_inc(sq_used, 1)

            def norm(n, width, tiles, src, dst, v, by_token=False):
                dve.wait_ge(ss_done, n + 1)
                own(dve.tensor_scalar(halves(rstd[:, :]), bank45[:, :, 0:HALF], 1.0 / width, EPS, ALU.mult, ALU.add))
                settle()
                dve.reciprocal(rstd[:, :], rstd[:, :]).then_inc(var_ready, 1)
                dve.wait_ge(rstd_ready, n + 1)
                for k in range(tiles):
                    out, x, r = dst[:, k, :], src[:, k, :], rstd[:, :]
                    if by_token:
                        out = out.rearrange("p (s c) -> p s c", s=T)
                        x = x.rearrange("p (c s) -> p s c", s=T)
                        r = r.rearrange("p (c s) -> p s c", s=T)
                    dve.scalar_tensor_tensor(out=out, in0=x, scalar=vecs[:, v + k:v + k + 1], in1=r,
                                             op0=ALU.mult, op1=ALU.mult).then_inc(h_ready, 1)

            def cut_rest(n, raw=None, place=None):
                raw = n % RAW if raw is None else raw
                place = n % CUT if place is None else place
                dve.wait_ge(w_hi, n + 1)
                tt(wR[:, place, LO, :, :], wraw[:, raw, :, :], wR[:, place, HI, :, :].bitcast(F32), ALU.subtract)\
                    .then_inc(w_lo, 1)

            clear_acc()
            for k in range(KT):
                add_square(k, k % 2)

            nt = lambda a: nat[0:GP, a, :]
            ar, ai, dtr, th, er, sn, sh, t1, t2 = (nt(0), nt(1), nt(23), nt(24), nt(25), nt(26), nt(27), nt(28), nt(29))
            pr, pi = (lambda k: nt(3 + k)), (lambda k: nt(12 + k))
            dve.wait_ge(aprep, 1)
            dt_ = nat[0:GP, 2, 2:4].unsqueeze(2).to_broadcast([GP, 2, ST])
            two = lambda a: a.rearrange("p (a n) -> p a n", a=2)
            own(tt(two(dtr), two(ar), dt_, ALU.mult))
            own(tt(two(th), two(ai), dt_, ALU.mult))
            settle()
            magic = 1.5 * 2.0 ** 23
            own(dve.tensor_scalar(t1, th, 1.0 / (2 * math.pi), magic, ALU.mult, ALU.add))
            settle()
            own(dve.tensor_scalar(t1, t1, -magic, None, ALU.add))
            settle()
            c1, c2 = 6.28125, 2029.0 / 2 ** 20
            for part in (c1, c2, 2 * math.pi - c1 - c2):
                own(dve.scalar_tensor_tensor(out=th, in0=t1, scalar=-part, in1=th, op0=ALU.mult, op1=ALU.add))
                settle()
            lim = 3.1415925
            dve.tensor_scalar(th, th, lim, -lim, ALU.min, ALU.max).then_inc(dprep, 1)
            own(dve.memset(pr(0), 1.0))
            own(dve.memset(pi(0), 0.0))
            dve.wait_ge(aprep, 2)
            own(tt(t1, sh, sh, ALU.mult))
            own(tt(pi(1), er, sn, ALU.mult))
            settle()
            own(dve.tensor_scalar(t1, t1, -2.0, 1.0, ALU.mult, ALU.add))
            settle()
            own(tt(pr(1), er, t1, ALU.mult))
            settle()
            fr, fi = nt(21), nt(22)
            own(tt(t1, ar, ar, ALU.mult))
            own(tt(t2, ai, ai, ALU.mult))
            own(dve.tensor_scalar(er, pr(1), -1.0, None, ALU.add))
            settle()
            own(tt(t1, t1, t2, ALU.add))
            own(tt(sn, er, ar, ALU.mult))
            own(tt(sh, pi(1), ai, ALU.mult))
            settle()
            own(dve.reciprocal(t1, t1))
            own(tt(sn, sn, sh, ALU.add))
            settle()
            own(tt(fr, sn, t1, ALU.mult))
            own(tt(t2, pi(1), ar, ALU.mult))
            own(tt(th, er, ai, ALU.mult))
            settle()
            own(tt(t2, t2, th, ALU.subtract))
            settle()
            own(tt(fi, t2, t1, ALU.mult))
            settle()
            for k in range(2, 9):
                own(tt(t1, pr(k - 1), pr(1), ALU.mult))
                own(tt(t2, pi(k - 1), pi(1), ALU.mult))
                own(tt(er, pr(k - 1), pi(1), ALU.mult))
                own(tt(sn, pi(k - 1), pr(1), ALU.mult))
                settle()
                own(tt(pr(k), t1, t2, ALU.subtract))
                last = own(tt(pi(k), er, sn, ALU.add))
                settle()
            dve.tensor_copy(t1, pi(8)).then_inc(y_ready, 1)
            dve.wait_ge(pw_sb, 1)
            own(dve.tensor_copy(a8[:, 0, :], PW[:, 8, :]))
            own(dve.tensor_copy(a8[:, 1, :], PW[:, 8, :]))
            own(dve.tensor_copy(a8[:, 2, :], PW[:, 17, :]))
            dve.wait_ge(c_sb, 1)

            def complex_product(out_re, out_im, xr, xi, yr, yi, shape, neg):
                n = 1
                for d in shape:
                    n *= d
                names = dict(zip("abc", shape[1:]))
                tv = lambda j: tm[:, j, 0:n].rearrange("p (z a b) -> p z a b", a=shape[1], b=shape[2]) \
                    if len(shape) == 3 else tm[:, j, 0:n].rearrange("p (z a) -> p z a", a=shape[1])
                own(tt(tv(0), xr, yr, ALU.mult))
                own(tt(tv(1), xi, yi, ALU.mult))
                own(tt(tv(2), xr, yi, ALU.mult))
                own(tt(tv(3), xi, yr, ALU.mult))
                settle()
                own(tt(out_re, tm[:, 0, 0:n], tm[:, 1, 0:n], ALU.subtract))
                if neg:
                    return dve.scalar_tensor_tensor(out=out_im, in0=tm[:, 2, 0:n], scalar=-1.0, in1=tm[:, 3, 0:n],
                                                    op0=ALU.mult, op1=ALU.subtract)
                return tt(out_im, tm[:, 2, 0:n], tm[:, 3, 0:n], ALU.add)

            flat = lambda a: a.rearrange("p q k o -> p (q k o)")
            with dve.Fori(0, GP // QC) as c:
                step.enter(c, 17)
                chunk = lambda t, a: t[:, a, ds(c * QC, QC), :]
                pw = lambda a, k, n: PW[:, 9 * a:9 * a + k, ds(c * QC, QC)].rearrange("p k q -> p q k")\
                    .unsqueeze(3).to_broadcast([P, QC, k, n])
                f = lambda a: PW[:, 18 + a, ds(c * QC, QC)].unsqueeze(2).to_broadcast([P, QC, GS])
                dve.wait_ge(kd_done, c + CREDIT)
                dve.wait_ge(ca_ready, c + CREDIT)
                dve.wait_ge(prep_left, c + CREDIT)
                own(complex_product(bb[:, 0].rearrange("p q i -> p (q i)"), bb[:, 1].rearrange("p q i -> p (q i)"),
                                    f(0), f(1), chunk(Bn, 0), chunk(Bn, 1), (QC, GS), False))
                settle()
                b_ = lambda a: bb[:, a].unsqueeze(2).to_broadcast([P, QC, T, GS])
                own(complex_product(Y[:, 0].rearrange("p q n -> p (q n)"), Y[:, 1].rearrange("p q n -> p (q n)"),
                                    pw(0, T, GS), pw(1, T, GS), b_(0), b_(1), (QC, T, GS), False))
                settle()
                c_ = lambda a: chunk(Cp, a).unsqueeze(2).to_broadcast([P, QC, 9, GS])
                dve.tensor_scalar(bb[:, 1].rearrange("p q i -> p (q i)"), bb[:, 1].rearrange("p q i -> p (q i)"),
                                  1.0, None, ALU.mult).then_inc(y_ready, 1)
                complex_product(flat(CA[:, 0]), flat(CA[:, 1]), pw(0, 9, GS), pw(1, 9, GS), c_(0), c_(1),
                                (QC, 9, GS), True).then_inc(ca_ready, 1)
                step.leave(GP // QC)

            norm(0, D, KT, xT, hT, V_MIX)
            own(dve.memset(acc[:, :], 0.0))
            settle()
            cut_rest(0)
            for m in range(4):
                cut_rest(m + 1)
                add_square(Q_CQ + m, m % 2)
            dve.wait_ge(ss_done, 2)
            own(dve.memset(acc[:, :], 0.0))
            settle()
            for m in range(2):
                cut_rest(5 + m)
                add_square(Q_CKV + m, m % 2)
            norm(1, QL_D, 4, cqT, cqT, V_Q)
            dve.wait_ge(blk_done, B_B)
            bank = pair[(T_A + 6) % 2]
            own(tt(halves(tmpa[64:96, 0, :]), bank[64:96, :, 0:HALF], halves(ropek[64:96, :]), ALU.mult))
            tt(halves(tmpa[64:96, 1, :]), bank[96:128, :, 0:HALF], halves(ropek[96:128, :]), ALU.mult)\
                .then_inc(tile_free, 1)
            settle()
            dve.wait_ge(tile_free, T_B)
            own(tt(kpR[64:96, :], tmpa[64:96, 0, :], tmpa[64:96, 1, :], ALU.add))
            settle()
            for h in range(2):
                own(dve.tensor_copy(kT[64:96, h, :], kpR[64:96, 0:SEQ]))
            dve.tensor_copy(kpeN[0:ROPE, :], kpR[64:96, SEQ:N]).then_inc(kpe_raw, 1)
            norm(2, KV_D, 2, ckvT, ckvT, V_KV)

            dve.wait_ge(out_sem, 16 * 5)

            def unit_max(U_, blk):
                n = (blk + 1) * P
                dve.wait_ge(s_done, U_ + 1)
                dve.wait_ge(p_exp, (U_ if blk == 0 else U_ - 1) + CREDIT)
                dve.tensor_reduce(stat[:, blk % 2:blk % 2 + 1], bank01[:, blk % 2, 0:n], AX.X, ALU.max, negate=True)\
                    .then_inc(nm_ready, 1)

            def unit_scale(U_, blk):
                n = (blk + 1) * P
                dve.wait_ge(p_exp, U_ + 1 + CREDIT)
                b = blk % 2
                own(dve.reciprocal(stat[:, 4 + b:5 + b], stat[:, 2 + b:3 + b]))
                settle()
                dve.tensor_scalar(prob[:, b, 0:n], prob[:, b, 0:n], stat[:, 4 + b:5 + b], None, ALU.mult)\
                    .then_inc(p_sb, 1)

            with dve.Fori(0, PAIRS) as p:
                step.enter(p, 4 + 8)
                for h in range(2):
                    dve.wait_ge(q_done, p * 2 + (h + 1))
                    own(tt(halves(tmpa[64:96, 0, :]), pair[h][64:96, :, 0:HALF], halves(ropeq[64:96, :]), ALU.mult))
                    own(tt(halves(tmpa[64:96, 1, :]), pair[h][96:128, :, 0:HALF], halves(ropeq[96:128, :]), ALU.mult))
                    settle()
                    tt(qT[64:96, h, :], tmpa[64:96, 0, :], tmpa[64:96, 1, :], ALU.add).then_inc(qr_sb, 1)
                    dve.wait_ge(qr_sb, p * 2 + (h + 1))
                dve.wait_ge(v_done, p + 1)
                dve.tensor_copy(V[:, :, :].rearrange("p t n -> p (t n)"), bank45[:, 1, :]).then_inc(v_sb, 1)
                for h in range(2):
                    dve.tensor_copy(QPE[0:ROPE, :].rearrange("p (t h) -> p t h", h=HEADS)[:, :, ds(p * 2 + h, 1)],
                                    qT[64:96, h, SEQ:N].unsqueeze(2)).then_inc(ql_sb, 1)
                dve.wait_ge(ql_done, p + 1)
                for h in range(2):
                    dve.tensor_copy(QL[:, :, :].rearrange("p r (t h) -> p r t h", h=HEADS)[:, :, :, ds(p * 2 + h, 1)],
                                    bank7[:, 2 * h * NS:(2 * h + 2) * NS].rearrange("p (r t o) -> p r t o", r=2, o=1))\
                        .then_inc(ql_sb, 1)
                unit_max(p * 8, 0)
                for u in range(8):
                    if u + 1 < 8:
                        unit_max(p * 8 + (u + 1), (u + 1) % 4)
                    unit_scale(p * 8 + u, u % 4)
                step.leave(PAIRS)

            def keys_turned(i, par, g):
                dve.wait_ge(ct_done, i * 16 + (par * 8 + g + 1))
                dve.wait_ge(sc_done, i * 18 + (par * 9 + max(g - 1, 0)) + CREDIT)
                dve.tensor_copy(kpT[0:ROPE, g % 2, :], bank23[0:ROPE, g % 2, 0:256]).then_inc(kp_sb, 1)

            with dve.Fori(0, DEC_B // 2) as i:
                step.enter(i, 2)
                for par in range(2):
                    keys_turned(i, par, 0)
                    for g in range(9):
                        if g + 1 < 8:
                            keys_turned(i, par, g + 1)
                        n = DEC_Q if g == 8 else 256
                        dve.wait_ge(sc_sb, i * 18 + (par * 9 + g + 1) + CREDIT)
                        dve.tensor_reduce(stat[:, 6 + 9 * par + g:7 + 9 * par + g], S[:, par, g * 256:g * 256 + n],
                                          AX.X, ALU.max).then_inc(gm_done, 1)
                    dve.wait_ge(gm_done, i * 18 + (par * 9 + 9))
                    dve.tensor_reduce(stat[:, 24 + par:25 + par], stat[:, 6 + 9 * par:15 + 9 * par], AX.X, ALU.max,
                                      negate=True).then_inc(dm_ready, 1)
                for par in range(2):
                    dve.wait_ge(d_exp, i * 2 + (par + 1))
                    own(dve.reciprocal(stat[:, 28 + par:29 + par], stat[:, 26 + par:27 + par]))
                    settle()
                    dve.wait_ge(ov_done, i * 2 + (par + 1) + CREDIT)
                    dve.wait_ge(olt_done, i * 2 + par + CREDIT)
                    dve.tensor_scalar(OLn[:, :], bank23[:, 0, 0:256], stat[:, 28 + par:29 + par], None, ALU.mult)\
                        .then_inc(ol_sb, 1)
                    dve.wait_ge(olt_done, i * 2 + (par + 1) + CREDIT)
                    dve.tensor_copy(OLT[:, :, ds(i * 2 + par, 1), :].rearrange("p r o n -> p r (o n)"),
                                    bank23[:, 1, 0:256].rearrange("p (r n) -> p r n", r=2)).then_inc(olt_sb, 1)
                step.leave(DEC_B // 2)

            def residual(m, j):
                x = row(xT, m)
                tt(halves(x), halves(x), pair[j][:, :, 0:HALF], ALU.add).then_inc(tile_free, 1)

            def mlp(i):
                for half in range(2):
                    n0, t0, z0 = B_MLP[i] + 32 * half, T_MLP[i] + 24 * half, 32 * i + 16 * half
                    with dve.Fori(0, 4) as it:
                        for s in range(4):
                            n = it * 4 + (n0 + s)
                            cut_rest(n + 1, (n0 + s + 1) % RAW, (n0 + s + 1) % CUT)
                            dve.wait_ge(tile_free, it * 4 + (t0 + s + 1))
                            dve.wait_ge(z_lo, it * 4 + max(z0 + s - 1, 0) + CREDIT)
                            tt(hid[:, s % 2, :], tmpa[:, s % 2, :], tmpa[:, s % 2, :], ALU.mult).then_inc(z_ready, 1)
                    n0, t0 = n0 + 16, t0 + 16
                    q0 = (Q_MIX1, Q_FIN)[i]
                    if half == 1:
                        clear_acc()

                    def down(it):
                        for j in range(2):
                            for c in range(2):
                                n = it * 4 + (n0 + 2 * j + c)
                                if isinstance(n, int) and n + 1 == B_END:
                                    continue
                                cut_rest(n + 1, (n0 + 2 * j + c + 1) % RAW, (n0 + 2 * j + c + 1) % CUT)
                            dve.wait_ge(blk_done, it * 4 + (n0 + 2 * j + 2))
                            residual(it * 2 + j, (t0 + j) % 2)
                            if half == 1:
                                add_square(it * 2 + (q0 + j), j)

                    final = (i, half) == (1, 1)
                    with dve.Fori(0, 4 - final) as it:
                        down(it)
                    if final:
                        down(3)

            clear_acc()
            cut_rest(B_B)
            for m in range(KT):
                cut_rest(B_B + m + 1)
                dve.wait_ge(blk_done, B_B + m + 1)
                residual(m, (T_B + m) % 2)
                add_square(Q_MLP0 + m, m % 2)
            norm(3, D, KT, xT, hT, V_MLP)
            mlp(0)
            norm(4, D, KT, xT, hT, V_MIX + 8, by_token=True)

            own(dve.memset(Z[:, 0, :, :], 0.0))
            dve.wait_ge(h0_done, 1)
            dve.tensor_copy(Z[:, PC:NC, :, :].rearrange("p b a q -> p a b q"),
                            bank6[:, :].rearrange("p (a b q) -> p a b q", a=2, b=DEC_B)).then_inc(h0_sb, 1)
            dve.wait_ge(xs_sb, 11)
            settle()
            ts = yblk[:, 1, 0, 0:P].rearrange("p (a q) -> p a q", q=GP)
            with dve.Fori(0, PC - 1) as c:
                step.enter(c, 6)
                z = Z[:, ds(c, 1), :, :].rearrange("p o a q -> p (o a) q")
                nxt = Z[:, ds(c + 1, 1), :, :].rearrange("p o a q -> p (o a) q")
                own(tt(ts[:, 0:2, :], a8[:, 0:2, :], z, ALU.mult))
                own(tt(ts[:, 2, :], a8[:, 2, :], z[:, 1, :], ALU.mult))
                own(tt(ts[:, 3, :], a8[:, 2, :], z[:, 0, :], ALU.mult))
                settle()
                own(tt(ts[:, 0:2, :], ts[:, 0:2, :], nxt, ALU.add))
                settle()
                own(tt(nxt[:, 0, :], ts[:, 0, :], ts[:, 2, :], ALU.subtract))
                own(tt(nxt[:, 1, :], ts[:, 1, :], ts[:, 3, :], ALU.add))
                settle()
                step.leave(PC - 1)
            own(dve.memset(ts[:, 0:1, 0:1], 0.0)).wait_ge(dstep, 0) if False else None
            dve.tensor_copy(ts[:, 0, :], a8[:, 0, :]).then_inc(z_state, 1)
            M = DEC_B + 1
            last = Z[:, PC - 1:NC, :, :]
            w = yblk[:, 1, 1:6, :].rearrange("p t n -> p (t n)")[:, 0:2 * M * GP].rearrange("p (a c q) -> p a c q", a=2, q=GP)
            bc = lambda a: a8[:, a, :].unsqueeze(1).to_broadcast([P, M, GP])
            for a in range(2):
                own(tt(XG[:, a], last[:, :, a, :], bc(0), ALU.mult))
                own(tt(w[:, a], last[:, :, 1 - a, :], bc(2), ALU.mult))
            settle()
            for a in range(2):
                own(tt(XG[:, a], XG[:, a], XF[:, :, a, :], ALU.add))
            settle()
            own(tt(XG[:, 0], XG[:, 0], w[:, 0], ALU.subtract))
            own(tt(XG[:, 1], XG[:, 1], w[:, 1], ALU.add))
            settle()
            dve.tensor_copy(rstd[:, 0:1], a8[:, 0, 0:1]).then_inc(f_ready, 1)
            dve.wait_ge(hd_out, 16 * 8)
            for k in range(KT):
                dve.wait_ge(yb_done, k + 1)
                dve.scalar_tensor_tensor(out=halves(hT[:, k, :]), in0=halves(hT[:, k, :]),
                                         scalar=vecs[:, V_D + k:V_D + k + 1], in1=bank45[:, :, 0:HALF],
                                         op0=ALU.mult, op1=ALU.add).then_inc(yb_sb, 1)
            clear_acc()
            for m in range(KT):
                g = tmpa[:, m % 2, :]
                cut_rest(B_GLU + 2 * m + 1)
                cut_rest(B_GLU + 2 * m + 2)
                dve.wait_ge(sig_ready, m + 1)
                tt(halves(g), halves(g), pair[T_GLU % 2][:, :, 0:HALF], ALU.mult).then_inc(tile_free, 2)
                dve.wait_ge(tile_free, T_GLU + 2 * m + 2)
                x = xT[:, m, :].rearrange("p (c s) -> p s c", s=T)
                tt(x, x, g.rearrange("p (s c) -> p s c", s=T), ALU.add).then_inc(x_new, 1)
                add_square(Q_MLP1 + m, m % 2)
            norm(5, D, KT, xT, hT, V_MLP + 8)
            mlp(1)
            norm(6, D, KT, xT, hT, V_FIN)


_INS = ["x_prompt", "x_sample", "cache_ckv", "cache_kpe", "state_ssm_re", "state_ssm_im", "page_table",
        "norm_mix", "norm_mlp", "norm_final", "mla_w_in", "mla_q_norm", "mla_kv_norm", "mla_w_q_up",
        "mla_w_kv_up", "mla_w_o", "ssm_a_re", "ssm_a_im", "ssm_log_dt", "ssm_b_re", "ssm_b_im", "ssm_c_re",
        "ssm_c_im", "ssm_d", "ssm_w_glu", "mlp_w1", "mlp_w2"]
_OUTS = [("y_prompt", (1, SEQ, D)), ("y_sample", (DEC_B, DEC_Q, D)),
         ("prompt_ckv", (1, 1, SEQ, KV_D)), ("prompt_kpe", (1, 1, SEQ, ROPE)),
         ("prompt_ssm_re", (1, 1, GROUPS, ST)), ("prompt_ssm_im", (1, 1, GROUPS, ST)),
         ("sample_ckv", (1, DEC_B, DEC_Q, KV_D)), ("sample_kpe", (1, DEC_B, DEC_Q, ROPE)),
         ("sample_ssm_re", (1, DEC_B, GROUPS, ST)), ("sample_ssm_im", (1, DEC_B, GROUPS, ST))]


def constants():
    import numpy as np
    half = ROPE // 2
    pos = np.concatenate([np.arange(SEQ), PAST + np.tile(np.arange(DEC_Q), DEC_B)]).astype(np.float32)
    inv = np.float32(10000.0) ** (-np.arange(half, dtype=np.float32) / np.float32(half))
    ang = inv[:, None] * pos[None, :]
    cos, sin = np.cos(ang), np.sin(ang)
    rope = np.concatenate([cos, cos, -sin, sin]).astype(np.float32)
    q, k = np.arange(P)[:, None], np.arange(P)[None, :]
    return {
        "c_ident": np.eye(P, dtype=np.float32),
        "c_ropeq": (rope * np.float32(SCALE)).astype(np.float32),
        "c_ropek": rope,
        "c_cmask": np.where(q >= k, 0.0, NEG).astype(np.float32),
        "c_nmask": np.where(q // HEADS >= np.arange(DEC_Q)[None, :], 0.0, NEG).astype(np.float32),
    }


def kernel(**inputs):
    import numpy as np
    import concourse.bacc as bacc
    from concourse.bass_utils import run_bass_kernel_spmd

    nc = bacc.Bacc("TRN2", target_bir_lowering=False, num_devices=1)
    arrays, ins, outs = {}, {}, {}
    for name, a in [(n, inputs[n]) for n in _INS] + list(constants().items()):
        a = np.ascontiguousarray(a)
        arrays[f"in_{name}"] = a
        ins[name] = nc.dram_tensor(f"in_{name}", a.shape, mybir.dt.from_np(a.dtype), kind="ExternalInput").ap()
    for name, shape in _OUTS:
        outs[name] = nc.dram_tensor(f"out_{name}", shape, F32, kind="ExternalOutput").ap()
    build(nc, ins, outs)
    r = run_bass_kernel_spmd(nc, [arrays], core_ids=[0])
    return tuple(r.results[0][f"out_{name}"] for name, _ in _OUTS)
```

```python
from contextlib import ExitStack
import math

import concourse.bass as bass
from concourse import mybir
from concourse.alu_op_type import AluOpType as ALU

F32 = mybir.dt.float32
F32R = mybir.dt.float32r
I32 = mybir.dt.int32
ACT = mybir.ActivationFunctionType
AX = mybir.AxisListType
ds = bass.ds

P = 128
D = 1024
KT = D // P
SEQ, DEC_B, DEC_Q = 512, 8, 8
NS = DEC_B * DEC_Q
N = SEQ + NS
HALF = N // 2
HEADS, NOPE, ROPE, DV = 16, 64, 32, 64
QL_D, KV_D = 512, 256
HD = NOPE + ROPE
SCALE = HD ** -0.5
PAIRS = HEADS // 2
BLK = SEQ // P
PAGES, PAGE = 16, 128
PAST = PAGES * PAGE
FF = 4 * D
EPS = 1e-6
NEG = -1e30

GROUPS, GS, ST = 64, 16, 64
GP = GROUPS // 2
T = 8
NC = N // T
PC = SEQ // T
SPAN = 8
SPANS = PC // SPAN
QC = 4

RAW = 4
CUT = 2
HI, LO = 0, 1
PASSES = ((HI, (HI, LO)), (LO, (HI,)))

V_MIX, V_MLP, V_FIN, V_Q, V_KV, V_D = 0, 16, 32, 40, 44, 46
VROWS = 54


AHEAD = 2
CREDIT = 1


class Tally:

    def __init__(self, sem):
        self.sem, self.n, self.i, self.stride, self.k = sem, 0, None, 0, 0

    def add(self, k=1):
        if self.i is None:
            self.n += k
        else:
            self.k += k

    def now(self, back=0):
        if self.i is None:
            return self.n - back
        return self.i * self.stride + (self.n + self.k - back)

    def enter(self, i, stride):
        self.i, self.stride, self.k = i, stride, 0

    def leave(self, count):
        assert self.k == self.stride, (self.k, self.stride)
        self.n += count * self.stride
        self.i = None


def build(nc, I, O):
    ctx = ExitStack()
    with ctx:
        def sb(name, shape, dt=F32):
            return ctx.enter_context(nc.sbuf_tensor(name, shape, dt))

        def sem(name):
            return ctx.enter_context(nc.semaphore(name))

        def sb_with_parts(name, shape, parts_shape, parts_dt):
            base = (nc.sbuf_base + 31) // 32 * 32
            whole = sb(name, shape)
            return whole, nc.alloc_sbuf_tensor_at(name + "_parts", parts_shape, parts_dt, offset=base)

        arena, zR = sb_with_parts("arena", [P, 18432], [P, FF // P // 2, 2, N], F32R)
        side, hR = sb_with_parts("side", [P, 2 * KT * N], [P, KT, 2, N], F32R)
        xT = sb("xT", [P, KT, N])
        hT = sb("hT", [P, KT, N])
        wraw = sb("wraw", [P, RAW, 8, P])
        wR = sb("wR", [P, CUT, 2, 8, P], F32R)
        yblk = sb("yblk", [P, 2, T, P])
        ident = sb("ident", [P, P])
        ones = sb("ones", [P, P])
        ropeq = sb("ropeq", [P, N])
        ropek = sb("ropek", [P, N])
        cmask = sb("cmask", [P, P])
        nmask = sb("nmask", [P, DEC_Q])
        vecs = sb("vecs", [P, VROWS])
        sq = sb("sq", [P, 2, N])
        kpR = sb("kpR", [P, N])
        acc = sb("acc", [P, N])
        rstd = sb("rstd", [P, N])
        tmpa = sb("tmpa", [P, 2, N])
        a8 = sb("a8", [P, 3, GP])
        stat = sb("stat", [P, 32])
        ptab = sb("ptab", [1, DEC_B * PAGES], I32)

        offset = [0]

        def view(n):
            offset[0] += n
            assert offset[0] <= 18432, offset[0]
            return arena[:, offset[0] - n:offset[0]]

        in_arena = view
        ckvT = view(2 * N).rearrange("p (r n) -> p r n", r=2)
        QL = view(2 * 1024).rearrange("p (r n) -> p r n", r=2)
        QPE = view(1024)
        OLT = view(2 * 1024).rearrange("p (r b n) -> p r b n", r=2, b=DEC_B)
        CN = view(2048).rearrange("p (b n) -> p b n", b=DEC_B)
        KP = view(2 * PAGES * ROPE).rearrange("p (a g n) -> p a g n", a=2, g=PAGES)
        mark = offset[0]
        cqT = view(4 * N).rearrange("p (r n) -> p r n", r=4)
        qT = view(2 * N).rearrange("p (h n) -> p h n", h=2)
        kT = view(2 * SEQ).rearrange("p (h n) -> p h n", h=2)
        V = view(BLK * P).rearrange("p (t n) -> p t n", t=BLK)
        wq = view(4 * 2 * P).rearrange("p (k h n) -> p k h n", k=4, h=2)
        wkv = view(2 * 2 * P).rearrange("p (r c h n) -> p r c h n", r=2, c=2, h=2)
        ukT = view(4 * P).rearrange("p (a n) -> p a n", a=4)
        prob = view(2 * SEQ).rearrange("p (a n) -> p a n", a=2)
        probT = view(2 * SEQ).rearrange("p (a t n) -> p a t n", a=2, t=BLK)
        offset[0] = mark
        SW = PAST + DEC_Q
        S = view(2 * SW).rearrange("p (a n) -> p a n", a=2)
        PT = view(PAST).rearrange("p (g n) -> p g n", g=PAGES)
        PTN = view(P)
        cT = view(2 * 2 * 256).rearrange("p (a r n) -> p a r n", a=2, r=2)
        kpT = view(2 * 256).rearrange("p (a n) -> p a n", a=2)
        QLb = view(2 * 256).rearrange("p (a r n) -> p a r n", a=2, r=2)
        QPb = view(2 * P).rearrange("p (a n) -> p a n", a=2)
        OLn = view(256)
        pages = side[:, 0:8192].rearrange("p (a g n) -> p a g n", a=2, g=PAGES)
        kpeN = sq[:, 0, 0:NS]
        kpeNat = sq[:, 1, 0:(BLK + 1) * ROPE].rearrange("p (t n) -> p t n", n=ROPE)
        ckvNat = tmpa[:, :, 0:512].rearrange("p a (t n) -> p a t n", t=2)
        wkvf = wraw[:, 0:4, :, :].rearrange("p a k n -> p (a k n)").rearrange("p (r n) -> p r n", r=2)
        hid = sq
        offset[0] = 0
        xnat = view((BLK + 1) * D).rearrange("p (t n) -> p t n", n=D)
        nat = view(30 * P).rearrange("p (a n) -> p a n", a=30)
        PW = view(20 * GP).rearrange("p (a q) -> p a q", a=20)
        Bn = view(2 * GP * GS).rearrange("p (a q i) -> p a q i", a=2, q=GP)
        Cn = view(2 * 8 * ST).rearrange("p (a t n) -> p a t n", a=2, t=8)
        Cp = view(2 * GP * GS).rearrange("p (a q i) -> p a q i", a=2, q=GP)
        def step_views():
            return (view(2 * QC * GS).rearrange("p (a q i) -> p a q i", a=2, q=QC),
                    view(2 * QC * P).rearrange("p (a q n) -> p a q n", a=2, q=QC),
                    view(2 * QC * 9 * GS).rearrange("p (a q k o) -> p a q k o", a=2, q=QC, k=9))

        even = step_views()
        tm = view(4 * QC * 9 * GS).rearrange("p (a n) -> p a n", a=4)
        offset[0] = 0
        view = lambda n: (offset.__setitem__(0, offset[0] + n), side[:, offset[0] - n:offset[0]])[1]
        odd = step_views()
        bbs, Ys, CAs = ([even[j], odd[j]] for j in range(3))
        bstcs = [view(2 * QC * P).rearrange("p (a q n) -> p a q n", a=2, q=QC) for _ in range(2)]
        kdcs = [view(2 * QC * P).rearrange("p (q a n) -> p q a n", a=2, q=QC) for _ in range(2)]
        vrow = view(P)
        offset[0] = 0
        view = in_arena
        U = view(GROUPS * NC).rearrange("p (g c) -> p g c", g=GROUPS)
        Z = view(NC * 2 * GP).rearrange("p (c a q) -> p c a q", a=2, q=GP)
        XF = view((DEC_B + 1) * 2 * GP).rearrange("p (c a q) -> p c a q", a=2, q=GP)
        BC = view(2 * GP * P).rearrange("p (a q n) -> p a q n", a=2, q=GP)
        MI = side[:, 0:8192].rearrange("p (g n) -> p g n", g=GROUPS)
        E = side[:, 8192:8192 + 2 * SPAN * GP].rearrange("p (a j q) -> p a j q", a=2, q=GP)
        h0n = yblk[:, 0, 0:4, :]
        XG = tmpa[:, 0, :].rearrange("p (a c q) -> p a c q", a=2, q=GP)

        bank01 = ctx.enter_context(nc.psum_tensor("bank01", [P, 2, 512], F32))
        bank23 = ctx.enter_context(nc.psum_tensor("bank23", [P, 2, 512], F32))
        bank45 = ctx.enter_context(nc.psum_tensor("bank45", [P, 2, 512], F32))
        bank6 = ctx.enter_context(nc.psum_tensor("bank6", [P, 512], F32))
        bank7 = ctx.enter_context(nc.psum_tensor("bank7", [P, 512], F32))
        pair = [bank01, bank23]
        y_banks = [bank01, bank45]
        kd_banks = [(bank23[:, 0, :], bank23[:, 1, :]), (bank6[:, :], bank7[:, :])]

        BSTD = nc.dram_tensor("s5_in_to_state", (P, 2, GP, P), F32, kind="Internal").ap()
        CSD = nc.dram_tensor("s5_state_to_out", (P, 2, GP, P), F32, kind="Internal").ap()
        KD = nc.dram_tensor("s5_lag_kernels", (GROUPS, GS, P), F32, kind="Internal").ap()
        HDR = nc.dram_tensor("s5_input", (D, T, NC), F32, kind="Internal").ap()

        ones_set = sem("ones_set")
        waited = sem("waited")
        const_in = sem("const_in")
        x_in = sem("x_in")
        a_in = sem("a_in")
        s5_in = sem("s5_in")
        vec_done = sem("vec_done")
        vec_sb = sem("vec_sb")
        w_loaded = [sem(f"w_loaded{s}") for s in range(RAW)]
        w_hi = sem("w_hi")
        w_lo = sem("w_lo")
        blk_done = sem("blk_done")
        h_hi, h_lo = sem("h_hi"), sem("h_lo")
        z_hi, z_lo = sem("z_hi"), sem("z_lo")
        tile_done = sem("tile_done")
        tile_free = sem("tile_free")
        sq_ready = sem("sq_ready")
        sq_used = sem("sq_used")
        ss_done = sem("ss_done")
        var_ready = sem("var_ready")
        rstd_ready = sem("rstd_ready")
        h_ready = sem("h_ready")
        z_ready = sem("z_ready")
        sig_ready = sem("sig_ready")
        x_new = sem("x_new")
        dstep = sem("dstep")
        dprep = sem("dprep")
        astep = sem("astep")
        kpe_raw = sem("kpe_raw")
        nat_done, nat_sb, nat_out = sem("nat_done"), sem("nat_sb"), sem("nat_out")
        hw_in, hw_swap = sem("hw_in"), sem("hw_swap")
        q_done, qn_sb, qr_sb = sem("q_done"), sem("qn_sb"), sem("qr_sb")
        k_done, k_sb, v_done, v_sb = sem("k_done"), sem("k_sb"), sem("v_done"), sem("v_sb")
        uk_done, uk_sb, ql_done, ql_sb = sem("uk_done"), sem("uk_sb"), sem("ql_done"), sem("ql_sb")
        s_done, nm_ready, p_exp, p_sb = sem("s_done"), sem("nm_ready"), sem("p_exp"), sem("p_sb")
        t_done, pt_sb, pv_done, o_sb = sem("t_done"), sem("pt_sb"), sem("pv_done"), sem("o_sb")
        tab_in = sem("tab_in")
        page_in = [[sem(f"page_in{a}{c}") for c in range(4)] for a in range(2)]
        keys_in = [sem(f"keys_in{a}") for a in range(2)]
        quarter_used = sem("quarter_used")
        qb_ready = sem("qb_ready")
        ct_done, ct_sb, kp_sb = sem("ct_done"), sem("ct_sb"), sem("kp_sb")
        sc_done, sc_sb, gm_done, dm_ready, d_exp = (sem("sc_done"), sem("sc_sb"), sem("gm_done"),
                                                    sem("dm_ready"), sem("d_exp"))
        dt_done, dt_sb, ov_done, ol_sb, olt_done, olt_sb = (
            sem("dt_done"), sem("dt_sb"), sem("ov_done"), sem("ol_sb"), sem("olt_done"), sem("olt_sb"))
        rl_ready = sem("rl_ready")
        wkvf_in, os_done, os_sb = sem("wkvf_in"), sem("os_done"), sem("os_sb")
        pw_done, pw_sb, c_done, c_sb = sem("pw_done"), sem("pw_sb"), sem("c_done"), sem("c_sb")
        y_ready, yt_done, yt_sb, kd_done, kd_sb = (sem("y_ready"), sem("yt_done"), sem("yt_sb"),
                                                   sem("kd_done"), sem("kd_sb"))
        ca_ready, prep_out, prep_left = sem("ca_ready"), sem("prep_out"), sem("prep_left")
        hd_out, u_in, mi_zero, mi_in, bst_in, cs_in, h0_in = (
            sem("hd_out"), sem("u_in"), sem("mi_zero"), sem("mi_in"), sem("bst_in"), sem("cs_in"),
            sem("h0_in"))
        xs_done, xs_sb, h0_done, z_state = sem("xs_done"), sem("xs_sb"), sem("h0_done"), sem("z_state")
        h0_sb = sem("h0_sb")
        yc_done, yc_sb, yb_done, yb_sb, g_sb = (sem("yc_done"), sem("yc_sb"), sem("yb_done"),
                                                sem("yb_sb"), sem("g_sb"))
        f_ready, f_done, f_sb = sem("f_ready"), sem("f_done"), sem("f_sb")
        out_sem, aprep = sem("out_sem"), sem("aprep")
        y_out = [sem("y_out0"), sem("y_out1")]

        B_A = 0
        B_B = B_A + 7
        B_MLP = [B_B + 8, B_B + 8 + 64 + 16]
        B_GLU = B_MLP[0] + 64
        B_END = B_MLP[1] + 64
        T_X, T_A = 0, 8
        T_B = T_A + 7
        T_MLP = [T_B + 8, T_B + 8 + 48 + 16]
        T_GLU = T_MLP[0] + 48
        T_OUT = T_MLP[1] + 48
        R_A, R_B, R_MLP, R_GLU, R_END = 0, 8, [16, 32], 24, 40
        Q_MIX0, Q_CQ, Q_CKV, Q_MLP0, Q_MIX1, Q_MLP1, Q_FIN, Q_END = 0, 8, 12, 14, 22, 30, 38, 46
        H_MIX0, H_CQ, H_CKV, H_MLP0, H_MIX1, H_MLP1, H_FIN = 0, 8, 12, 14, 22, 30, 38

        def loads(n, raw):
            extra = 32 if raw == 6 % RAW else 0
            if isinstance(n, int):
                return 16 * (n // RAW + 1) + (extra if n >= 6 else 0)
            return n * (16 // RAW) + (16 - (16 // RAW) * raw + extra)

        def halves(t):
            return t.rearrange("p (a n) -> p a n", a=2)

        def row(t, m):
            if isinstance(m, int):
                return t[:, m, :]
            return t[:, ds(m, 1), :].rearrange("p o n -> p (o n)")

        def part_of(t, m, which):
            if isinstance(m, int):
                return t[:, m, which, :]
            return t[:, ds(m, 1), which, :].rearrange("p o n -> p (o n)")

        w_in = I["mla_w_in"][0].rearrange("(k p) n -> p k n", p=P)
        w_qup = I["mla_w_q_up"][0].rearrange("(k p) n -> p k n", p=P)
        w_kvup = I["mla_w_kv_up"][0].rearrange("(r p) n -> p r n", p=P)
        w_o = I["mla_w_o"][0].rearrange("(k p) n -> p k n", p=P)
        w_glu = I["ssm_w_glu"][0].rearrange("(k p) n -> p k n", p=P)
        w_up = [I["mlp_w1"][i].rearrange("(k p) n -> p k n", p=P) for i in range(2)]
        w_down = [I["mlp_w2"][i].rearrange("(k p) n -> p k n", p=P) for i in range(2)]

        def col(w, k0, m):
            return w[:, k0:k0 + 8, m * P:(m + 1) * P] if isinstance(m, int) else w[:, k0:k0 + 8, ds(m * P, P)]

        def apart(eng):
            eng.sem_inc(waited, 1)

        def physical(eng, i, par, g):
            at = i * (2 * PAGES) + (par * PAGES + g)
            return eng.value_load(ptab[0:1, at:at + 1] if isinstance(at, int) else ptab[0:1, ds(at, 1)],
                                  min_val=0, max_val=I["cache_ckv"].shape[1] - 1)

        block = ctx.enter_context(nc.Block())

        @block.sync
        def _(sp):
            def load_block(n, src, slot=None):
                slot = n % RAW if slot is None else slot
                sp.wait_ge(w_hi, n - RAW + 1)
                sp.wait_ge(w_lo, n - RAW + 1)
                sp.dma_start(wraw[:, slot, :, :], src).then_inc(w_loaded[slot], 16)

            flat = lambda a: a[0].rearrange("g p -> (g p)").rearrange("(q n) -> q n", n=P)
            sp.dma_start(nat[0:GP, 0, :], flat(I["ssm_a_re"])).then_inc(a_in, 16)
            sp.dma_start(nat[0:GP, 1, :], flat(I["ssm_a_im"])).then_inc(a_in, 16)
            sp.dma_start(nat[0:GP, 2, 0:2], I["ssm_log_dt"][0].rearrange("(q a) -> q a", a=2)).then_inc(a_in, 16)
            sp.dma_start(ident[:, :], I["c_ident"]).then_inc(const_in, 16)
            sp.dma_start(ropeq[64:128, :], I["c_ropeq"]).then_inc(const_in, 16)
            sp.dma_start(ropek[64:128, :], I["c_ropek"]).then_inc(const_in, 16)
            sp.dma_start(cmask[:, :], I["c_cmask"]).then_inc(const_in, 16)
            sp.dma_start(nmask[:, :], I["c_nmask"]).then_inc(const_in, 16)
            at = 0
            for name, k in (("norm_mix", 16), ("norm_mlp", 16), ("norm_final", 8), ("mla_q_norm", 4),
                            ("mla_kv_norm", 2), ("ssm_d", 8)):
                a = I[name]
                if len(a.shape) == 2:
                    a = a.rearrange("a b -> (a b)")
                sp.dma_start(vrow[at:at + k, :], a.rearrange("(k p) -> k p", p=P)).then_inc(const_in, 16)
                at += k
            sp.dma_start(ptab[:, :], I["page_table"].rearrange("a b -> (a b)").rearrange("(o n) -> o n", o=1))\
                .then_inc(tab_in, 16)
            sp.dma_start(xnat[:, 0:BLK, :], I["x_prompt"][0].rearrange("(t p) n -> p t n", p=P)).then_inc(x_in, 16)
            sp.dma_start(xnat[0:NS, BLK, :], I["x_sample"].rearrange("b q n -> (b q) n")).then_inc(x_in, 16)
            for m in range(4):
                sp.dma_start(wraw[:, m, :, :], col(w_in, 0, m)).then_inc(w_loaded[m], 16)
            for a, part in enumerate(("re", "im")):
                sp.dma_start(Bn[:, a, :, :], I[f"ssm_b_{part}"][0].rearrange("g p i -> (g p) i")
                             .rearrange("(q n) i -> n q i", n=P)).then_inc(s5_in, 16)
                sp.dma_start(Cn[:, a, :, :], I[f"ssm_c_{part}"][0].rearrange("g o p -> (g o) p")
                             .rearrange("(t m) p -> m t p", m=P)).then_inc(s5_in, 16)
            for m in (4, 5):
                load_block(m, col(w_in, 0, m))
            sp.wait_ge(w_hi, 3)
            sp.wait_ge(w_lo, 3)
            c0 = QL_D + KV_D
            sp.dma_start(wraw[:, 2, :, 64:96], w_in[:, :, c0:c0 + 32]).then_inc(w_loaded[2], 16)
            sp.dma_start(wraw[:, 2, :, 96:112], w_in[:, :, c0 + 16:c0 + 32]).then_inc(w_loaded[2], 16)
            sp.dma_start(wraw[:, 2, :, 112:128], w_in[:, :, c0:c0 + 16]).then_inc(w_loaded[2], 16)
            sp.wait_ge(prep_left, GP // QC + AHEAD)
            sp.wait_ge(tile_free, T_X + 8)

            def pair_weights(p):
                for h in range(2):
                    sp.dma_start(wq[:, :, h, 0:HD], w_qup[:, :, ds(p * (2 * HD) + h * HD, HD)]).then_inc(hw_in, 16)
                for r in range(2):
                    for c in range(2):
                        sp.dma_start(wkv[:, r, c, :, :],
                                     w_kvup[:, r, ds(p * (2 * P), 2 * P)].rearrange("p (h c n) -> p c h n", h=2, c=2)
                                     [:, c]).then_inc(hw_in, 16)

            with sp.Fori(0, PAIRS) as p:
                sp.wait_ge(uk_done, p + CREDIT)
                pair_weights(p)
            sp.wait_ge(tab_in, 16)
            sp.wait_ge(blk_done, B_B)


            def load_pages(i, par):
                for c in range(4):
                    if not isinstance(i, int):
                        sp.wait_ge(quarter_used, i * 8 + (4 * par + c - 7))
                        apart(sp)
                    for g in range(4 * c, 4 * c + 4):
                        sp.dma_start(pages[:, par, g, :],
                                     I["cache_ckv"][0][ds(physical(sp, i, par, g), 1)].rearrange("o p n -> (o p) n"))\
                            .then_inc(page_in[par][c], 16)

            for par in range(2):
                load_pages(0, par)
            with sp.Fori(1, DEC_B // 2) as i:
                for par in range(2):
                    load_pages(i, par)
            sp.wait_ge(w_hi, B_B)
            sp.wait_ge(w_lo, B_B)
            sp.dma_start(wkvf[:, :, :], w_kvup).then_inc(wkvf_in, 16)
            sp.wait_ge(os_done, 1)
            for m in range(RAW):
                sp.dma_start(wraw[:, (B_B + m) % RAW, :, :], col(w_o, 0, m)).then_inc(w_loaded[(B_B + m) % RAW], 16)
            for m in range(RAW, 8):
                load_block(B_B + m, col(w_o, 0, m))

            def load_mlp(i):
                for half in range(2):
                    n0 = B_MLP[i] + 32 * half
                    with sp.Fori(0, 4) as it:
                        for s in range(4):
                            load_block(it * 4 + (n0 + s), w_up[i][:, :, ds(it * (4 * P) + (16 * half + s) * P, P)],
                                       (n0 + s) % RAW)
                    n0 += 16
                    with sp.Fori(0, 4) as it:
                        for s in range(4):
                            k0 = 16 * half + 8 * (s % 2)
                            load_block(it * 4 + (n0 + s), w_down[i][:, k0:k0 + 8, ds(it * (2 * P) + (s // 2) * P, P)],
                                       (n0 + s) % RAW)

            load_mlp(0)
            for s in range(4):
                load_block(B_GLU + s, w_glu[:, :, (s // 2) * P + (s % 2) * D:(s // 2 + 1) * P + (s % 2) * D])
            sp.wait_ge(blk_done, B_GLU)
            sp.wait_ge(prep_left, GP // QC + AHEAD)
            sp.dma_start(BC[:, :, :, :], BSTD[:, :, :, :]).then_inc(bst_in, 16)
            for a, part in enumerate(("re", "im")):
                sp.dma_start(h0n[:, 2 * a:2 * a + 2, :],
                             I[f"state_ssm_{part}"][0].rearrange("b g p -> (b g p)")
                             .rearrange("(t m n) -> m t n", m=P, n=P)).then_inc(h0_in, 16)
            sp.wait_ge(hd_out, 16 * 8)
            for r in range(T):
                sp.dma_start(U[GS * r:GS * r + GS, :, :],
                             HDR[:, T - 1 - r, :].rearrange("(g i) c -> i g c", i=GS)).then_inc(u_in, 16)
            sp.wait_ge(xs_done, 11)
            sp.dma_start(BC[:, :, :, :], CSD[:, :, :, :]).then_inc(cs_in, 16)
            with sp.Fori(1, 4) as it:
                for s in range(4):
                    load_block(it * 4 + (B_GLU + s), w_glu[:, :, ds(it * (2 * P) + (s // 2) * P + (s % 2) * D, P)],
                               (B_GLU + s) % RAW)
            load_mlp(1)

        @block.gpsimd
        def _(pool):
            pool.sem_inc(prep_left, AHEAD)
            pool.sem_inc(z_lo, CREDIT)
            pool.memset(ones[:, :], 1.0).then_inc(ones_set, 1)
            with pool.Fori(0, GP // QC // 2) as i:
                for par in range(2):
                    c = i * 2 + par
                    bstc, kdc, CA = bstcs[par], kdcs[par], CAs[par]
                    pool.wait_ge(yt_sb, c + (1 + AHEAD))
                    apart(pool)
                    pool.dma_start(BSTD[:, :, ds(c * QC, QC), :], bstc[:, :, :, :]).then_inc(prep_out, 16)
                    pool.wait_ge(ca_ready, c + (1 + CREDIT))
                    apart(pool)
                    for a in range(2):
                        pool.dma_start(CSD[:, a, ds(c * QC, QC), :],
                                       CA[:, a, :, 1:9, :].rearrange("p q k o -> p q (k o)")).then_inc(prep_out, 16)
                    pool.wait_ge(kd_sb, c + (1 + AHEAD))
                    apart(pool)
                    pool.dma_start(KD.rearrange("g i n -> i g n")[:, ds(c * (2 * QC), 2 * QC), :],
                                   kdc[0:GS].rearrange("p q a n -> p (q a) n")).then_inc(prep_out, 16)
                    pool.wait_ge(prep_out, c * 64 + 64)
                    pool.sem_inc(prep_left, 1)

            def rest_of(n0, mask=None):
                for k in range(KT):
                    pool.wait_ge(h_hi, n0 + k + 1)
                    pool.tensor_tensor(hR[:, k, LO, :], hT[:, k, :], hR[:, k, HI, :].bitcast(F32), ALU.subtract)\
                        .then_inc(h_lo, 1)

            rest_of(R_A)
            pool.wait_ge(nat_sb, 5)
            pool.dma_start(O["sample_kpe"].rearrange("a b q n -> (a b q) n"), kpeNat[0:NS, BLK, :]).then_inc(out_sem, 16)
            pool.dma_start(O["prompt_kpe"][0, 0].rearrange("(t p) n -> p t n", p=P), kpeNat[:, 0:BLK, :])\
                .then_inc(out_sem, 16)
            pool.dma_start(O["prompt_ckv"][0, 0].rearrange("(a t p) n -> p a t n", a=2, p=P)[:, 0],
                           ckvNat[:, 0, :, :]).then_inc(out_sem, 16)
            pool.dma_start(O["prompt_ckv"][0, 0].rearrange("(a t p) n -> p a t n", a=2, p=P)[:, 1],
                           ckvNat[:, 1, :, :]).then_inc(out_sem, 16)
            pool.wait_ge(nat_sb, 9)
            pool.dma_start(O["sample_ckv"][0].rearrange("b q n -> q b n"), CN[0:DEC_Q, :, :]).then_inc(out_sem, 16)
            pool.wait_ge(out_sem, 16 * 5)
            with pool.Fori(0, PAIRS) as p:
                pool.wait_ge(hw_in, p * 96 + 96)
                apart(pool)
                pool.tensor_copy(wq[:, :, :, 96:112], wq[:, :, :, 80:96]).then_inc(hw_swap, 1)
                pool.tensor_copy(wq[:, :, :, 112:128], wq[:, :, :, 64:80]).then_inc(hw_swap, 1)
            def load_keys(i, par):
                for g in range(PAGES):
                    pool.dma_start(KP[:, par, g, :],
                                   I["cache_kpe"][0][ds(physical(pool, i, par, g), 1)].rearrange("o p n -> (o p) n"))\
                        .then_inc(keys_in[par], 16)

            pool.wait_ge(tab_in, 16)
            for par in range(2):
                load_keys(0, par)
            pool.wait_ge(ql_sb, 4 * PAIRS + CREDIT)
            pool.wait_ge(o_sb, 2 * PAIRS + CREDIT)

            def fix_queries(b, par):
                pool.tensor_copy(QLb[:, par, :, :], QL[:, :, b * P:(b + 1) * P] if isinstance(b, int) else
                                 QL[:, :, ds(b * P, P)]).then_inc(qb_ready, 1)
                pool.tensor_copy(QPb[0:ROPE, par, :], QPE[0:ROPE, b * P:(b + 1) * P] if isinstance(b, int) else
                                 QPE[0:ROPE, ds(b * P, P)]).then_inc(qb_ready, 1)

            for par in range(2):
                fix_queries(par, par)
            with pool.Fori(1, DEC_B // 2) as i:
                for par in range(2):
                    pool.wait_ge(sc_done, i * 18 + (9 * par - 9) + CREDIT)
                    apart(pool)
                    fix_queries(i * 2 + par, par)
                    load_keys(i, par)
            rest_of(R_B)

            def rest_of_hidden(i):
                for half in range(2):
                    z0 = 32 * i + 16 * half
                    with pool.Fori(0, 8) as it:
                        for s in range(2):
                            pool.wait_ge(z_hi, it * 2 + (z0 + s + 1))
                            apart(pool)
                            m = it * 2 + s
                            pool.tensor_tensor(part_of(zR, m, LO), hid[:, s, :], part_of(zR, m, HI).bitcast(F32),
                                               ALU.subtract).then_inc(z_lo, 1)

            rest_of(R_MLP[0])
            rest_of_hidden(0)
            pool.wait_ge(blk_done, B_MLP[0] + 48)
            pool.memset(MI[:, :, :], 0.0).then_inc(mi_zero, 1)
            pool.wait_ge(mi_zero, 1)
            for r in range(T):
                s = T - 1 - r
                pool.dma_start(MI[GS * r:GS * r + GS, :, GS * s:P],
                               KD.rearrange("g i n -> i g n")[:, :, 0:P - GS * s]).then_inc(mi_in, 16)
            for k in range(KT):
                pool.wait_ge(h_ready, H_MIX1 + k + 1)
                pool.dma_start(HDR[k * P:(k + 1) * P].rearrange("p s c -> p (s c)"), hT[:, k, :]).then_inc(hd_out, 16)
            pool.wait_ge(f_sb, 2)
            for a, part in enumerate(("re", "im")):
                pool.dma_start(O[f"sample_ssm_{part}"][0].rearrange("b g p -> (b g p)")
                               .rearrange("(t m n) -> m t n", m=P, n=P),
                               tmpa[:, 1, a * 256:a * 256 + 256].rearrange("p (t n) -> p t n", t=2)).then_inc(out_sem, 16)
                pool.dma_start(O[f"prompt_ssm_{part}"][0, 0].rearrange("g p -> (g p)").rearrange("(q n) -> q n", n=P),
                               sq[0:GP, 0, a * P:a * P + P]).then_inc(out_sem, 16)
            rest_of(R_GLU)
            rest_of(R_MLP[1])
            rest_of_hidden(1)
            for j in range(BLK + 1):
                pool.wait_ge(tile_free, T_OUT + j + 1)
                dst = O["y_prompt"][0, j * P:(j + 1) * P, :] if j < BLK else O["y_sample"].rearrange("b q n -> (b q) n")
                rows = P if j < BLK else NS
                pool.dma_start(dst, arena[0:rows, (j % 2) * D:(j % 2) * D + D]).then_inc(y_out[j % 2], 16)
            pool.wait_ge(out_sem, 16 * (5 + 4))
            pool.wait_ge(y_out[0], 16 * 3)
            pool.wait_ge(y_out[1], 16 * 2)

        @block.tensor
        def _(pe):
            for s in (t_done, pv_done, sc_done, dt_done, ov_done, olt_done, uk_done):
                pe.sem_inc(s, CREDIT)
            pe.sem_inc(kd_done, AHEAD)
            def transpose(out, in_, rows=None):
                k = in_.shape[0]
                b = in_.base_partition()
                return pe.transpose(out, in_, ident[b:b + k, b:b + k])

            pe.wait_ge(const_in, 16 * 11)
            pe.wait_ge(ones_set, 1)
            transpose(bank6[:, 0:VROWS], vrow[0:VROWS, :]).then_inc(vec_done, 1)
            pe.wait_ge(x_in, 32)
            for k in range(KT):
                if k >= 2:
                    pe.wait_ge(tile_free, k - 1)
                for j in range(BLK):
                    transpose(pair[k % 2][:, 0, j * P:(j + 1) * P], xnat[:, j, k * P:(k + 1) * P])
                transpose(pair[k % 2][:, 1, 0:NS], xnat[0:NS, BLK, k * P:(k + 1) * P]).then_inc(tile_done, 1)

            pe.wait_ge(tile_free, 8)
            pe.wait_ge(y_ready, 1)
            for a in range(20):
                ins = transpose(pair[0][:, a // 16, (a % 16) * GP:(a % 16) * GP + GP], nat[0:GP, 3 + a, :])
            ins.then_inc(pw_done, 1)
            pe.wait_ge(s5_in, 16 * 4)
            for a in range(2):
                for t in range(8):
                    ins = transpose([bank23, bank45][a][0:ST, t // 4, (t % 4) * P:(t % 4 + 1) * P], Cn[:, a, t, :])
            ins.then_inc(c_done, 1)
            pe.wait_ge(pw_sb, 1)
            pe.wait_ge(c_sb, 1)
            with pe.Fori(0, GP // QC // 2) as i:
                for par in range(2):
                    c = i * 2 + par
                    bb, Y, CA = bbs[par], Ys[par], CAs[par]
                    pe.wait_ge(y_ready, c + 2)
                    pe.wait_ge(yt_sb, c + (AHEAD - 1))
                    for a in range(2):
                        for q in range(QC):
                            ins = transpose(y_banks[par][:, a, q * P:(q + 1) * P], Y[:, a, q, :])
                    ins.then_inc(yt_done, 1)
                    pe.wait_ge(ca_ready, c + (1 + CREDIT))
                    pe.wait_ge(kd_sb, c + (AHEAD - 1))
                    apart(pe)
                    for half in range(2):
                        for q in range(QC):
                            for a in range(2):
                                rows = slice(64 * half, 64 * half + 64)
                                ins = pe.matmul(kd_banks[par][half][0:GS, q * P:(q + 1) * P], bb[rows, a, q, :],
                                                CA[rows, a, q, 0:8, :].rearrange("p k o -> p (k o)"),
                                                start=(a == 0), stop=(a == 1))
                    ins.then_inc(kd_done, 1)
            pe.wait_ge(kd_sb, GP // QC + AHEAD)

            def sum_squares(n, q_end):
                pe.wait_ge(sq_used, q_end)
                for a in range(2):
                    ins = pe.matmul(bank45[:, a, 0:HALF], ones[:, :], acc[:, a * HALF:(a + 1) * HALF],
                                    start=True, stop=True)
                ins.then_inc(ss_done, 1)

            def block_mm(n, bank, tokens, first, last, s=None, m=slice(0, P)):
                s = n % CUT if s is None else s
                pe.wait_ge(w_hi, n + 1)
                pe.wait_ge(w_lo, n + 1)
                for k in range(8):
                    for wp, parts in PASSES:
                        for xp in parts:
                            for a in range(2):
                                ins = pe.matmul(bank[:, a, 0:HALF], wR[:, s, wp, k, :],
                                                tokens(k, xp)[:, a * HALF:(a + 1) * HALF],
                                                start=(first and k == 0 and (wp, xp) == (HI, HI)),
                                                stop=(last and k == 7 and wp == LO))
                ins.then_inc(blk_done, 1)

            from_h = lambda k, xp: hR[:, k, xp, :]

            sum_squares(0, Q_CQ)
            for m in range(7):
                if m == 5:
                    sum_squares(1, Q_CKV)
                pe.wait_ge(tile_free, T_A + m - 1)
                if m == 0:
                    pe.wait_ge(h_hi, R_A + 8)
                    pe.wait_ge(h_lo, R_A + 8)
                block_mm(B_A + m, pair[(T_A + m) % 2], from_h, True, True)
            pe.wait_ge(var_ready, 2)
            sum_squares(2, Q_MLP0)
            pe.wait_ge(tile_free, T_B)

            pe.wait_ge(h_ready, H_CKV + 2)
            pe.wait_ge(kpe_raw, 1)
            for j in range(BLK):
                if j >= 2:
                    pe.wait_ge(nat_sb, j - 1)
                for r in range(2):
                    transpose(pair[j % 2][:, 0, r * P:(r + 1) * P], ckvT[:, r, j * P:(j + 1) * P])
                transpose(pair[j % 2][:, 0, 256:256 + ROPE], kpR[64:96, j * P:(j + 1) * P]).then_inc(nat_done, 1)
            pe.wait_ge(nat_sb, 4)
            transpose(pair[0][0:NS, 0, 0:ROPE], kpR[64:96, SEQ:N]).then_inc(nat_done, 1)
            for j in range(4):
                for b in (2 * j, 2 * j + 1):
                    for r in range(2):
                        dst = [bank45[:, 0, :], bank45[:, 1, :], bank6[:, :], bank7[:, :]][j]
                        ins = transpose(dst[0:DEC_Q, (b % 2) * 256 + r * P:(b % 2) * 256 + (r + 1) * P],
                                        ckvT[:, r, SEQ + b * DEC_Q:SEQ + (b + 1) * DEC_Q])
                ins.then_inc(nat_done, 1)
            pe.wait_ge(nat_sb, 9)

            pe.wait_ge(h_ready, H_CQ + 4)

            def unit_scores(U_, h, blk):
                pe.wait_ge(p_exp, (U_ if blk == 0 else U_ - 1) + CREDIT)
                n = (blk + 1) * P
                bank = bank01[:, blk % 2, :]
                pe.matmul(bank[:, 0:n], qT[0:HD, h, blk * P:(blk + 1) * P], kT[0:HD, h, 0:n],
                          start=True, stop=False)
                pe.matmul(bank[:, blk * P:n], ident[:, :], cmask[:, :], start=False, stop=True).then_inc(s_done, 1)

            def unit_turn(U_, blk):
                pe.wait_ge(p_sb, U_ + 1)
                for t in range(blk + 1):
                    ins = transpose(bank23[:, blk % 2, t * P:(t + 1) * P], prob[:, blk % 2, t * P:(t + 1) * P])
                ins.then_inc(t_done, 1)

            def unit_values(U_, h, blk):
                pe.wait_ge(pt_sb, U_ + 1)
                for t in range(blk + 1):
                    ins = pe.matmul(bank45[64 * h:64 * h + 64, 0, blk * P:(blk + 1) * P],
                                    V[:, t, 64 * h:64 * h + 64], probT[:, blk % 2, t, :],
                                    start=(t == 0), stop=(t == blk))
                ins.then_inc(pv_done, 1)

            with pe.Fori(0, PAIRS) as p:
                pe.wait_ge(hw_in, p * 96 + 96)
                pe.wait_ge(hw_swap, p * 2 + 2)
                for h in range(2):
                    for a in range(2):
                        for k in range(4):
                            ins = pe.matmul(pair[h][:, a, 0:HALF], wq[:, k, h, :], cqT[:, k, a * HALF:(a + 1) * HALF],
                                            start=(k == 0), stop=(k == 3))
                    ins.then_inc(q_done, 1)
                pe.wait_ge(o_sb, p * 2 + CREDIT)
                for r in range(2):
                    ins = pe.matmul(bank45[:, 0, :], wkv[:, r, 0, :, :].rearrange("p h n -> p (h n)"), ckvT[:, r, 0:SEQ],
                                    start=(r == 0), stop=(r == 1))
                ins.then_inc(k_done, 1)
                for t in range(BLK):
                    for r in range(2):
                        ins = pe.matmul(bank45[:, 1, t * P:(t + 1) * P], ckvT[:, r, t * P:(t + 1) * P],
                                        wkv[:, r, 1, :, :].rearrange("p h n -> p (h n)"), start=(r == 0), stop=(r == 1))
                ins.then_inc(v_done, 1)
                for h in range(2):
                    for r in range(2):
                        ins = transpose(bank6[0:NOPE, (2 * h + r) * P:(2 * h + r + 1) * P], wkv[:, r, 0, h, :])
                ins.then_inc(uk_done, 1)
                pe.wait_ge(uk_sb, p + 1)
                pe.wait_ge(qn_sb, p * 2 + 2)
                pe.wait_ge(ql_sb, p * 4 + CREDIT)
                for h in range(2):
                    for r in range(2):
                        ins = pe.matmul(bank7[:, (2 * h + r) * NS:(2 * h + r + 1) * NS], ukT[0:NOPE, 2 * h + r, :],
                                        qT[0:NOPE, h, SEQ:N], start=True, stop=True)
                ins.then_inc(ql_done, 1)
                pe.wait_ge(qr_sb, p * 2 + 2)
                pe.wait_ge(k_sb, p * 2 + 2)
                units = [(h, blk) for h in range(2) for blk in range(BLK)]
                unit_scores(p * 8, 0, 0)
                for u, (h, blk) in enumerate(units):
                    if u + 1 < 8:
                        unit_scores(p * 8 + (u + 1), *units[u + 1])
                    unit_turn(p * 8 + u, blk)
                    if u == 0:
                        pe.wait_ge(v_sb, p + 1)
                    if u >= 1:
                        unit_values(p * 8 + (u - 1), *units[u - 1])
                unit_values(p * 8 + 7, *units[7])

            def turn_pages(b, par, g):
                if g % 2 == 0:
                    pe.wait_ge(page_in[par][g // 2], b * 32 + (64 - 32 * par))
                if g == 0:
                    pe.wait_ge(keys_in[par], b * 128 + (256 - 128 * par))
                if not (isinstance(b, int) and b == 0 and g < 2):
                    pe.wait_ge(ct_sb, b * 8 + (g - 1))
                    pe.wait_ge(kp_sb, b * 8 + (g - 1))
                for j in range(2):
                    for r in range(2):
                        transpose(bank01[:, g % 2, r * 256 + j * P:r * 256 + (j + 1) * P],
                                  pages[:, par, 2 * g + j, r * P:(r + 1) * P])
                for j in range(2):
                    ins = transpose(bank23[0:ROPE, g % 2, j * P:(j + 1) * P], KP[:, par, 2 * g + j, :])
                ins.then_inc(ct_done, 1)

            def group_scores(b, par, g):
                n = DEC_Q if g == 8 else 256
                bank = bank45[:, g % 2, 0:n]
                if g < 8:
                    pe.wait_ge(ct_sb, b * 8 + (g + 1))
                    pe.wait_ge(kp_sb, b * 8 + (g + 1))
                pe.wait_ge(sc_sb, b * 9 + (g - 1 if g >= 2 else 0) + CREDIT)
                new = b * DEC_Q
                for r in range(2):
                    if g < 8:
                        rhs = cT[:, g % 2, r, :]
                    elif isinstance(b, int):
                        rhs = ckvT[:, r, SEQ + new:SEQ + new + DEC_Q]
                    else:
                        rhs = ckvT[:, r, ds(new + SEQ, DEC_Q)]
                    pe.matmul(bank, QLb[:, par, r, :], rhs, start=(r == 0), stop=False)
                if g < 8:
                    rhs = kpT[0:ROPE, g % 2, :]
                elif isinstance(b, int):
                    rhs = kpeN[0:ROPE, new:new + DEC_Q]
                else:
                    rhs = kpeN[0:ROPE, ds(new, DEC_Q)]
                ins = pe.matmul(bank, QPb[0:ROPE, par, :], rhs, start=False, stop=(g < 8))
                if g == 8:
                    ins = pe.matmul(bank, ident[:, :], nmask[:, :], start=False, stop=True)
                ins.then_inc(sc_done, 1)

            def scores(b, par):
                pe.wait_ge(qb_ready, b * 2 + 2)
                turn_pages(b, par, 0)
                pe.wait_ge(olt_sb, b + (CREDIT - 1) if not isinstance(b, int) else max(b - 1, 0) + CREDIT)
                for g in range(9):
                    if g + 1 < 8:
                        turn_pages(b, par, g + 1)
                    group_scores(b, par, g)

            def values(b, par):
                pe.wait_ge(d_exp, b + 1)
                for j in range(5):
                    bank = [bank6, bank7][j % 2]
                    pe.wait_ge(dt_sb, b * 5 + max(j - 1, 0) + CREDIT)
                    if j < 4:
                        for t in range(4):
                            c0 = (4 * j + t) * P
                            ins = transpose(bank[:, t * P:(t + 1) * P], S[:, par, c0:c0 + P])
                    else:
                        ins = transpose(bank[0:DEC_Q, 0:P], S[:, par, PAST:PAST + DEC_Q])
                    ins.then_inc(dt_done, 1)
                pe.wait_ge(olt_sb, b + CREDIT)
                for g in range(PAGES):
                    if g % 4 == 0:
                        pe.wait_ge(dt_sb, b * 5 + (g // 4 + 1) + CREDIT)
                    ins = pe.matmul(bank23[:, 0, 0:256], PT[:, g, :], pages[:, par, g, :], start=(g == 0), stop=False)
                    if g % 4 == 3:
                        ins.then_inc(quarter_used, 1)
                pe.wait_ge(dt_sb, b * 5 + 5 + CREDIT)
                new = CN[0:DEC_Q, b, :] if isinstance(b, int) else CN[0:DEC_Q, ds(b, 1), :].rearrange("p o n -> p (o n)")
                pe.matmul(bank23[:, 0, 0:256], PTN[0:DEC_Q, :], new, start=False, stop=True).then_inc(ov_done, 1)
                pe.wait_ge(ol_sb, b + 1)
                for r in range(2):
                    ins = transpose(bank23[:, 1, r * P:(r + 1) * P], OLn[:, r * P:(r + 1) * P])
                ins.then_inc(olt_done, 1)

            pe.wait_ge(o_sb, 2 * PAIRS + CREDIT)
            pe.wait_ge(ql_sb, 4 * PAIRS + CREDIT)
            scores(0, 0)
            with pe.Fori(0, DEC_B // 2 - 1) as i:
                scores(i * 2 + 1, 1)
                values(i * 2, 0)
                scores(i * 2 + 2, 0)
                values(i * 2 + 1, 1)
            scores(DEC_B - 1, 1)
            values(DEC_B - 2, 0)
            values(DEC_B - 1, 1)
            pe.wait_ge(olt_sb, DEC_B + CREDIT)
            pe.wait_ge(wkvf_in, 16)
            for h in range(HEADS):
                for r in range(2):
                    ins = pe.matmul(bank01[64 * (h % 2):64 * (h % 2) + 64, 0, (h // 2) * NS:(h // 2 + 1) * NS],
                                    wkvf[:, r, h * P + NOPE:(h + 1) * P],
                                    OLT[:, r, :, :].rearrange("p b (q h) -> p b q h", h=HEADS)[:, :, :, h],
                                    start=(r == 0), stop=(r == 1))
            ins.then_inc(os_done, 1)

            pe.wait_ge(h_hi, R_B + 8)
            pe.wait_ge(h_lo, R_B + 8)
            for m in range(8):
                pe.wait_ge(tile_free, T_B + m - 1)
                block_mm(B_B + m, pair[(T_B + m) % 2], from_h, True, True)

            def mlp(i):
                pe.wait_ge(h_hi, R_MLP[i] + 8)
                pe.wait_ge(h_lo, R_MLP[i] + 8)
                for half in range(2):
                    n0, t0, z0 = B_MLP[i] + 32 * half, T_MLP[i] + 24 * half, 32 * i + 16 * half
                    with pe.Fori(0, 4) as it:
                        for s in range(4):
                            pe.wait_ge(tile_free, it * 4 + (t0 + s - 1))
                            block_mm(it * 4 + (n0 + s), pair[(t0 + s) % 2], from_h, True, True, (n0 + s) % CUT)
                    pe.wait_ge(z_lo, z0 + 16 + CREDIT)
                    pe.wait_ge(z_hi, z0 + 16)
                    n0, t0 = n0 + 16, t0 + 16
                    with pe.Fori(0, 4) as it:
                        for s in range(4):
                            if s % 2 == 0:
                                pe.wait_ge(tile_free, it * 2 + (t0 + s // 2 - 1))
                            block_mm(it * 4 + (n0 + s), pair[(t0 + s // 2) % 2],
                                     lambda k, xp, c=s % 2: zR[:, 8 * c + k, xp, :],
                                     s % 2 == 0, s % 2 == 1, (n0 + s) % CUT)

            sum_squares(3, Q_MIX1)
            mlp(0)
            sum_squares(4, Q_MLP1)

            pe.wait_ge(h0_in, 32)
            pe.wait_ge(tile_free, T_GLU)
            for a in range(2):
                for t in range(2):
                    ins = transpose(bank6[:, (2 * a + t) * P:(2 * a + t + 1) * P], h0n[:, 2 * a + t, :])
            ins.then_inc(h0_done, 1)
            pe.wait_ge(bst_in, 16)
            pe.wait_ge(u_in, 16 * T)
            for j in range(11):
                qs = range(3 * j, min(3 * j + 3, GP))
                if j >= 2:
                    pe.wait_ge(xs_sb, j - 1)
                for q in qs:
                    for half in range(2):
                        for a in range(2):
                            ins = pe.matmul(bank01[64 * half:64 * half + 64, j % 2,
                                                   ((q % 3) * 2 + a) * NC:((q % 3) * 2 + a + 1) * NC],
                                            BC[:, a, q, 64 * half:64 * half + 64], U[:, 2 * q + half, :],
                                            start=True, stop=True)
                ins.then_inc(xs_done, 1)
            pe.wait_ge(cs_in, 16)
            pe.wait_ge(mi_in, 16 * T)
            pe.wait_ge(z_state, 1)

            def chunk_outputs(k):
                banks = pair[k % 2]
                if k >= 2:
                    pe.wait_ge(yc_sb, k - 1)
                for q4 in range(4):
                    for half in range(2):
                        q = 4 * k + q4
                        rows = slice(64 * half, 64 * half + 64)
                        out = banks[0:NC, half, q4 * P:(q4 + 1) * P]
                        pe.matmul(out, U[:, 2 * q + half, :], MI[:, 2 * q + half, :], start=True, stop=False)
                        for a in range(2):
                            ins = pe.matmul(out, Z[rows, :, a, q], BC[rows, a, q, :], start=False, stop=(a == 1))
                ins.then_inc(yc_done, 1)

            def outputs_by_channel(k):
                pe.wait_ge(yc_sb, k + 1)
                if k >= 1:
                    pe.wait_ge(yb_sb, k)
                for t in range(T):
                    ins = transpose(bank45[:, t // 4, (t % 4) * NC:(t % 4 + 1) * NC], yblk[0:NC, k % 2, t, :])
                ins.then_inc(yb_done, 1)

            chunk_outputs(0)
            pe.wait_ge(f_ready, 1)
            pe.wait_ge(h0_sb, 1)
            for a in range(2):
                for t in range(2):
                    transpose(bank7[:, (2 * a + t) * P:(2 * a + t + 1) * P],
                              XG[:, a, 1 + 4 * t:5 + 4 * t, :].rearrange("p c q -> p (c q)"))
                ins = transpose(bank6[0:GP, a * P:(a + 1) * P], XG[:, a, 0, :])
            ins.then_inc(f_done, 1)
            for k in range(KT):
                if k + 1 < KT:
                    chunk_outputs(k + 1)
                outputs_by_channel(k)

            pe.wait_ge(h_hi, R_GLU + 8)
            pe.wait_ge(h_lo, R_GLU + 8)
            with pe.Fori(0, 4) as it:
                for s in range(4):
                    pe.wait_ge(tile_free, it * 4 + (T_GLU + s - 1))
                    block_mm(it * 4 + (B_GLU + s), pair[(T_GLU + s) % 2], from_h, True, True, (B_GLU + s) % CUT)
            sum_squares(5, Q_FIN)
            mlp(1)
            sum_squares(6, Q_END)
            for j in range(BLK + 1):
                pe.wait_ge(tile_free, T_OUT + j - 1)
                rows = P if j < BLK else NS
                for k in range(KT):
                    if j == 0:
                        pe.wait_ge(h_ready, H_FIN + k + 1)
                    ins = transpose(pair[j % 2][0:rows, k // 4, (k % 4) * P:(k % 4 + 1) * P],
                                    hT[:, k, j * P:j * P + rows])
                ins.then_inc(tile_done, 1)


        @block.scalar
        def _(act):
            for s in (yt_sb, kd_sb):
                act.sem_inc(s, AHEAD)
            for s in (o_sb, p_exp, sc_sb, dt_sb):
                act.sem_inc(s, CREDIT)
            def copy(out, in_, scale=1.0):
                return act.activation(out, in_, ACT.Copy, scale=scale)

            def square(n, src):
                act.wait_ge(sq_used, n - 1)
                return act.activation(sq[:, square_place[0], :], src, ACT.Square)

            square_place = [0]

            def root(n):
                act.wait_ge(var_ready, n + 1)
                act.activation(rstd[:, :], rstd[:, :], ACT.Sqrt).then_inc(rstd_ready, 1)

            act.wait_ge(a_in, 16 * 3)
            act.activation(nat[0:GP, 2, 2:4], nat[0:GP, 2, 0:2], ACT.Exp).then_inc(aprep, 1)
            act.wait_ge(dprep, 1)
            act.activation(nat[0:GP, 25, :], nat[0:GP, 23, :], ACT.Exp)
            act.activation(nat[0:GP, 26, :], nat[0:GP, 24, :], ACT.Sin)
            act.activation(nat[0:GP, 27, :], nat[0:GP, 24, :], ACT.Sin, scale=0.5).then_inc(aprep, 1)
            act.wait_ge(vec_done, 1)
            copy(vecs[:, :], bank6[:, 0:VROWS]).then_inc(vec_sb, 1)
            for k in range(KT):
                act.wait_ge(tile_done, k + 1)
                copy(xT[:, k, 0:SEQ], pair[k % 2][:, 0, :])
                copy(xT[:, k, SEQ:N], pair[k % 2][:, 1, 0:NS]).then_inc(tile_free, 1)
                act.wait_ge(tile_free, k + 1)
                if k >= 2:
                    act.wait_ge(sq_used, k - 1)
                act.activation(sq[:, k % 2, :], xT[:, k, :], ACT.Square).then_inc(sq_ready, 1)

            act.wait_ge(pw_done, 1)
            copy(PW[:, 0:16, :].rearrange("p a q -> p (a q)"), bank01[:, 0, :])
            copy(PW[:, 16:20, :].rearrange("p a q -> p (a q)"), bank01[:, 1, 0:4 * GP]).then_inc(pw_sb, 1)
            act.wait_ge(c_done, 1)
            for a in range(2):
                for half in range(2):
                    ins = copy(Cp[64 * half:64 * half + 64, a, :, :].rearrange("p (b q) o -> p b q o", b=2),
                               [bank23, bank45][a][0:ST, :, :].rearrange("p b (q h o) -> p h b q o", h=2, o=GS)[:, half])
            ins.then_inc(c_sb, 1)
            with act.Fori(0, GP // QC // 2) as i:
                for par in range(2):
                    c = i * 2 + par
                    kdc = kdcs[par]
                    act.wait_ge(yt_done, c + 1)
                    act.wait_ge(prep_left, c + (AHEAD - 1))
                    copy(bstcs[par].rearrange("p a q n -> p a (q n)"), y_banks[par][:, :, :]).then_inc(yt_sb, 1)
                    act.wait_ge(kd_done, c + (1 + AHEAD))
                    for half in range(2):
                        ins = copy(kdc[0:GS, :, half, :],
                                   kd_banks[par][half][0:GS, :].rearrange("p (q n) -> p q n", q=QC))
                    ins.then_inc(kd_sb, 1)

            def cut_block(n, raw=None, place=None):
                raw = n % RAW if raw is None else raw
                place = n % CUT if place is None else place
                q = n // RAW if isinstance(n, int) else None
                act.wait_ge(w_loaded[raw], loads(n, raw))
                if not (isinstance(n, int) and n < CUT):
                    act.wait_ge(blk_done, n - CUT + 1)
                act.activation(wR[:, place, HI, :, :], wraw[:, raw, :, :], ACT.Copy).then_inc(w_hi, 1)

            def cut_tokens(n0, ready, r0):
                for k in range(KT):
                    act.wait_ge(ready, r0 + k + 1 if r0 is not None else 1)
                    act.activation(hR[:, k, HI, :], hT[:, k, :], ACT.Copy).then_inc(h_hi, 1)

            root(0)
            act.wait_ge(prep_left, GP // QC + AHEAD)
            cut_tokens(R_A, h_ready, H_MIX0)
            cut_block(0)
            for m in range(6):
                n = Q_CQ + m
                cut_block(m + 1)
                act.wait_ge(blk_done, B_A + m + 1)
                act.wait_ge(sq_used, n - 1)
                src = pair[(T_A + m) % 2][:, :, 0:HALF]
                act.activation(halves(sq[:, n % 2, :]), src, ACT.Square).then_inc(sq_ready, 1)
                copy(halves(cqT[:, m, :] if m < 4 else ckvT[:, m - 4, :]), src).then_inc(tile_free, 1)
            root(1)
            root(2)
            for j in range(BLK):
                act.wait_ge(nat_done, j + 1)
                copy(ckvNat[:, j // 2, j % 2, :], pair[j % 2][:, 0, 0:KV_D])
                copy(kpeNat[:, j, :], pair[j % 2][:, 0, KV_D:KV_D + ROPE]).then_inc(nat_sb, 1)
            act.wait_ge(nat_done, 5)
            copy(kpeNat[0:NS, BLK, :], pair[0][0:NS, 0, 0:ROPE]).then_inc(nat_sb, 1)
            for j, src in enumerate((bank45[:, 0, :], bank45[:, 1, :], bank6[:, :], bank7[:, :])):
                act.wait_ge(nat_done, 6 + j)
                copy(CN[0:DEC_Q, 2 * j:2 * j + 2, :].rearrange("p b n -> p (b n)"), src[0:DEC_Q]).then_inc(nat_sb, 1)

            def unit_exp(U_, blk):
                n = (blk + 1) * P
                act.wait_ge(nm_ready, U_ + 1)
                act.wait_ge(t_done, (U_ if blk == 0 else U_ - 1) + CREDIT)
                act.activation(prob[:, blk % 2, 0:n], bank01[:, blk % 2, 0:n], ACT.Exp,
                               bias=stat[:, blk % 2:blk % 2 + 1],
                               accum_out=stat[:, 2 + blk % 2:3 + blk % 2]).then_inc(p_exp, 1)

            def unit_turned(U_, blk):
                n = (blk + 1) * P
                act.wait_ge(t_done, U_ + 1 + CREDIT)
                act.wait_ge(pv_done, (U_ if blk == 0 else U_ - 1) + CREDIT)
                copy(probT[:, blk % 2, 0:blk + 1, :].rearrange("p t n -> p (t n)"), bank23[:, blk % 2, 0:n])\
                    .then_inc(pt_sb, 1)

            def head_out(p, h):
                act.wait_ge(pv_done, p * 8 + (4 * h + 4) + CREDIT)
                copy(hT[64 * h:64 * h + 64, ds(p, 1), 0:SEQ].rearrange("p o n -> p (o n)"),
                     bank45[64 * h:64 * h + 64, 0, :]).then_inc(o_sb, 1)

            with act.Fori(0, PAIRS) as p:
                for h in range(2):
                    act.wait_ge(q_done, p * 2 + (h + 1))
                    copy(halves(qT[0:NOPE, h, :]), pair[h][0:NOPE, :, 0:HALF], SCALE).then_inc(qn_sb, 1)
                act.wait_ge(k_done, p + 1)
                copy(kT[0:NOPE, 0, :], bank45[0:NOPE, 0, :]).then_inc(k_sb, 1)
                copy(kT[0:NOPE, 1, :], bank45[NOPE:P, 0, :]).then_inc(k_sb, 1)
                act.wait_ge(uk_done, p + 1 + CREDIT)
                copy(ukT[0:NOPE, :, :].rearrange("p a n -> p (a n)"), bank6[0:NOPE, :]).then_inc(uk_sb, 1)
                unit_exp(p * 8, 0)
                for u in range(8):
                    if u + 1 < 8:
                        unit_exp(p * 8 + (u + 1), (u + 1) % 4)
                    unit_turned(p * 8 + u, u % 4)
                    if u == 5:
                        head_out(p, 0)
                head_out(p, 1)

            def pages_turned(b, par, g):
                act.wait_ge(ct_done, b * 8 + (g + 1))
                act.wait_ge(sc_done, b * 9 + max(g - 1, 0) + CREDIT)
                copy(cT[:, g % 2, :, :].rearrange("p r n -> p (r n)"), bank01[:, g % 2, :]).then_inc(ct_sb, 1)

            def scores(b, par):
                for g in range(9):
                    if g == 0:
                        pages_turned(b, par, 0)
                        act.wait_ge(dt_done, b * 5 - 5 + CREDIT if not isinstance(b, int) else
                                    max(b - 1, 0) * 5 + CREDIT)
                    if g + 1 < 8:
                        pages_turned(b, par, g + 1)
                    n = DEC_Q if g == 8 else 256
                    act.wait_ge(sc_done, b * 9 + (g + 1) + CREDIT)
                    copy(S[:, par, g * 256:g * 256 + n], bank45[:, g % 2, 0:n]).then_inc(sc_sb, 1)

            def softmax(b, par):
                act.wait_ge(dm_ready, b + 1)
                act.activation(S[:, par, :], S[:, par, :], ACT.Exp, bias=stat[:, 24 + par:25 + par],
                               accum_out=stat[:, 26 + par:27 + par]).then_inc(d_exp, 1)

            def values(b, par):
                act.wait_ge(ov_done, b + CREDIT)
                for j in range(5):
                    act.wait_ge(dt_done, b * 5 + (j + 1) + CREDIT)
                    bank = [bank6, bank7][j % 2]
                    if j < 4:
                        copy(PT[:, 4 * j:4 * j + 4, :].rearrange("p g n -> p (g n)"), bank[:, :]).then_inc(dt_sb, 1)
                    else:
                        copy(PTN[0:DEC_Q, :], bank[0:DEC_Q, 0:P]).then_inc(dt_sb, 1)

            scores(0, 0)
            softmax(0, 0)
            with act.Fori(0, DEC_B // 2 - 1) as i:
                scores(i * 2 + 1, 1)
                values(i * 2, 0)
                softmax(i * 2 + 1, 1)
                scores(i * 2 + 2, 0)
                values(i * 2 + 1, 1)
                softmax(i * 2 + 2, 0)
            scores(DEC_B - 1, 1)
            values(DEC_B - 2, 0)
            softmax(DEC_B - 1, 1)
            values(DEC_B - 1, 1)
            act.wait_ge(os_done, 1)
            copy(hT[:, :, SEQ:N], bank01[:, 0, :].rearrange("p (k n) -> p k n", k=KT)).then_inc(os_sb, 1)

            def mlp(i):
                for half in range(2):
                    n0, t0, z0 = B_MLP[i] + 32 * half, T_MLP[i] + 24 * half, 32 * i + 16 * half
                    act.wait_ge(tile_free, t0)
                    with act.Fori(0, 4) as it:
                        for s in range(4):
                            n = it * 4 + (n0 + s)
                            cut_block(n + 1, (n0 + s + 1) % RAW, (n0 + s + 1) % CUT)
                            act.wait_ge(blk_done, n + 1)
                            act.wait_ge(z_ready, it * 4 + max(z0 + s - 1, 0) + CREDIT)
                            act.activation(halves(tmpa[:, s % 2, :]), pair[(t0 + s) % 2][:, :, 0:HALF], ACT.Relu)\
                                .then_inc(tile_free, 1)
                            act.wait_ge(z_ready, it * 4 + (z0 + s + 1 + CREDIT))
                            act.activation(part_of(zR, it * 4 + s, HI), hid[:, s % 2, :], ACT.Copy).then_inc(z_hi, 1)
                    n0, t0 = n0 + 16, t0 + 16
                    q0 = (Q_MIX1, Q_FIN)[i]

                    def down(it):
                        for j in range(2):
                            for c in range(2):
                                n = it * 4 + (n0 + 2 * j + c)
                                if isinstance(n, int) and n + 1 == B_END:
                                    continue
                                cut_block(n + 1, (n0 + 2 * j + c + 1) % RAW, (n0 + 2 * j + c + 1) % CUT)
                            if half == 1:
                                act.wait_ge(tile_free, it * 2 + (t0 + j + 1))
                                act.wait_ge(sq_used, it * 2 + (q0 + j - 1))
                                act.activation(sq[:, j, :], row(xT, it * 2 + j), ACT.Square).then_inc(sq_ready, 1)

                    final = (i, half) == (1, 1)
                    with act.Fori(0, 4 - final) as it:
                        down(it)
                    if final:
                        down(3)

            cut_tokens(R_B, os_sb, None)
            cut_block(B_B)
            for m in range(KT):
                cut_block(B_B + m + 1)
                act.wait_ge(tile_free, T_B + m + 1)
                act.wait_ge(sq_used, Q_MLP0 + m - 1)
                act.activation(sq[:, m % 2, :], xT[:, m, :], ACT.Square).then_inc(sq_ready, 1)
            root(3)
            cut_tokens(R_MLP[0], h_ready, H_MLP0)
            mlp(0)
            root(4)

            for j in range(11):
                n = min(3, GP - 3 * j)
                act.wait_ge(xs_done, j + 1)
                src = bank01[:, j % 2, 0:n * 2 * NC].rearrange("p (q a c) -> p q a c", q=n, a=2)
                copy(Z[:, 1:PC, :, 3 * j:3 * j + n].rearrange("p c a q -> p q a c"), src[:, :, :, 0:PC - 1])
                copy(XF[:, :, :, 3 * j:3 * j + n].rearrange("p c a q -> p q a c"), src[:, :, :, PC - 1:NC])\
                    .then_inc(xs_sb, 1)

            def chunk_outputs(k):
                act.wait_ge(yc_done, k + 1)
                if k >= 2:
                    act.wait_ge(yb_done, k - 1)
                for half in range(2):
                    ins = copy(yblk[0:NC, k % 2, :, :].rearrange("p t (q a o) -> p a q t o", a=2, o=GS)[:, half],
                               pair[k % 2][0:NC, half, :].rearrange("p (q t o) -> p q t o", q=4, o=GS))
                ins.then_inc(yc_sb, 1)

            chunk_outputs(0)
            act.wait_ge(f_done, 1)
            copy(tmpa[:, 1, 0:512], bank7[:, :]).then_inc(f_sb, 1)
            copy(sq[0:GP, 0, 0:2 * P], bank6[0:GP, 0:2 * P]).then_inc(f_sb, 1)
            for k in range(KT):
                if k + 1 < KT:
                    chunk_outputs(k + 1)
                act.wait_ge(yb_sb, k + 1)
                act.activation(hT[:, k, :], hT[:, k, :], ACT.Gelu_apprx_tanh).then_inc(g_sb, 1)
            act.wait_ge(yc_done, KT)
            cut_tokens(R_GLU, g_sb, 0)
            act.wait_ge(out_sem, 16 * 9)
            for m in range(KT):
                cut_block(B_GLU + 2 * m + 1)
                cut_block(B_GLU + 2 * m + 2)
                act.wait_ge(blk_done, B_GLU + 2 * m + 2)
                if m >= 2:
                    act.wait_ge(x_new, m - 1)
                act.activation(halves(tmpa[:, m % 2, :]), pair[(T_GLU + 1) % 2][:, :, 0:HALF], ACT.Sigmoid)\
                    .then_inc(sig_ready, 1)
                act.wait_ge(x_new, m + 1)
                act.wait_ge(sq_used, Q_MLP1 + m - 1)
                act.activation(sq[:, m % 2, :], xT[:, m, :], ACT.Square).then_inc(sq_ready, 1)
            root(5)
            cut_tokens(R_MLP[1], h_ready, H_MLP1)
            mlp(1)
            root(6)
            for j in range(BLK + 1):
                rows = P if j < BLK else NS
                act.wait_ge(tile_done, 8 + j + 1)
                if j >= 2:
                    act.wait_ge(y_out[j % 2], 16 * (j // 2))
                copy(arena[0:rows, (j % 2) * D:(j % 2 + 1) * D].rearrange("p (a n) -> p a n", a=2), pair[j % 2][0:rows, :, :])\
                    .then_inc(tile_free, 1)

        @block.vector
        def _(dve):
            for s in (ql_sb, olt_sb, ca_ready, z_ready):
                dve.sem_inc(s, CREDIT)
            step = Tally(dstep)

            def own(ins):
                step.add()
                return ins.then_inc(dstep, 1)

            def settle():
                dve.wait_ge(dstep, step.now())

            tt = dve.tensor_tensor

            def clear_acc():
                own(dve.memset(acc[:, :], 0.0))
                settle()

            def add_square(n, place):
                dve.wait_ge(sq_ready, n + 1)
                dve.wait_ge(sq_used, n)
                tt(acc[:, :], acc[:, :], sq[:, place, :], ALU.add).then_inc(sq_used, 1)

            def norm(n, width, tiles, src, dst, v, by_token=False):
                dve.wait_ge(ss_done, n + 1)
                own(dve.tensor_scalar(halves(rstd[:, :]), bank45[:, :, 0:HALF], 1.0 / width, EPS, ALU.mult, ALU.add))
                settle()
                dve.reciprocal(rstd[:, :], rstd[:, :]).then_inc(var_ready, 1)
                dve.wait_ge(rstd_ready, n + 1)
                for k in range(tiles):
                    out, x, r = dst[:, k, :], src[:, k, :], rstd[:, :]
                    if by_token:
                        out = out.rearrange("p (s c) -> p s c", s=T)
                        x = x.rearrange("p (c s) -> p s c", s=T)
                        r = r.rearrange("p (c s) -> p s c", s=T)
                    dve.scalar_tensor_tensor(out=out, in0=x, scalar=vecs[:, v + k:v + k + 1], in1=r,
                                             op0=ALU.mult, op1=ALU.mult).then_inc(h_ready, 1)

            def cut_rest(n, raw=None, place=None):
                raw = n % RAW if raw is None else raw
                place = n % CUT if place is None else place
                dve.wait_ge(w_hi, n + 1)
                tt(wR[:, place, LO, :, :], wraw[:, raw, :, :], wR[:, place, HI, :, :].bitcast(F32), ALU.subtract)\
                    .then_inc(w_lo, 1)

            nt = lambda a: nat[0:GP, a, :]
            ar, ai, dtr, th, er, sn, sh, t1, t2 = (nt(0), nt(1), nt(23), nt(24), nt(25), nt(26), nt(27), nt(28), nt(29))
            pr, pi = (lambda k: nt(3 + k)), (lambda k: nt(12 + k))
            dve.wait_ge(aprep, 1)
            dt_ = nat[0:GP, 2, 2:4].unsqueeze(2).to_broadcast([GP, 2, ST])
            two = lambda a: a.rearrange("p (a n) -> p a n", a=2)
            own(tt(two(dtr), two(ar), dt_, ALU.mult))
            own(tt(two(th), two(ai), dt_, ALU.mult))
            settle()
            magic = 1.5 * 2.0 ** 23
            own(dve.tensor_scalar(t1, th, 1.0 / (2 * math.pi), magic, ALU.mult, ALU.add))
            settle()
            own(dve.tensor_scalar(t1, t1, -magic, None, ALU.add))
            settle()
            c1, c2 = 6.28125, 2029.0 / 2 ** 20
            for part in (c1, c2, 2 * math.pi - c1 - c2):
                own(dve.scalar_tensor_tensor(out=th, in0=t1, scalar=-part, in1=th, op0=ALU.mult, op1=ALU.add))
                settle()
            lim = 3.1415925
            dve.tensor_scalar(th, th, lim, -lim, ALU.min, ALU.max).then_inc(dprep, 1)
            own(dve.memset(pr(0), 1.0))
            own(dve.memset(pi(0), 0.0))
            dve.wait_ge(aprep, 2)
            own(tt(t1, sh, sh, ALU.mult))
            own(tt(pi(1), er, sn, ALU.mult))
            settle()
            own(dve.tensor_scalar(t1, t1, -2.0, 1.0, ALU.mult, ALU.add))
            settle()
            own(tt(pr(1), er, t1, ALU.mult))
            settle()
            fr, fi = nt(21), nt(22)
            own(tt(t1, ar, ar, ALU.mult))
            own(tt(t2, ai, ai, ALU.mult))
            own(dve.tensor_scalar(er, pr(1), -1.0, None, ALU.add))
            settle()
            own(tt(t1, t1, t2, ALU.add))
            own(tt(sn, er, ar, ALU.mult))
            own(tt(sh, pi(1), ai, ALU.mult))
            settle()
            own(dve.reciprocal(t1, t1))
            own(tt(sn, sn, sh, ALU.add))
            settle()
            own(tt(fr, sn, t1, ALU.mult))
            own(tt(t2, pi(1), ar, ALU.mult))
            own(tt(th, er, ai, ALU.mult))
            settle()
            own(tt(t2, t2, th, ALU.subtract))
            settle()
            own(tt(fi, t2, t1, ALU.mult))
            settle()
            clear_acc()
            for k in range(KT):
                add_square(k, k % 2)
            for k in range(2, 9):
                own(tt(t1, pr(k - 1), pr(1), ALU.mult))
                own(tt(t2, pi(k - 1), pi(1), ALU.mult))
                own(tt(er, pr(k - 1), pi(1), ALU.mult))
                own(tt(sn, pi(k - 1), pr(1), ALU.mult))
                settle()
                own(tt(pr(k), t1, t2, ALU.subtract))
                last = own(tt(pi(k), er, sn, ALU.add))
                settle()
            dve.tensor_copy(t1, pi(8)).then_inc(y_ready, 1)
            dve.wait_ge(pw_sb, 1)
            own(dve.tensor_copy(a8[:, 0, :], PW[:, 8, :]))
            own(dve.tensor_copy(a8[:, 1, :], PW[:, 8, :]))
            own(dve.tensor_copy(a8[:, 2, :], PW[:, 17, :]))
            dve.wait_ge(c_sb, 1)

            def complex_product(out_re, out_im, xr, xi, yr, yi, shape, neg):
                n = 1
                for d in shape:
                    n *= d
                names = dict(zip("abc", shape[1:]))
                tv = lambda j: tm[:, j, 0:n].rearrange("p (z a b) -> p z a b", a=shape[1], b=shape[2]) \
                    if len(shape) == 3 else tm[:, j, 0:n].rearrange("p (z a) -> p z a", a=shape[1])
                own(tt(tv(0), xr, yr, ALU.mult))
                own(tt(tv(1), xi, yi, ALU.mult))
                own(tt(tv(2), xr, yi, ALU.mult))
                own(tt(tv(3), xi, yr, ALU.mult))
                settle()
                own(tt(out_re, tm[:, 0, 0:n], tm[:, 1, 0:n], ALU.subtract))
                if neg:
                    return dve.scalar_tensor_tensor(out=out_im, in0=tm[:, 2, 0:n], scalar=-1.0, in1=tm[:, 3, 0:n],
                                                    op0=ALU.mult, op1=ALU.subtract)
                return tt(out_im, tm[:, 2, 0:n], tm[:, 3, 0:n], ALU.add)

            flat = lambda a: a.rearrange("p q k o -> p (q k o)")
            with dve.Fori(0, GP // QC // 2) as i:
                step.enter(i, 34)
                for par in range(2):
                    c = i * 2 + par
                    bb, Y, CA = bbs[par], Ys[par], CAs[par]
                    chunk = lambda t, a: t[:, a, ds(c * QC, QC), :]
                    pw = lambda a, k, n: PW[:, 9 * a:9 * a + k, ds(c * QC, QC)].rearrange("p k q -> p q k")\
                        .unsqueeze(3).to_broadcast([P, QC, k, n])
                    f = lambda a: PW[:, 18 + a, ds(c * QC, QC)].unsqueeze(2).to_broadcast([P, QC, GS])
                    dve.wait_ge(kd_done, c + (AHEAD - 1))
                    dve.wait_ge(ca_ready, c + CREDIT)
                    dve.wait_ge(prep_left, c + (AHEAD - 1))
                    own(complex_product(bb[:, 0].rearrange("p q i -> p (q i)"), bb[:, 1].rearrange("p q i -> p (q i)"),
                                        f(0), f(1), chunk(Bn, 0), chunk(Bn, 1), (QC, GS), False))
                    settle()
                    b_ = lambda a: bb[:, a].unsqueeze(2).to_broadcast([P, QC, T, GS])
                    own(complex_product(Y[:, 0].rearrange("p q n -> p (q n)"), Y[:, 1].rearrange("p q n -> p (q n)"),
                                        pw(0, T, GS), pw(1, T, GS), b_(0), b_(1), (QC, T, GS), False))
                    settle()
                    c_ = lambda a: chunk(Cp, a).unsqueeze(2).to_broadcast([P, QC, 9, GS])
                    dve.tensor_scalar(bb[:, 1].rearrange("p q i -> p (q i)"), bb[:, 1].rearrange("p q i -> p (q i)"),
                                      1.0, None, ALU.mult).then_inc(y_ready, 1)
                    complex_product(flat(CA[:, 0]), flat(CA[:, 1]), pw(0, 9, GS), pw(1, 9, GS), c_(0), c_(1),
                                    (QC, 9, GS), True).then_inc(ca_ready, 1)
                step.leave(GP // QC // 2)

            norm(0, D, KT, xT, hT, V_MIX)
            own(dve.memset(acc[:, :], 0.0))
            settle()
            cut_rest(0)
            for m in range(4):
                cut_rest(m + 1)
                add_square(Q_CQ + m, m % 2)
            dve.wait_ge(ss_done, 2)
            own(dve.memset(acc[:, :], 0.0))
            settle()
            for m in range(2):
                cut_rest(5 + m)
                add_square(Q_CKV + m, m % 2)
            norm(1, QL_D, 4, cqT, cqT, V_Q)
            dve.wait_ge(blk_done, B_B)
            bank = pair[(T_A + 6) % 2]
            own(tt(halves(tmpa[64:96, 0, :]), bank[64:96, :, 0:HALF], halves(ropek[64:96, :]), ALU.mult))
            tt(halves(tmpa[64:96, 1, :]), bank[96:128, :, 0:HALF], halves(ropek[96:128, :]), ALU.mult)\
                .then_inc(tile_free, 1)
            settle()
            dve.wait_ge(tile_free, T_B)
            own(tt(kpR[64:96, :], tmpa[64:96, 0, :], tmpa[64:96, 1, :], ALU.add))
            settle()
            for h in range(2):
                own(dve.tensor_copy(kT[64:96, h, :], kpR[64:96, 0:SEQ]))
            dve.tensor_copy(kpeN[0:ROPE, :], kpR[64:96, SEQ:N]).then_inc(kpe_raw, 1)
            norm(2, KV_D, 2, ckvT, ckvT, V_KV)

            dve.wait_ge(out_sem, 16 * 5)

            def unit_max(U_, blk):
                n = (blk + 1) * P
                dve.wait_ge(s_done, U_ + 1)
                dve.wait_ge(p_exp, (U_ if blk == 0 else U_ - 1) + CREDIT)
                dve.tensor_reduce(stat[:, blk % 2:blk % 2 + 1], bank01[:, blk % 2, 0:n], AX.X, ALU.max, negate=True)\
                    .then_inc(nm_ready, 1)

            def unit_scale(U_, blk):
                n = (blk + 1) * P
                dve.wait_ge(p_exp, U_ + 1 + CREDIT)
                b = blk % 2
                own(dve.reciprocal(stat[:, 4 + b:5 + b], stat[:, 2 + b:3 + b]))
                settle()
                dve.tensor_scalar(prob[:, b, 0:n], prob[:, b, 0:n], stat[:, 4 + b:5 + b], None, ALU.mult)\
                    .then_inc(p_sb, 1)

            with dve.Fori(0, PAIRS) as p:
                step.enter(p, 4 + 8)
                for h in range(2):
                    dve.wait_ge(q_done, p * 2 + (h + 1))
                    own(tt(halves(tmpa[64:96, 0, :]), pair[h][64:96, :, 0:HALF], halves(ropeq[64:96, :]), ALU.mult))
                    own(tt(halves(tmpa[64:96, 1, :]), pair[h][96:128, :, 0:HALF], halves(ropeq[96:128, :]), ALU.mult))
                    settle()
                    tt(qT[64:96, h, :], tmpa[64:96, 0, :], tmpa[64:96, 1, :], ALU.add).then_inc(qr_sb, 1)
                    dve.wait_ge(qr_sb, p * 2 + (h + 1))
                dve.wait_ge(v_done, p + 1)
                dve.tensor_copy(V[:, :, :].rearrange("p t n -> p (t n)"), bank45[:, 1, :]).then_inc(v_sb, 1)
                for h in range(2):
                    dve.tensor_copy(QPE[0:ROPE, :].rearrange("p (t h) -> p t h", h=HEADS)[:, :, ds(p * 2 + h, 1)],
                                    qT[64:96, h, SEQ:N].unsqueeze(2)).then_inc(ql_sb, 1)
                dve.wait_ge(ql_done, p + 1)
                for h in range(2):
                    dve.tensor_copy(QL[:, :, :].rearrange("p r (t h) -> p r t h", h=HEADS)[:, :, :, ds(p * 2 + h, 1)],
                                    bank7[:, 2 * h * NS:(2 * h + 2) * NS].rearrange("p (r t o) -> p r t o", r=2, o=1))\
                        .then_inc(ql_sb, 1)
                unit_max(p * 8, 0)
                for u in range(8):
                    if u + 1 < 8:
                        unit_max(p * 8 + (u + 1), (u + 1) % 4)
                    unit_scale(p * 8 + u, u % 4)
                step.leave(PAIRS)

            def keys_turned(b, par, g):
                dve.wait_ge(ct_done, b * 8 + (g + 1))
                dve.wait_ge(sc_done, b * 9 + max(g - 1, 0) + CREDIT)
                dve.tensor_copy(kpT[0:ROPE, g % 2, :], bank23[0:ROPE, g % 2, 0:256]).then_inc(kp_sb, 1)

            def scores(b, par):
                keys_turned(b, par, 0)
                for g in range(9):
                    if g + 1 < 8:
                        keys_turned(b, par, g + 1)
                    n = DEC_Q if g == 8 else 256
                    dve.wait_ge(sc_sb, b * 9 + (g + 1) + CREDIT)
                    dve.tensor_reduce(stat[:, 6 + 9 * par + g:7 + 9 * par + g], S[:, par, g * 256:g * 256 + n],
                                      AX.X, ALU.max).then_inc(gm_done, 1)
                dve.wait_ge(gm_done, b * 9 + 9)
                dve.tensor_reduce(stat[:, 24 + par:25 + par], stat[:, 6 + 9 * par:15 + 9 * par], AX.X, ALU.max,
                                  negate=True).then_inc(dm_ready, 1)

            def values(b, par):
                dve.wait_ge(d_exp, b + 1)
                dve.reciprocal(stat[:, 28 + par:29 + par], stat[:, 26 + par:27 + par]).then_inc(rl_ready, 1)
                dve.wait_ge(rl_ready, b + 1)
                dve.wait_ge(ov_done, b + 1 + CREDIT)
                dve.wait_ge(olt_done, b + CREDIT)
                dve.tensor_scalar(OLn[:, :], bank23[:, 0, 0:256], stat[:, 28 + par:29 + par], None, ALU.mult)\
                    .then_inc(ol_sb, 1)
                dve.wait_ge(olt_done, b + 1 + CREDIT)
                out = OLT[:, :, b, :] if isinstance(b, int) else OLT[:, :, ds(b, 1), :].rearrange("p r o n -> p r (o n)")
                dve.tensor_copy(out, bank23[:, 1, 0:256].rearrange("p (r n) -> p r n", r=2)).then_inc(olt_sb, 1)

            scores(0, 0)
            with dve.Fori(0, DEC_B // 2 - 1) as i:
                scores(i * 2 + 1, 1)
                values(i * 2, 0)
                scores(i * 2 + 2, 0)
                values(i * 2 + 1, 1)
            scores(DEC_B - 1, 1)
            values(DEC_B - 2, 0)
            values(DEC_B - 1, 1)

            def residual(m, j):
                x = row(xT, m)
                tt(halves(x), halves(x), pair[j][:, :, 0:HALF], ALU.add).then_inc(tile_free, 1)

            def mlp(i):
                for half in range(2):
                    n0, t0, z0 = B_MLP[i] + 32 * half, T_MLP[i] + 24 * half, 32 * i + 16 * half
                    with dve.Fori(0, 4) as it:
                        for s in range(4):
                            n = it * 4 + (n0 + s)
                            cut_rest(n + 1, (n0 + s + 1) % RAW, (n0 + s + 1) % CUT)
                            dve.wait_ge(tile_free, it * 4 + (t0 + s + 1))
                            dve.wait_ge(z_lo, it * 4 + max(z0 + s - 1, 0) + CREDIT)
                            tt(hid[:, s % 2, :], tmpa[:, s % 2, :], tmpa[:, s % 2, :], ALU.mult).then_inc(z_ready, 1)
                    n0, t0 = n0 + 16, t0 + 16
                    q0 = (Q_MIX1, Q_FIN)[i]
                    if half == 1:
                        clear_acc()

                    def down(it):
                        for j in range(2):
                            for c in range(2):
                                n = it * 4 + (n0 + 2 * j + c)
                                if isinstance(n, int) and n + 1 == B_END:
                                    continue
                                cut_rest(n + 1, (n0 + 2 * j + c + 1) % RAW, (n0 + 2 * j + c + 1) % CUT)
                            dve.wait_ge(blk_done, it * 4 + (n0 + 2 * j + 2))
                            residual(it * 2 + j, (t0 + j) % 2)
                            if half == 1:
                                add_square(it * 2 + (q0 + j), j)

                    final = (i, half) == (1, 1)
                    with dve.Fori(0, 4 - final) as it:
                        down(it)
                    if final:
                        down(3)

            clear_acc()
            cut_rest(B_B)
            for m in range(KT):
                cut_rest(B_B + m + 1)
                dve.wait_ge(blk_done, B_B + m + 1)
                residual(m, (T_B + m) % 2)
                add_square(Q_MLP0 + m, m % 2)
            norm(3, D, KT, xT, hT, V_MLP)
            mlp(0)
            norm(4, D, KT, xT, hT, V_MIX + 8, by_token=True)

            for a in range(2):
                own(dve.tensor_copy(E[:, a, 0, :], a8[:, 2 * a, :]))
            settle()
            for n in (1, 2, 4):
                shape = [P, n, GP]
                tv = [yblk[:, 1, j, 0:n * GP].rearrange("p (j q) -> p j q", q=GP) for j in range(4)]
                top = lambda a: E[:, a, n - 1:n, :].to_broadcast(shape)
                low = lambda a: E[:, a, 0:n, :]
                for j, (x, y) in enumerate(((0, 0), (1, 1), (0, 1), (1, 0))):
                    own(tt(tv[j], top(x), low(y), ALU.mult))
                settle()
                own(tt(E[:, 0, n:2 * n, :], tv[0], tv[1], ALU.subtract))
                own(tt(E[:, 1, n:2 * n, :], tv[2], tv[3], ALU.add))
                settle()
            own(dve.memset(Z[:, 0, :, :], 0.0))
            dve.wait_ge(h0_done, 1)
            dve.tensor_copy(Z[:, PC:NC, :, :].rearrange("p b a q -> p a b q"),
                            bank6[:, :].rearrange("p (a b q) -> p a b q", a=2, b=DEC_B)).then_inc(h0_sb, 1)
            dve.wait_ge(xs_sb, 11)
            settle()
            Z1 = Z[:, 1:PC + 1, :, :].rearrange("p (s j) a q -> p s j a q", j=SPAN)
            Z0 = Z[:, 0:PC, :, :].rearrange("p (s j) a q -> p s j a q", j=SPAN)
            temps = yblk[:, 1, :, :].rearrange("p t n -> p (t n)")

            def advance(z, nxt, power, spans):
                n = spans * 2 * GP
                shape = [P, spans, 2, GP]
                tv = lambda j: temps[:, j * 512:j * 512 + n].rearrange("p (s a q) -> p s a q", a=2, q=GP)
                e = lambda a: E[:, a, power - 1, :].unsqueeze(1).unsqueeze(1).to_broadcast(shape)
                own(tt(tv(0), e(0), z, ALU.mult))
                own(tt(tv(1), e(1), z, ALU.mult))
                settle()
                own(tt(tv(0), tv(0), nxt, ALU.add))
                settle()
                own(tt(nxt[:, :, 0, :], tv(0)[:, :, 0, :], tv(1)[:, :, 1, :], ALU.subtract))
                own(tt(nxt[:, :, 1, :], tv(0)[:, :, 1, :], tv(1)[:, :, 0, :], ALU.add))
                settle()

            at = lambda j: Z1[:, :, ds(j, 1), :, :].rearrange("p s o a q -> p s (o a) q")
            with dve.Fori(0, SPAN - 2) as j:
                step.enter(j, 5)
                advance(at(j), at(j + 1), 1, SPANS)
                step.leave(SPAN - 2)
            advance(Z1[:, 0:SPANS - 1, SPAN - 2], Z1[:, 0:SPANS - 1, SPAN - 1], 1, SPANS - 1)
            end = lambda s: Z[:, ds(s * SPAN, 1), :, :]
            with dve.Fori(0, SPANS - 2) as s:
                step.enter(s, 5)
                advance(end(s + 1), end(s + 2), SPAN, 1)
                step.leave(SPANS - 2)
            big = [tmpa.rearrange("p a n -> p (a n)"), sq.rearrange("p a n -> p (a n)"), temps]
            for j0, j1 in ((0, 4), (4, SPAN - 1)):
                shape = [P, SPANS - 1, j1 - j0, GP]
                tv = [t[:, 0:shape[1] * shape[2] * GP].rearrange("p (s j q) -> p s j q", j=j1 - j0, q=GP) for t in big]
                e = lambda a: E[:, a, j0:j1, :].unsqueeze(1).to_broadcast(shape)
                carry = lambda a: Z0[:, 1:SPANS, 0:1, a, :].to_broadcast(shape)
                z = lambda a: Z1[:, 1:SPANS, j0:j1, a, :]
                own(tt(tv[0], e(0), carry(0), ALU.mult))
                own(tt(tv[1], e(1), carry(1), ALU.mult))
                own(tt(tv[2], e(0), carry(1), ALU.mult))
                settle()
                own(tt(z(0), z(0), tv[0], ALU.add))
                own(tt(z(1), z(1), tv[2], ALU.add))
                settle()
                own(tt(z(0), z(0), tv[1], ALU.subtract))
                own(tt(tv[0], e(1), carry(0), ALU.mult))
                settle()
                own(tt(z(1), z(1), tv[0], ALU.add))
                settle()
            dve.tensor_copy(temps[:, 0:GP], a8[:, 0, :]).then_inc(z_state, 1)
            M = DEC_B + 1
            last = Z[:, PC - 1:NC, :, :]
            w = yblk[:, 1, 1:6, :].rearrange("p t n -> p (t n)")[:, 0:2 * M * GP].rearrange("p (a c q) -> p a c q", a=2, q=GP)
            bc = lambda a: a8[:, a, :].unsqueeze(1).to_broadcast([P, M, GP])
            for a in range(2):
                own(tt(XG[:, a], last[:, :, a, :], bc(0), ALU.mult))
                own(tt(w[:, a], last[:, :, 1 - a, :], bc(2), ALU.mult))
            settle()
            for a in range(2):
                own(tt(XG[:, a], XG[:, a], XF[:, :, a, :], ALU.add))
            settle()
            own(tt(XG[:, 0], XG[:, 0], w[:, 0], ALU.subtract))
            own(tt(XG[:, 1], XG[:, 1], w[:, 1], ALU.add))
            settle()
            dve.tensor_copy(rstd[:, 0:1], a8[:, 0, 0:1]).then_inc(f_ready, 1)
            dve.wait_ge(hd_out, 16 * 8)
            for k in range(KT):
                dve.wait_ge(yb_done, k + 1)
                dve.scalar_tensor_tensor(out=halves(hT[:, k, :]), in0=halves(hT[:, k, :]),
                                         scalar=vecs[:, V_D + k:V_D + k + 1], in1=bank45[:, :, 0:HALF],
                                         op0=ALU.mult, op1=ALU.add).then_inc(yb_sb, 1)
            clear_acc()
            for m in range(KT):
                g = tmpa[:, m % 2, :]
                cut_rest(B_GLU + 2 * m + 1)
                cut_rest(B_GLU + 2 * m + 2)
                dve.wait_ge(sig_ready, m + 1)
                tt(halves(g), halves(g), pair[T_GLU % 2][:, :, 0:HALF], ALU.mult).then_inc(tile_free, 2)
                dve.wait_ge(tile_free, T_GLU + 2 * m + 2)
                x = xT[:, m, :].rearrange("p (c s) -> p s c", s=T)
                tt(x, x, g.rearrange("p (s c) -> p s c", s=T), ALU.add).then_inc(x_new, 1)
                add_square(Q_MLP1 + m, m % 2)
            norm(5, D, KT, xT, hT, V_MLP + 8)
            mlp(1)
            norm(6, D, KT, xT, hT, V_FIN)


_INS = ["x_prompt", "x_sample", "cache_ckv", "cache_kpe", "state_ssm_re", "state_ssm_im", "page_table",
        "norm_mix", "norm_mlp", "norm_final", "mla_w_in", "mla_q_norm", "mla_kv_norm", "mla_w_q_up",
        "mla_w_kv_up", "mla_w_o", "ssm_a_re", "ssm_a_im", "ssm_log_dt", "ssm_b_re", "ssm_b_im", "ssm_c_re",
        "ssm_c_im", "ssm_d", "ssm_w_glu", "mlp_w1", "mlp_w2"]
_OUTS = [("y_prompt", (1, SEQ, D)), ("y_sample", (DEC_B, DEC_Q, D)),
         ("prompt_ckv", (1, 1, SEQ, KV_D)), ("prompt_kpe", (1, 1, SEQ, ROPE)),
         ("prompt_ssm_re", (1, 1, GROUPS, ST)), ("prompt_ssm_im", (1, 1, GROUPS, ST)),
         ("sample_ckv", (1, DEC_B, DEC_Q, KV_D)), ("sample_kpe", (1, DEC_B, DEC_Q, ROPE)),
         ("sample_ssm_re", (1, DEC_B, GROUPS, ST)), ("sample_ssm_im", (1, DEC_B, GROUPS, ST))]


def constants():
    import numpy as np
    half = ROPE // 2
    pos = np.concatenate([np.arange(SEQ), PAST + np.tile(np.arange(DEC_Q), DEC_B)]).astype(np.float32)
    inv = np.float32(10000.0) ** (-np.arange(half, dtype=np.float32) / np.float32(half))
    ang = inv[:, None] * pos[None, :]
    cos, sin = np.cos(ang), np.sin(ang)
    rope = np.concatenate([cos, cos, -sin, sin]).astype(np.float32)
    q, k = np.arange(P)[:, None], np.arange(P)[None, :]
    return {
        "c_ident": np.eye(P, dtype=np.float32),
        "c_ropeq": (rope * np.float32(SCALE)).astype(np.float32),
        "c_ropek": rope,
        "c_cmask": np.where(q >= k, 0.0, NEG).astype(np.float32),
        "c_nmask": np.where(q // HEADS >= np.arange(DEC_Q)[None, :], 0.0, NEG).astype(np.float32),
    }


def kernel(**inputs):
    import numpy as np
    import concourse.bacc as bacc
    from concourse.bass_utils import run_bass_kernel_spmd

    nc = bacc.Bacc("TRN2", target_bir_lowering=False, num_devices=1)
    arrays, ins, outs = {}, {}, {}
    for name, a in [(n, inputs[n]) for n in _INS] + list(constants().items()):
        a = np.ascontiguousarray(a)
        arrays[f"in_{name}"] = a
        ins[name] = nc.dram_tensor(f"in_{name}", a.shape, mybir.dt.from_np(a.dtype), kind="ExternalInput").ap()
    for name, shape in _OUTS:
        outs[name] = nc.dram_tensor(f"out_{name}", shape, F32, kind="ExternalOutput").ap()
    build(nc, ins, outs)
    r = run_bass_kernel_spmd(nc, [arrays], core_ids=[0])
    return tuple(r.results[0][f"out_{name}"] for name, _ in _OUTS)
```

```python
from contextlib import ExitStack
import math

import concourse.bass as bass
from concourse import mybir
from concourse.alu_op_type import AluOpType as ALU

F32 = mybir.dt.float32
F32R = mybir.dt.float32r
BF16 = mybir.dt.bfloat16
I32 = mybir.dt.int32
ACT = mybir.ActivationFunctionType
AX = mybir.AxisListType
ds = bass.ds

P = 128
D = 1024
KT = D // P
SEQ, DEC_B, DEC_Q = 512, 8, 8
NS = DEC_B * DEC_Q
N = SEQ + NS
HALF = N // 2
HEADS, NOPE, ROPE, DV = 16, 64, 32, 64
QL_D, KV_D = 512, 256
HD = NOPE + ROPE
SCALE = HD ** -0.5
PAIRS = HEADS // 2
BLK = SEQ // P
PAGES, PAGE = 16, 128
PAST = PAGES * PAGE
FF = 4 * D
EPS = 1e-6
NEG = -1e30

GROUPS, GS, ST = 64, 16, 64
GP = GROUPS // 2
T = 8
NC = N // T
PC = SEQ // T
SPAN = 8
SPANS = PC // SPAN
QC = 4

RAW = 4
CUT = 2
HI, LO = 0, 1
PASSES = ((HI, (HI, LO)), (LO, (HI,)))

V_MIX, V_MLP, V_FIN, V_Q, V_KV, V_D = 0, 16, 32, 40, 44, 46
VROWS = 54


LOW_SPLIT = 4
AHEAD = 2
CREDIT = 1


class Tally:

    def __init__(self, sem):
        self.sem, self.n, self.i, self.stride, self.k = sem, 0, None, 0, 0

    def add(self, k=1):
        if self.i is None:
            self.n += k
        else:
            self.k += k

    def now(self, back=0):
        if self.i is None:
            return self.n - back
        return self.i * self.stride + (self.n + self.k - back)

    def enter(self, i, stride):
        self.i, self.stride, self.k = i, stride, 0

    def leave(self, count):
        assert self.k == self.stride, (self.k, self.stride)
        self.n += count * self.stride
        self.i = None


def build(nc, I, O):
    ctx = ExitStack()
    with ctx:
        def sb(name, shape, dt=F32):
            return ctx.enter_context(nc.sbuf_tensor(name, shape, dt))

        def sem(name):
            return ctx.enter_context(nc.semaphore(name))

        def sb_with_parts(name, shape, parts_shape, parts_dt):
            base = (nc.sbuf_base + 31) // 32 * 32
            whole = sb(name, shape)
            return whole, nc.alloc_sbuf_tensor_at(name + "_parts", parts_shape, parts_dt, offset=base)

        arena, zR = sb_with_parts("arena", [P, 18432], [P, FF // P // 2, 2, N], F32R)
        side, hR = sb_with_parts("side", [P, 2 * KT * N], [P, KT, 2, N], F32R)
        xT = sb("xT", [P, KT, N])
        hT = sb("hT", [P, KT, N])
        wraw = sb("wraw", [P, RAW, 8, P])
        wR = sb("wR", [P, CUT, 2, 8, P], F32R)
        yblk = sb("yblk", [P, 2, T, P])
        ident = sb("ident", [P, P])
        ones = sb("ones", [P, P])
        ropeq = sb("ropeq", [P, N])
        ropek = sb("ropek", [P, N])
        cmask = sb("cmask", [P, P])
        ident16 = sb("ident16", [P, P], BF16)
        cmask16 = sb("cmask16", [P, P], BF16)
        nmask = sb("nmask", [P, DEC_Q])
        vecs = sb("vecs", [P, VROWS])
        sq = sb("sq", [P, 2, N])
        kpR = sb("kpR", [P, N])
        acc = sb("acc", [P, N])
        rstd = sb("rstd", [P, N])
        tmpa = sb("tmpa", [P, 2, N])
        a8 = sb("a8", [P, 3, GP])
        stat = sb("stat", [P, 36])
        ptab = sb("ptab", [1, DEC_B * PAGES], I32)

        offset = [0]

        def view(n):
            offset[0] += n
            assert offset[0] <= 18432, offset[0]
            return arena[:, offset[0] - n:offset[0]]

        in_arena = view
        ckvT = view(2 * N).rearrange("p (r n) -> p r n", r=2)
        QL = view(2 * 1024).rearrange("p (r n) -> p r n", r=2)
        QPE = view(1024)
        OLT = view(2 * 1024).rearrange("p (r b n) -> p r b n", r=2, b=DEC_B)
        CN = view(2048).rearrange("p (b n) -> p b n", b=DEC_B)
        KP = view(2 * PAGES * ROPE).rearrange("p (a g n) -> p a g n", a=2, g=PAGES)
        mark = offset[0]
        cqT = view(4 * N).rearrange("p (r n) -> p r n", r=4)
        qT = view(2 * N).rearrange("p (h n) -> p h n", h=2)
        kT = view(2 * SEQ).rearrange("p (h n) -> p h n", h=2)
        V = view(BLK * P).rearrange("p (t n) -> p t n", t=BLK)
        wq = view(4 * 2 * P).rearrange("p (k h n) -> p k h n", k=4, h=2)
        wkv = view(2 * 2 * P).rearrange("p (r c h n) -> p r c h n", r=2, c=2, h=2)
        ukT = view(4 * P).rearrange("p (a n) -> p a n", a=4)
        probs = [view(SEQ), view(SEQ), side[:, 8192:8192 + SEQ]]
        probT = view(2 * SEQ).rearrange("p (a t n) -> p a t n", a=2, t=BLK)
        offset[0] = mark
        SW = PAST + DEC_Q
        S = view(2 * SW).rearrange("p (a n) -> p a n", a=2)
        PT = view(PAST).rearrange("p (g n) -> p g n", g=PAGES)
        PTN = view(P)
        cT = view(2 * 2 * 256).rearrange("p (a r n) -> p a r n", a=2, r=2)
        kpT = view(2 * 256).rearrange("p (a n) -> p a n", a=2)
        QLb = view(2 * 256).rearrange("p (a r n) -> p a r n", a=2, r=2)
        QPb = view(2 * P).rearrange("p (a n) -> p a n", a=2)
        OLn = view(256)
        pages = side[:, 0:8192].rearrange("p (a g n) -> p a g n", a=2, g=PAGES)
        kpeN = sq[:, 0, 0:NS]
        kpeNat = sq[:, 1, 0:(BLK + 1) * ROPE].rearrange("p (t n) -> p t n", n=ROPE)
        ckvNat = tmpa[:, :, 0:512].rearrange("p a (t n) -> p a t n", t=2)
        wkvf = side[:, 0:PAGES * 256].rearrange("p (r n) -> p r n", r=2)
        hid = sq
        offset[0] = 0
        xnat = view((BLK + 1) * D).rearrange("p (t n) -> p t n", n=D)
        nat = view(30 * P).rearrange("p (a n) -> p a n", a=30)
        PW = view(20 * GP).rearrange("p (a q) -> p a q", a=20)
        Bn = view(2 * GP * GS).rearrange("p (a q i) -> p a q i", a=2, q=GP)
        Cn = view(2 * 8 * ST).rearrange("p (a t n) -> p a t n", a=2, t=8)
        Cp = view(2 * GP * GS).rearrange("p (a q i) -> p a q i", a=2, q=GP)
        def step_views():
            return (view(2 * QC * GS).rearrange("p (a q i) -> p a q i", a=2, q=QC),
                    view(2 * QC * P).rearrange("p (a q n) -> p a q n", a=2, q=QC),
                    view(2 * QC * 9 * GS).rearrange("p (a q k o) -> p a q k o", a=2, q=QC, k=9))

        even = step_views()
        tm = view(4 * QC * 9 * GS).rearrange("p (a n) -> p a n", a=4)
        tp = view(2 * QC * 9 * GS).rearrange("p (a n) -> p a n", a=2)
        nCi = arena[:, 0:GP * GS].rearrange("p (q i) -> p q i", q=GP)
        offset[0] = 0
        view = lambda n: (offset.__setitem__(0, offset[0] + n), side[:, offset[0] - n:offset[0]])[1]
        odd = step_views()
        bbs, Ys, CAs = ([even[j], odd[j]] for j in range(3))
        bstcs = [view(2 * QC * P).rearrange("p (a q n) -> p a q n", a=2, q=QC) for _ in range(2)]
        kdcs = [view(2 * QC * P).rearrange("p (q a n) -> p q a n", a=2, q=QC) for _ in range(2)]
        vrow = view(P)
        offset[0] = 0
        view = in_arena
        U = view(GROUPS * NC).rearrange("p (g c) -> p g c", g=GROUPS)
        Z = view(NC * 2 * GP).rearrange("p (c a q) -> p c a q", a=2, q=GP)
        XF = view((DEC_B + 1) * 2 * GP).rearrange("p (c a q) -> p c a q", a=2, q=GP)
        BC = view(2 * GP * P).rearrange("p (a q n) -> p a q n", a=2, q=GP)
        MI = side[:, 0:8192].rearrange("p (g n) -> p g n", g=GROUPS)
        E = side[:, 8192:8192 + 2 * SPAN * GP].rearrange("p (a j q) -> p a j q", a=2, q=GP)
        h0n = yblk[:, 0, 0:4, :]
        XG = tmpa[:, 0, :].rearrange("p (a c q) -> p a c q", a=2, q=GP)

        bank01 = ctx.enter_context(nc.psum_tensor("bank01", [P, 2, 512], F32))
        bank23 = ctx.enter_context(nc.psum_tensor("bank23", [P, 2, 512], F32))
        bank45 = ctx.enter_context(nc.psum_tensor("bank45", [P, 2, 512], F32))
        bank6 = ctx.enter_context(nc.psum_tensor("bank6", [P, 512], F32))
        bank7 = ctx.enter_context(nc.psum_tensor("bank7", [P, 512], F32))
        pair = [bank01, bank23]
        score_banks = [bank01[:, 0, :], bank01[:, 1, :], bank6[:, :]]
        y_banks = [bank01, bank45]
        kd_banks = [(bank23[:, 0, :], bank23[:, 1, :]), (bank6[:, :], bank7[:, :])]

        BSTD = nc.dram_tensor("s5_in_to_state", (P, 2, GP, P), F32, kind="Internal").ap()
        CSD = nc.dram_tensor("s5_state_to_out", (P, 2, GP, P), F32, kind="Internal").ap()
        KD = nc.dram_tensor("s5_lag_kernels", (GROUPS, GS, P), F32, kind="Internal").ap()
        HDR = nc.dram_tensor("s5_input", (D, T, NC), F32, kind="Internal").ap()

        ones_set = sem("ones_set")
        waited = sem("waited")
        const_in = sem("const_in")
        x_in = sem("x_in")
        a_in = sem("a_in")
        s5_in = sem("s5_in")
        mask_cut = sem("mask_cut")
        vec_done = sem("vec_done")
        vec_sb = sem("vec_sb")
        w_loaded = [sem(f"w_loaded{s}") for s in range(RAW)]
        w_hi = sem("w_hi")
        w_lo = sem("w_lo")
        blk_done = sem("blk_done")
        h_hi, h_lo = sem("h_hi"), sem("h_lo")
        h_lo_v = sem("h_lo_v")
        z_hi, z_lo = sem("z_hi"), sem("z_lo")
        tile_done = sem("tile_done")
        tile_free = sem("tile_free")
        sq_ready = sem("sq_ready")
        sq_used = sem("sq_used")
        ss_done = sem("ss_done")
        var_ready = sem("var_ready")
        rstd_ready = sem("rstd_ready")
        h_ready = sem("h_ready")
        z_ready = sem("z_ready")
        sig_ready = sem("sig_ready")
        x_new = sem("x_new")
        dstep = sem("dstep")
        pstep = sem("pstep")
        dprep = sem("dprep")
        kpe_raw = sem("kpe_raw")
        nat_done, nat_sb = sem("nat_done"), sem("nat_sb")
        hw_in, hw_swap = sem("hw_in"), sem("hw_swap")
        q_done, qn_sb, qr_sb = sem("q_done"), sem("qn_sb"), sem("qr_sb")
        k_done, k_sb, v_done, v_sb = sem("k_done"), sem("k_sb"), sem("v_done"), sem("v_sb")
        uk_done, uk_sb, ql_done, ql_sb = sem("uk_done"), sem("uk_sb"), sem("ql_done"), sem("ql_sb")
        s_done, nm_ready, p_exp, p_sb = sem("s_done"), sem("nm_ready"), sem("p_exp"), sem("p_sb")
        t_done, pt_sb, pv_done, o_sb = sem("t_done"), sem("pt_sb"), sem("pv_done"), sem("o_sb")
        tab_in = sem("tab_in")
        page_in = [[sem(f"page_in{a}{c}") for c in range(4)] for a in range(2)]
        keys_in = [sem(f"keys_in{a}") for a in range(2)]
        quarter_used = sem("quarter_used")
        qb_ready = sem("qb_ready")
        ct_done, ct_sb, kp_sb = sem("ct_done"), sem("ct_sb"), sem("kp_sb")
        sc_done, sc_sb, gm_done, dm_ready, d_exp = (sem("sc_done"), sem("sc_sb"), sem("gm_done"),
                                                    sem("dm_ready"), sem("d_exp"))
        dt_done, dt_sb, ov_done, ol_sb, olt_done, olt_sb = (
            sem("dt_done"), sem("dt_sb"), sem("ov_done"), sem("ol_sb"), sem("olt_done"), sem("olt_sb"))
        rl_ready = sem("rl_ready")
        wkvf_in, os_done, os_sb = sem("wkvf_in"), sem("os_done"), sem("os_sb")
        pw_done, pw_sb, c_done, c_sb = sem("pw_done"), sem("pw_sb"), sem("c_done"), sem("c_sb")
        y_ready, yt_done, yt_sb, kd_done, kd_sb = (sem("y_ready"), sem("yt_done"), sem("yt_sb"),
                                                   sem("kd_done"), sem("kd_sb"))
        ca_im = sem("ca_im")
        ca_ready, prep_out, prep_left = sem("ca_ready"), sem("prep_out"), sem("prep_left")
        hd_out, u_in, mi_zero, mi_in, bst_in, cs_in, h0_in = (
            [sem("hd_out0"), sem("hd_out1")], [sem("u_in0"), sem("u_in1")], sem("mi_zero"), sem("mi_in"), sem("bst_in"), sem("cs_in"),
            sem("h0_in"))
        xs_done, xs_sb, h0_done, z_state = sem("xs_done"), sem("xs_sb"), sem("h0_done"), sem("z_state")
        h0_sb = sem("h0_sb")
        yc_done, yc_sb, yb_done, yb_sb, g_sb = (sem("yc_done"), sem("yc_sb"), sem("yb_done"),
                                                sem("yb_sb"), sem("g_sb"))
        f_ready, f_done, f_sb = sem("f_ready"), sem("f_done"), sem("f_sb")
        out_sem, aprep = sem("out_sem"), sem("aprep")
        y_out = sem("y_out")

        B_A = 0
        B_B = B_A + 7
        B_MLP = [B_B + 8, B_B + 8 + 64 + 16]
        B_GLU = B_MLP[0] + 64
        B_END = B_MLP[1] + 64
        T_X, T_A = 0, 8
        T_B = T_A + 7
        T_MLP = [T_B + 8, T_B + 8 + 48 + 16]
        T_GLU = T_MLP[0] + 48
        T_OUT = T_MLP[1] + 48
        R_A, R_B, R_MLP, R_GLU, R_END = 0, 8, [16, 32], 24, 40
        Q_MIX0, Q_CQ, Q_CKV, Q_MLP0, Q_MIX1, Q_MLP1, Q_FIN, Q_END = 0, 8, 12, 14, 22, 30, 38, 46
        H_MIX0, H_CQ, H_CKV, H_MLP0, H_MIX1, H_MLP1, H_FIN = 0, 8, 12, 14, 22, 30, 38

        def loads(n, raw):
            extra = 32 if raw == 6 % RAW else 0
            if isinstance(n, int):
                return 16 * (n // RAW + 1) + (extra if n >= 6 else 0)
            return n * (16 // RAW) + (16 - (16 // RAW) * raw + extra)

        def halves(t):
            return t.rearrange("p (a n) -> p a n", a=2)

        def row(t, m):
            if isinstance(m, int):
                return t[:, m, :]
            return t[:, ds(m, 1), :].rearrange("p o n -> p (o n)")

        def part_of(t, m, which):
            if isinstance(m, int):
                return t[:, m, which, :]
            return t[:, ds(m, 1), which, :].rearrange("p o n -> p (o n)")

        w_in = I["mla_w_in"][0].rearrange("(k p) n -> p k n", p=P)
        w_qup = I["mla_w_q_up"][0].rearrange("(k p) n -> p k n", p=P)
        w_kvup = I["mla_w_kv_up"][0].rearrange("(r p) n -> p r n", p=P)
        w_o = I["mla_w_o"][0].rearrange("(k p) n -> p k n", p=P)
        w_glu = I["ssm_w_glu"][0].rearrange("(k p) n -> p k n", p=P)
        w_up = [I["mlp_w1"][i].rearrange("(k p) n -> p k n", p=P) for i in range(2)]
        w_down = [I["mlp_w2"][i].rearrange("(k p) n -> p k n", p=P) for i in range(2)]

        def col(w, k0, m):
            return w[:, k0:k0 + 8, m * P:(m + 1) * P] if isinstance(m, int) else w[:, k0:k0 + 8, ds(m * P, P)]

        def apart(eng):
            eng.sem_inc(waited, 1)

        def low_part(n0, k):
            return (h_lo, n0 // 2 + k + 1) if k < LOW_SPLIT else (h_lo_v, n0 // 2 + k - LOW_SPLIT + 1)

        def physical(eng, i, par, g):
            at = i * (2 * PAGES) + (par * PAGES + g)
            return eng.value_load(ptab[0:1, at:at + 1] if isinstance(at, int) else ptab[0:1, ds(at, 1)],
                                  min_val=0, max_val=I["cache_ckv"].shape[1] - 1)

        UNITS = [(h, blk) for h in range(2) for blk in range(BLK)]

        def before(u, ring):
            return max(u - ring + 1, 0)

        block = ctx.enter_context(nc.Block())

        @block.sync
        def _(sp):
            def load_block(n, src, slot=None):
                slot = n % RAW if slot is None else slot
                sp.wait_ge(w_hi, n - RAW + 1)
                sp.wait_ge(w_lo, n - RAW + 1)
                if not isinstance(n, int):
                    apart(sp)
                sp.dma_start(wraw[:, slot, :, :], src).then_inc(w_loaded[slot], 16)

            sp.sem_inc(prep_left, AHEAD)
            flat = lambda a: a[0].rearrange("g p -> (g p)").rearrange("(q n) -> q n", n=P)
            sp.dma_start(nat[0:GP, 0, :], flat(I["ssm_a_re"])).then_inc(a_in, 16)
            sp.dma_start(nat[0:GP, 1, :], flat(I["ssm_a_im"])).then_inc(a_in, 16)
            sp.dma_start(nat[0:GP, 2, 0:2], I["ssm_log_dt"][0].rearrange("(q a) -> q a", a=2)).then_inc(a_in, 16)
            sp.dma_start(ident[:, :], I["c_ident"]).then_inc(const_in, 16)
            sp.dma_start(ropeq[64:128, :], I["c_ropeq"]).then_inc(const_in, 16)
            sp.dma_start(ropek[64:128, :], I["c_ropek"]).then_inc(const_in, 16)
            sp.dma_start(cmask[:, :], I["c_cmask"]).then_inc(const_in, 16)
            sp.dma_start(nmask[:, :], I["c_nmask"]).then_inc(const_in, 16)
            at = 0
            for name, k in (("norm_mix", 16), ("norm_mlp", 16), ("norm_final", 8), ("mla_q_norm", 4),
                            ("mla_kv_norm", 2), ("ssm_d", 8)):
                a = I[name]
                if len(a.shape) == 2:
                    a = a.rearrange("a b -> (a b)")
                sp.dma_start(vrow[at:at + k, :], a.rearrange("(k p) -> k p", p=P)).then_inc(const_in, 16)
                at += k
            sp.dma_start(ptab[:, :], I["page_table"].rearrange("a b -> (a b)").rearrange("(o n) -> o n", o=1))\
                .then_inc(tab_in, 16)
            sp.dma_start(xnat[:, 0:BLK, :], I["x_prompt"][0].rearrange("(t p) n -> p t n", p=P)).then_inc(x_in, 16)
            sp.dma_start(xnat[0:NS, BLK, :], I["x_sample"].rearrange("b q n -> (b q) n")).then_inc(x_in, 16)
            for m in range(4):
                sp.dma_start(wraw[:, m, :, :], col(w_in, 0, m)).then_inc(w_loaded[m], 16)
            for a, part in enumerate(("re", "im")):
                sp.dma_start(Bn[:, a, :, :], I[f"ssm_b_{part}"][0].rearrange("g p i -> (g p) i")
                             .rearrange("(q n) i -> n q i", n=P)).then_inc(s5_in, 16)
                sp.dma_start(Cn[:, a, :, :], I[f"ssm_c_{part}"][0].rearrange("g o p -> (g o) p")
                             .rearrange("(t m) p -> m t p", m=P)).then_inc(s5_in, 16)
            with sp.Fori(0, GP // QC // 2) as i:
                for par in range(2):
                    c = i * 2 + par
                    bstc, kdc, CA = bstcs[par], kdcs[par], CAs[par]
                    sp.wait_ge(yt_sb, c + (1 + AHEAD))
                    apart(sp)
                    sp.dma_start(BSTD[:, :, ds(c * QC, QC), :], bstc[:, :, :, :]).then_inc(prep_out, 16)
                    sp.wait_ge(ca_ready, c + (1 + CREDIT))
                    apart(sp)
                    sp.wait_ge(ca_im, c + (1 + CREDIT))
                    apart(sp)
                    for a in range(2):
                        sp.dma_start(CSD[:, a, ds(c * QC, QC), :],
                                       CA[:, a, :, 1:9, :].rearrange("p q k o -> p q (k o)")).then_inc(prep_out, 16)
                    sp.wait_ge(kd_sb, c + (1 + AHEAD))
                    apart(sp)
                    sp.dma_start(KD.rearrange("g i n -> i g n")[:, ds(c * (2 * QC), 2 * QC), :],
                                   kdc[0:GS].rearrange("p q a n -> p (q a) n")).then_inc(prep_out, 16)
                    sp.wait_ge(prep_out, c * 64 + 64)
                    sp.sem_inc(prep_left, 1)
            for m in (4, 5):
                load_block(m, col(w_in, 0, m))
            sp.wait_ge(w_hi, 3)
            sp.wait_ge(w_lo, 3)
            c0 = QL_D + KV_D
            sp.dma_start(wraw[:, 2, :, 64:96], w_in[:, :, c0:c0 + 32]).then_inc(w_loaded[2], 16)
            sp.dma_start(wraw[:, 2, :, 96:112], w_in[:, :, c0 + 16:c0 + 32]).then_inc(w_loaded[2], 16)
            sp.dma_start(wraw[:, 2, :, 112:128], w_in[:, :, c0:c0 + 16]).then_inc(w_loaded[2], 16)
            sp.wait_ge(prep_left, GP // QC + AHEAD)
            sp.wait_ge(tile_free, T_X + 8)

            def pair_weights(p):
                for h in range(2):
                    sp.dma_start(wq[:, :, h, 0:HD], w_qup[:, :, ds(p * (2 * HD) + h * HD, HD)]).then_inc(hw_in, 16)
                for r in range(2):
                    for c in range(2):
                        sp.dma_start(wkv[:, r, c, :, :],
                                     w_kvup[:, r, ds(p * (2 * P), 2 * P)].rearrange("p (h c n) -> p c h n", h=2, c=2)
                                     [:, c]).then_inc(hw_in, 16)

            with sp.Fori(0, PAIRS) as p:
                sp.wait_ge(uk_done, p + CREDIT)
                pair_weights(p)
            for m in range(RAW):
                load_block(B_B + m, col(w_o, 0, m))
            sp.wait_ge(tab_in, 16)
            sp.wait_ge(blk_done, B_B)


            def load_pages(i, par):
                for c in range(4):
                    if not isinstance(i, int):
                        sp.wait_ge(quarter_used, i * 8 + (4 * par + c - 7))
                        apart(sp)
                    for g in range(4 * c, 4 * c + 4):
                        sp.dma_start(pages[:, par, g, :],
                                     I["cache_ckv"][0][ds(physical(sp, i, par, g), 1)].rearrange("o p n -> (o p) n"))\
                            .then_inc(page_in[par][c], 16)

            for par in range(2):
                load_pages(0, par)
            with sp.Fori(1, DEC_B // 2) as i:
                for par in range(2):
                    load_pages(i, par)
            sp.wait_ge(quarter_used, 4 * (DEC_B - 1))
            sp.dma_start(wkvf[:, :, :], w_kvup).then_inc(wkvf_in, 16)
            for m in range(RAW, 8):
                load_block(B_B + m, col(w_o, 0, m))

            def load_mlp(i):
                for half in range(2):
                    n0 = B_MLP[i] + 32 * half
                    with sp.Fori(0, 4) as it:
                        for s in range(4):
                            load_block(it * 4 + (n0 + s), w_up[i][:, :, ds(it * (4 * P) + (16 * half + s) * P, P)],
                                       (n0 + s) % RAW)
                    n0 += 16
                    with sp.Fori(0, 4) as it:
                        for s in range(4):
                            k0 = 16 * half + 8 * (s % 2)
                            load_block(it * 4 + (n0 + s), w_down[i][:, k0:k0 + 8, ds(it * (2 * P) + (s // 2) * P, P)],
                                       (n0 + s) % RAW)

            load_mlp(0)
            for s in range(4):
                load_block(B_GLU + s, w_glu[:, :, (s // 2) * P + (1 - s % 2) * D:(s // 2 + 1) * P + (1 - s % 2) * D])
            sp.wait_ge(blk_done, B_GLU)
            sp.wait_ge(prep_left, GP // QC + AHEAD)
            sp.dma_start(BC[:, :, :, :], BSTD[:, :, :, :]).then_inc(bst_in, 16)
            for a, part in enumerate(("re", "im")):
                sp.dma_start(h0n[:, 2 * a:2 * a + 2, :],
                             I[f"state_ssm_{part}"][0].rearrange("b g p -> (b g p)")
                             .rearrange("(t m n) -> m t n", m=P, n=P)).then_inc(h0_in, 16)
            for part in range(2):
                sp.wait_ge(hd_out[part], 16 * 4)
                gs = slice(part * GP, (part + 1) * GP)
                rows = slice(part * D // 2, (part + 1) * D // 2)
                for r in range(T):
                    sp.dma_start(U[GS * r:GS * r + GS, gs, :],
                                 HDR[rows, T - 1 - r, :].rearrange("(g i) c -> i g c", i=GS)).then_inc(u_in[part], 16)
            sp.wait_ge(xs_done, 11)
            sp.dma_start(BC[:, :, :, :], CSD[:, :, :, :]).then_inc(cs_in, 16)
            with sp.Fori(1, 4) as it:
                for s in range(4):
                    load_block(it * 4 + (B_GLU + s), w_glu[:, :, ds(it * (2 * P) + (s // 2) * P + (1 - s % 2) * D, P)],
                               (B_GLU + s) % RAW)
            load_mlp(1)

        @block.gpsimd
        def _(pool):
            pool.sem_inc(ca_im, CREDIT)
            pool.sem_inc(z_lo, CREDIT)
            pool.memset(ones[:, :], 1.0).then_inc(ones_set, 1)
            pool.wait_ge(pw_sb, 1)
            pool.wait_ge(c_sb, 1)
            with pool.Fori(0, GP // QC // 2) as i:
                for par in range(2):
                    c = i * 2 + par
                    shape = [P, QC, 9, GS]
                    pw = lambda a: PW[:, 9 * a:9 * a + 9, ds(c * QC, QC)].rearrange("p k q -> p q k")\
                        .unsqueeze(3).to_broadcast(shape)
                    tv = lambda j: tp[:, j, :].rearrange("p (z a b) -> p z a b", a=9, b=GS)
                    pool.wait_ge(kd_done, c + (AHEAD - 1))
                    pool.wait_ge(prep_left, c + (AHEAD - 1))
                    pool.wait_ge(ca_im, c + CREDIT)
                    apart(pool)
                    pool.tensor_tensor(tv(0), pw(0), nCi[:, ds(c * QC, QC), :].unsqueeze(2).to_broadcast(shape),
                                       ALU.mult).then_inc(pstep, 1)
                    pool.tensor_tensor(tv(1), pw(1), Cp[:, 0, ds(c * QC, QC), :].unsqueeze(2).to_broadcast(shape),
                                       ALU.mult).then_inc(pstep, 1)
                    pool.wait_ge(pstep, c * 2 + 2)
                    apart(pool)
                    pool.tensor_tensor(CAs[par][:, 1].rearrange("p q k o -> p (q k o)"), tp[:, 0, :], tp[:, 1, :],
                                       ALU.subtract).then_inc(ca_im, 1)

            def rest_of(n0, mask=None):
                for k in range(LOW_SPLIT):
                    pool.wait_ge(h_hi, n0 + k + 1)
                    pool.tensor_tensor(hR[:, k, LO, :], hT[:, k, :], hR[:, k, HI, :].bitcast(F32), ALU.subtract)\
                        .then_inc(h_lo, 1)

            rest_of(R_A)
            with pool.Fori(0, PAIRS) as p:
                pool.wait_ge(hw_in, p * 96 + 96)
                apart(pool)
                pool.tensor_copy(wq[:, :, :, 96:112], wq[:, :, :, 80:96]).then_inc(hw_swap, 1)
                pool.tensor_copy(wq[:, :, :, 112:128], wq[:, :, :, 64:80]).then_inc(hw_swap, 1)
            def load_keys(i, par):
                for g in range(PAGES):
                    pool.dma_start(KP[:, par, g, :],
                                   I["cache_kpe"][0][ds(physical(pool, i, par, g), 1)].rearrange("o p n -> (o p) n"))\
                        .then_inc(keys_in[par], 16)

            pool.wait_ge(tab_in, 16)
            for par in range(2):
                load_keys(0, par)
            pool.wait_ge(ql_sb, 4 * PAIRS + CREDIT)
            pool.wait_ge(o_sb, 2 * PAIRS + CREDIT)

            def fix_queries(b, par):
                pool.tensor_copy(QLb[:, par, :, :], QL[:, :, b * P:(b + 1) * P] if isinstance(b, int) else
                                 QL[:, :, ds(b * P, P)]).then_inc(qb_ready, 1)
                pool.tensor_copy(QPb[0:ROPE, par, :], QPE[0:ROPE, b * P:(b + 1) * P] if isinstance(b, int) else
                                 QPE[0:ROPE, ds(b * P, P)]).then_inc(qb_ready, 1)

            for par in range(2):
                fix_queries(par, par)
            with pool.Fori(1, DEC_B // 2) as i:
                for par in range(2):
                    pool.wait_ge(sc_done, i * 18 + (9 * par - 9) + CREDIT)
                    apart(pool)
                    fix_queries(i * 2 + par, par)
                    load_keys(i, par)
            pool.wait_ge(nat_sb, 5)
            pool.dma_start(O["sample_kpe"].rearrange("a b q n -> (a b q) n"), kpeNat[0:NS, BLK, :]).then_inc(out_sem, 16)
            pool.dma_start(O["prompt_kpe"][0, 0].rearrange("(t p) n -> p t n", p=P), kpeNat[:, 0:BLK, :])\
                .then_inc(out_sem, 16)
            pool.dma_start(O["prompt_ckv"][0, 0].rearrange("(a t p) n -> p a t n", a=2, p=P)[:, 0],
                           ckvNat[:, 0, :, :]).then_inc(out_sem, 16)
            pool.dma_start(O["prompt_ckv"][0, 0].rearrange("(a t p) n -> p a t n", a=2, p=P)[:, 1],
                           ckvNat[:, 1, :, :]).then_inc(out_sem, 16)
            pool.wait_ge(nat_sb, 9)
            pool.dma_start(O["sample_ckv"][0].rearrange("b q n -> q b n"), CN[0:DEC_Q, :, :]).then_inc(out_sem, 16)
            rest_of(R_B)

            def rest_of_hidden(i):
                for half in range(2):
                    z0 = 32 * i + 16 * half
                    with pool.Fori(0, 8) as it:
                        for s in range(2):
                            pool.wait_ge(z_hi, it * 2 + (z0 + s + 1))
                            apart(pool)
                            m = it * 2 + s
                            pool.tensor_tensor(part_of(zR, m, LO), hid[:, s, :], part_of(zR, m, HI).bitcast(F32),
                                               ALU.subtract).then_inc(z_lo, 1)

            rest_of(R_MLP[0])
            rest_of_hidden(0)
            pool.wait_ge(blk_done, B_MLP[0] + 48)
            pool.memset(MI[:, :, :], 0.0).then_inc(mi_zero, 1)
            pool.wait_ge(mi_zero, 1)
            for r in range(T):
                s = T - 1 - r
                pool.dma_start(MI[GS * r:GS * r + GS, :, GS * s:P],
                               KD.rearrange("g i n -> i g n")[:, :, 0:P - GS * s]).then_inc(mi_in, 16)
            for k in range(KT):
                pool.wait_ge(h_ready, H_MIX1 + k + 1)
                pool.dma_start(HDR[k * P:(k + 1) * P].rearrange("p s c -> p (s c)"), hT[:, k, :]).then_inc(hd_out[k // 4], 16)
            pool.wait_ge(f_sb, 2)
            for a, part in enumerate(("re", "im")):
                pool.dma_start(O[f"sample_ssm_{part}"][0].rearrange("b g p -> (b g p)")
                               .rearrange("(t m n) -> m t n", m=P, n=P),
                               tmpa[:, 1, a * 256:a * 256 + 256].rearrange("p (t n) -> p t n", t=2)).then_inc(out_sem, 16)
                pool.dma_start(O[f"prompt_ssm_{part}"][0, 0].rearrange("g p -> (g p)").rearrange("(q n) -> q n", n=P),
                               sq[0:GP, 0, a * P:a * P + P]).then_inc(out_sem, 16)
            rest_of(R_GLU)
            rest_of(R_MLP[1])
            rest_of_hidden(1)
            for j in range(BLK + 1):
                pool.wait_ge(tile_free, T_OUT + j + 1)
                dst = O["y_prompt"][0, j * P:(j + 1) * P, :] if j < BLK else O["y_sample"].rearrange("b q n -> (b q) n")
                rows = P if j < BLK else NS
                pool.dma_start(dst, arena[0:rows, j * D:(j + 1) * D]).then_inc(y_out, 16)
            pool.wait_ge(out_sem, 16 * (5 + 4))
            pool.wait_ge(y_out, 16 * (BLK + 1))

        @block.tensor
        def _(pe):
            for s in (t_done, pv_done, sc_done, dt_done, ov_done, olt_done, uk_done):
                pe.sem_inc(s, CREDIT)
            pe.sem_inc(kd_done, AHEAD)
            def transpose(out, in_, rows=None):
                k = in_.shape[0]
                b = in_.base_partition()
                return pe.transpose(out, in_, ident[b:b + k, b:b + k])

            pe.wait_ge(const_in, 16 * 11)
            pe.wait_ge(ones_set, 1)
            transpose(bank6[:, 0:VROWS], vrow[0:VROWS, :]).then_inc(vec_done, 1)
            pe.wait_ge(x_in, 32)
            for k in range(KT):
                if k >= 2:
                    pe.wait_ge(tile_free, k - 1)
                for j in range(BLK):
                    transpose(pair[k % 2][:, 0, j * P:(j + 1) * P], xnat[:, j, k * P:(k + 1) * P])
                transpose(pair[k % 2][:, 1, 0:NS], xnat[0:NS, BLK, k * P:(k + 1) * P]).then_inc(tile_done, 1)

            pe.wait_ge(tile_free, 8)
            pe.wait_ge(s5_in, 16 * 4)
            for a in range(2):
                for t in range(8):
                    ins = transpose([bank23, bank45][a][0:ST, t // 4, (t % 4) * P:(t % 4 + 1) * P], Cn[:, a, t, :])
            ins.then_inc(c_done, 1)
            pe.wait_ge(y_ready, 1)
            for a in range(20):
                ins = transpose(pair[0][:, a // 16, (a % 16) * GP:(a % 16) * GP + GP], nat[0:GP, 3 + a, :])
            ins.then_inc(pw_done, 1)
            pe.wait_ge(pw_sb, 1)
            pe.wait_ge(c_sb, 1)
            with pe.Fori(0, GP // QC // 2) as i:
                for par in range(2):
                    c = i * 2 + par
                    bb, Y, CA = bbs[par], Ys[par], CAs[par]
                    pe.wait_ge(y_ready, c + 2)
                    pe.wait_ge(yt_sb, c + (AHEAD - 1))
                    for a in range(2):
                        for q in range(QC):
                            ins = transpose(y_banks[par][:, a, q * P:(q + 1) * P], Y[:, a, q, :])
                    ins.then_inc(yt_done, 1)
                    pe.wait_ge(ca_ready, c + (1 + CREDIT))
                    pe.wait_ge(ca_im, c + (1 + CREDIT))
                    pe.wait_ge(kd_sb, c + (AHEAD - 1))
                    apart(pe)
                    for half in range(2):
                        for q in range(QC):
                            for a in range(2):
                                rows = slice(64 * half, 64 * half + 64)
                                ins = pe.matmul(kd_banks[par][half][0:GS, q * P:(q + 1) * P], bb[rows, a, q, :],
                                                CA[rows, a, q, 0:8, :].rearrange("p k o -> p (k o)"),
                                                start=(a == 0), stop=(a == 1))
                    ins.then_inc(kd_done, 1)
            pe.wait_ge(kd_sb, GP // QC + AHEAD)

            def sum_squares(n, q_end):
                pe.wait_ge(sq_used, q_end)
                for a in range(2):
                    ins = pe.matmul(bank45[:, a, 0:HALF], ones[:, :], acc[:, a * HALF:(a + 1) * HALF],
                                    start=True, stop=True)
                ins.then_inc(ss_done, 1)

            def block_mm(n, bank, tokens, first, last, s=None, new=None):
                s = n % CUT if s is None else s
                pe.wait_ge(w_hi, n + 1)
                pe.wait_ge(w_lo, n + 1)
                steps = [(k, wp, xp) for k in range(8) for wp, parts in PASSES for xp in parts]
                if new is not None:
                    steps = [(k, wp, HI) for k in range(8) for wp in (HI, LO)] + [(k, HI, LO) for k in range(8)]
                for j, (k, wp, xp) in enumerate(steps):
                    if new is not None and wp == HI and xp == HI:
                        pe.wait_ge(h_hi, new + k + 1)
                    if new is not None and xp == LO:
                        pe.wait_ge(*low_part(new, k))
                    for a in range(2):
                        ins = pe.matmul(bank[:, a, 0:HALF], wR[:, s, wp, k, :],
                                        tokens(k, xp)[:, a * HALF:(a + 1) * HALF],
                                        start=(first and j == 0), stop=(last and j == len(steps) - 1))
                ins.then_inc(blk_done, 1)

            from_h = lambda k, xp: hR[:, k, xp, :]

            sum_squares(0, Q_CQ)
            for m in range(7):
                if m == 5:
                    sum_squares(1, Q_CKV)
                pe.wait_ge(tile_free, T_A + m - 1)
                block_mm(B_A + m, pair[(T_A + m) % 2], from_h, True, True, new=R_A if m == 0 else None)
            pe.wait_ge(var_ready, 2)
            sum_squares(2, Q_MLP0)
            pe.wait_ge(tile_free, T_B)

            pe.wait_ge(h_ready, H_CQ + 4)
            pe.wait_ge(kpe_raw, 1)
            pe.wait_ge(mask_cut, 2)

            def unit_scores(p, u):
                h, blk = UNITS[u]
                pe.wait_ge(p_exp, p * 8 + (before(u, 3) + CREDIT))
                n = (blk + 1) * P
                bank = score_banks[u % 3]
                pe.matmul(bank[:, 0:n], qT[0:HD, h, blk * P:(blk + 1) * P], kT[0:HD, h, 0:n],
                          start=True, stop=False)
                pe.matmul(bank[:, blk * P:n], ident16[:, :], cmask16[:, :], start=False, stop=True).then_inc(s_done, 1)

            def unit_turn(p, u):
                h, blk = UNITS[u]
                pe.wait_ge(p_sb, p * 8 + (u + 1))
                for t in range(blk + 1):
                    ins = transpose(bank23[:, u % 2, t * P:(t + 1) * P], probs[u % 3][:, t * P:(t + 1) * P])
                ins.then_inc(t_done, 1)

            def unit_values(p, u):
                h, blk = UNITS[u]
                pe.wait_ge(pt_sb, p * 8 + (u + 1))
                for t in range(blk + 1):
                    ins = pe.matmul(bank45[64 * h:64 * h + 64, 0, blk * P:(blk + 1) * P],
                                    V[:, t, 64 * h:64 * h + 64], probT[:, u % 2, t, :],
                                    start=(t == 0), stop=(t == blk))
                ins.then_inc(pv_done, 1)

            with pe.Fori(0, PAIRS) as p:
                pe.wait_ge(hw_in, p * 96 + 96)
                pe.wait_ge(hw_swap, p * 2 + 2)
                for h in range(2):
                    for a in range(2):
                        for k in range(4):
                            ins = pe.matmul(pair[h][:, a, 0:HALF], wq[:, k, h, :], cqT[:, k, a * HALF:(a + 1) * HALF],
                                            start=(k == 0), stop=(k == 3))
                    ins.then_inc(q_done, 1)
                pe.wait_ge(h_ready, H_CKV + 2)
                pe.wait_ge(o_sb, p * 2 + CREDIT)
                for r in range(2):
                    ins = pe.matmul(bank45[:, 0, :], wkv[:, r, 0, :, :].rearrange("p h n -> p (h n)"), ckvT[:, r, 0:SEQ],
                                    start=(r == 0), stop=(r == 1))
                ins.then_inc(k_done, 1)
                for t in range(BLK):
                    for r in range(2):
                        ins = pe.matmul(bank45[:, 1, t * P:(t + 1) * P], ckvT[:, r, t * P:(t + 1) * P],
                                        wkv[:, r, 1, :, :].rearrange("p h n -> p (h n)"), start=(r == 0), stop=(r == 1))
                ins.then_inc(v_done, 1)
                for h in range(2):
                    for r in range(2):
                        ins = transpose(bank6[0:NOPE, (2 * h + r) * P:(2 * h + r + 1) * P], wkv[:, r, 0, h, :])
                ins.then_inc(uk_done, 1)
                pe.wait_ge(uk_sb, p + 1)
                pe.wait_ge(qn_sb, p * 2 + 2)
                pe.wait_ge(ql_sb, p * 4 + CREDIT)
                for h in range(2):
                    for r in range(2):
                        ins = pe.matmul(bank7[:, (2 * h + r) * NS:(2 * h + r + 1) * NS], ukT[0:NOPE, 2 * h + r, :],
                                        qT[0:NOPE, h, SEQ:N], start=True, stop=True)
                ins.then_inc(ql_done, 1)
                pe.wait_ge(qr_sb, p * 2 + 2)
                pe.wait_ge(k_sb, p * 2 + 2)
                unit_scores(p, 0)
                unit_scores(p, 1)
                for u in range(8):
                    if u + 2 < 8:
                        unit_scores(p, u + 2)
                    unit_turn(p, u)
                    if u == 0:
                        pe.wait_ge(v_sb, p + 1)
                    if u >= 1:
                        unit_values(p, u - 1)
                unit_values(p, 7)

            def turn_pages(b, par, g):
                if g % 2 == 0:
                    pe.wait_ge(page_in[par][g // 2], b * 32 + (64 - 32 * par))
                if g == 0:
                    pe.wait_ge(keys_in[par], b * 128 + (256 - 128 * par))
                if not (isinstance(b, int) and b == 0 and g < 2):
                    pe.wait_ge(ct_sb, b * 8 + (g - 1))
                    pe.wait_ge(kp_sb, b * 8 + (g - 1))
                for j in range(2):
                    for r in range(2):
                        transpose(bank01[:, g % 2, r * 256 + j * P:r * 256 + (j + 1) * P],
                                  pages[:, par, 2 * g + j, r * P:(r + 1) * P])
                for j in range(2):
                    ins = transpose(bank23[0:ROPE, g % 2, j * P:(j + 1) * P], KP[:, par, 2 * g + j, :])
                ins.then_inc(ct_done, 1)

            def group_scores(b, par, g):
                n = DEC_Q if g == 8 else 256
                bank = bank45[:, g % 2, 0:n]
                if g < 8:
                    pe.wait_ge(ct_sb, b * 8 + (g + 1))
                    pe.wait_ge(kp_sb, b * 8 + (g + 1))
                pe.wait_ge(sc_sb, b * 9 + (g - 1 if g >= 2 else 0) + CREDIT)
                new = b * DEC_Q
                for r in range(2):
                    if g < 8:
                        rhs = cT[:, g % 2, r, :]
                    elif isinstance(b, int):
                        rhs = ckvT[:, r, SEQ + new:SEQ + new + DEC_Q]
                    else:
                        rhs = ckvT[:, r, ds(new + SEQ, DEC_Q)]
                    pe.matmul(bank, QLb[:, par, r, :], rhs, start=(r == 0), stop=False)
                if g < 8:
                    rhs = kpT[0:ROPE, g % 2, :]
                elif isinstance(b, int):
                    rhs = kpeN[0:ROPE, new:new + DEC_Q]
                else:
                    rhs = kpeN[0:ROPE, ds(new, DEC_Q)]
                ins = pe.matmul(bank, QPb[0:ROPE, par, :], rhs, start=False, stop=(g < 8))
                if g == 8:
                    ins = pe.matmul(bank, ident[:, :], nmask[:, :], start=False, stop=True)
                ins.then_inc(sc_done, 1)

            def scores(b, par):
                pe.wait_ge(qb_ready, b * 2 + 2)
                turn_pages(b, par, 0)
                pe.wait_ge(olt_sb, b + (CREDIT - 1) if not isinstance(b, int) else max(b - 1, 0) + CREDIT)
                for g in range(9):
                    if g + 1 < 8:
                        turn_pages(b, par, g + 1)
                    group_scores(b, par, g)

            def values(b, par):
                pe.wait_ge(d_exp, b + 1)
                for j in range(5):
                    bank = [bank6, bank7][j % 2]
                    pe.wait_ge(dt_sb, b * 5 + max(j - 1, 0) + CREDIT)
                    if j < 4:
                        for t in range(4):
                            c0 = (4 * j + t) * P
                            ins = transpose(bank[:, t * P:(t + 1) * P], S[:, par, c0:c0 + P])
                    else:
                        ins = transpose(bank[0:DEC_Q, 0:P], S[:, par, PAST:PAST + DEC_Q])
                    ins.then_inc(dt_done, 1)
                pe.wait_ge(olt_sb, b + CREDIT)
                for g in range(PAGES):
                    if g % 4 == 0:
                        pe.wait_ge(dt_sb, b * 5 + (g // 4 + 1) + CREDIT)
                    ins = pe.matmul(bank23[:, 0, 0:256], PT[:, g, :], pages[:, par, g, :], start=(g == 0), stop=False)
                    if g % 4 == 3:
                        ins.then_inc(quarter_used, 1)
                pe.wait_ge(dt_sb, b * 5 + 5 + CREDIT)
                new = CN[0:DEC_Q, b, :] if isinstance(b, int) else CN[0:DEC_Q, ds(b, 1), :].rearrange("p o n -> p (o n)")
                pe.matmul(bank23[:, 0, 0:256], PTN[0:DEC_Q, :], new, start=False, stop=True).then_inc(ov_done, 1)
                pe.wait_ge(ol_sb, b + 1)
                for r in range(2):
                    ins = transpose(bank23[:, 1, r * P:(r + 1) * P], OLn[:, r * P:(r + 1) * P])
                ins.then_inc(olt_done, 1)

            pe.wait_ge(o_sb, 2 * PAIRS + CREDIT)
            pe.wait_ge(ql_sb, 4 * PAIRS + CREDIT)

            pe.wait_ge(h_ready, H_CKV + 2)
            pe.wait_ge(kpe_raw, 1)
            for j in range(BLK):
                if j >= 2:
                    pe.wait_ge(nat_sb, j - 1)
                for r in range(2):
                    transpose(pair[j % 2][:, 0, r * P:(r + 1) * P], ckvT[:, r, j * P:(j + 1) * P])
                transpose(pair[j % 2][:, 0, 256:256 + ROPE], kpR[64:96, j * P:(j + 1) * P]).then_inc(nat_done, 1)
            pe.wait_ge(nat_sb, 4)
            transpose(pair[0][0:NS, 0, 0:ROPE], kpR[64:96, SEQ:N]).then_inc(nat_done, 1)
            for j in range(4):
                for b in (2 * j, 2 * j + 1):
                    for r in range(2):
                        dst = [bank45[:, 0, :], bank45[:, 1, :], bank6[:, :], bank7[:, :]][j]
                        ins = transpose(dst[0:DEC_Q, (b % 2) * 256 + r * P:(b % 2) * 256 + (r + 1) * P],
                                        ckvT[:, r, SEQ + b * DEC_Q:SEQ + (b + 1) * DEC_Q])
                ins.then_inc(nat_done, 1)
            pe.wait_ge(nat_sb, 9)

            scores(0, 0)
            with pe.Fori(0, DEC_B // 2 - 1) as i:
                scores(i * 2 + 1, 1)
                values(i * 2, 0)
                scores(i * 2 + 2, 0)
                values(i * 2 + 1, 1)
            scores(DEC_B - 1, 1)
            values(DEC_B - 2, 0)
            values(DEC_B - 1, 1)
            pe.wait_ge(olt_sb, DEC_B + CREDIT)
            pe.wait_ge(wkvf_in, 16)
            for h in range(HEADS):
                for r in range(2):
                    ins = pe.matmul(bank01[64 * (h % 2):64 * (h % 2) + 64, 0, (h // 2) * NS:(h // 2 + 1) * NS],
                                    wkvf[:, r, h * P + NOPE:(h + 1) * P],
                                    OLT[:, r, :, :].rearrange("p b (q h) -> p b q h", h=HEADS)[:, :, :, h],
                                    start=(r == 0), stop=(r == 1))
            ins.then_inc(os_done, 1)

            for m in range(8):
                pe.wait_ge(tile_free, T_B + m - 1)
                block_mm(B_B + m, pair[(T_B + m) % 2], from_h, True, True, new=R_B if m == 0 else None)

            def mlp(i):
                for half in range(2):
                    n0, t0, z0 = B_MLP[i] + 32 * half, T_MLP[i] + 24 * half, 32 * i + 16 * half
                    with pe.Fori(0, 4) as it:
                        for s in range(4):
                            pe.wait_ge(tile_free, it * 4 + (t0 + s - 1))
                            block_mm(it * 4 + (n0 + s), pair[(t0 + s) % 2], from_h, True, True, (n0 + s) % CUT,
                                     new=R_MLP[i] if half == 0 and s == 0 else None)
                    pe.wait_ge(z_lo, z0 + 16 + CREDIT)
                    pe.wait_ge(z_hi, z0 + 16)
                    n0, t0 = n0 + 16, t0 + 16
                    with pe.Fori(0, 4) as it:
                        for s in range(4):
                            if s % 2 == 0:
                                pe.wait_ge(tile_free, it * 2 + (t0 + s // 2 - 1))
                            block_mm(it * 4 + (n0 + s), pair[(t0 + s // 2) % 2],
                                     lambda k, xp, c=s % 2: zR[:, 8 * c + k, xp, :],
                                     s % 2 == 0, s % 2 == 1, (n0 + s) % CUT)

            sum_squares(3, Q_MIX1)
            mlp(0)
            sum_squares(4, Q_MLP1)

            pe.wait_ge(h0_in, 32)
            pe.wait_ge(tile_free, T_GLU)
            for a in range(2):
                for t in range(2):
                    ins = transpose(bank6[:, (2 * a + t) * P:(2 * a + t + 1) * P], h0n[:, 2 * a + t, :])
            ins.then_inc(h0_done, 1)
            pe.wait_ge(bst_in, 16)
            pe.wait_ge(u_in[0], 16 * T)
            for j in range(11):
                if j == 5:
                    pe.wait_ge(u_in[1], 16 * T)
                qs = range(3 * j, min(3 * j + 3, GP))
                if j >= 2:
                    pe.wait_ge(xs_sb, j - 1)
                for q in qs:
                    for half in range(2):
                        for a in range(2):
                            ins = pe.matmul(bank01[64 * half:64 * half + 64, j % 2,
                                                   ((q % 3) * 2 + a) * NC:((q % 3) * 2 + a + 1) * NC],
                                            BC[:, a, q, 64 * half:64 * half + 64], U[:, 2 * q + half, :],
                                            start=True, stop=True)
                ins.then_inc(xs_done, 1)
            pe.wait_ge(cs_in, 16)
            pe.wait_ge(mi_in, 16 * T)
            pe.wait_ge(z_state, 1)

            def chunk_outputs(k):
                banks = pair[k % 2]
                if k >= 2:
                    pe.wait_ge(yc_sb, k - 1)
                for q4 in range(4):
                    for half in range(2):
                        q = 4 * k + q4
                        rows = slice(64 * half, 64 * half + 64)
                        out = banks[0:NC, half, q4 * P:(q4 + 1) * P]
                        pe.matmul(out, U[:, 2 * q + half, :], MI[:, 2 * q + half, :], start=True, stop=False)
                        for a in range(2):
                            ins = pe.matmul(out, Z[rows, :, a, q], BC[rows, a, q, :], start=False, stop=(a == 1))
                ins.then_inc(yc_done, 1)

            def outputs_by_channel(k):
                pe.wait_ge(yc_sb, k + 1)
                if k >= 1:
                    pe.wait_ge(yb_sb, k)
                for t in range(T):
                    ins = transpose(bank45[:, t // 4, (t % 4) * NC:(t % 4 + 1) * NC], yblk[0:NC, k % 2, t, :])
                ins.then_inc(yb_done, 1)

            chunk_outputs(0)
            pe.wait_ge(f_ready, 1)
            pe.wait_ge(h0_sb, 1)
            for a in range(2):
                for t in range(2):
                    transpose(bank7[:, (2 * a + t) * P:(2 * a + t + 1) * P],
                              XG[:, a, 1 + 4 * t:5 + 4 * t, :].rearrange("p c q -> p (c q)"))
                ins = transpose(bank6[0:GP, a * P:(a + 1) * P], XG[:, a, 0, :])
            ins.then_inc(f_done, 1)
            for k in range(KT):
                if k + 1 < KT:
                    chunk_outputs(k + 1)
                outputs_by_channel(k)

            pe.wait_ge(yc_sb, KT)
            with pe.Fori(0, 4) as it:
                for s in range(4):
                    if s % 2 == 0:
                        pe.wait_ge(sig_ready, it * 2 + (s // 2 + CREDIT))
                    else:
                        pe.wait_ge(tile_free, it * 4 + (T_GLU + s - 1))
                    block_mm(it * 4 + (B_GLU + s), pair[(T_GLU + s) % 2], from_h, True, True, (B_GLU + s) % CUT,
                             new=R_GLU if s == 0 else None)
            sum_squares(5, Q_FIN)
            mlp(1)
            sum_squares(6, Q_END)
            for j in range(BLK + 1):
                pe.wait_ge(tile_free, T_OUT + j - 1)
                rows = P if j < BLK else NS
                for k in range(KT):
                    if j == 0:
                        pe.wait_ge(h_ready, H_FIN + k + 1)
                    ins = transpose(pair[j % 2][0:rows, k // 4, (k % 4) * P:(k % 4 + 1) * P],
                                    hT[:, k, j * P:j * P + rows])
                ins.then_inc(tile_done, 1)


        @block.scalar
        def _(act):
            for s in (yt_sb, kd_sb):
                act.sem_inc(s, AHEAD)
            for s in (sig_ready, o_sb, p_exp, sc_sb, dt_sb):
                act.sem_inc(s, CREDIT)

            def copy(out, in_, scale=1.0):
                return act.activation(out, in_, ACT.Copy, scale=scale)

            def root(n):
                act.wait_ge(var_ready, n + 1)
                act.activation(rstd[:, :], rstd[:, :], ACT.Sqrt).then_inc(rstd_ready, 1)

            act.wait_ge(a_in, 16 * 3)
            act.activation(nat[0:GP, 2, 2:4], nat[0:GP, 2, 0:2], ACT.Exp).then_inc(aprep, 1)
            act.wait_ge(dprep, 1)
            act.activation(nat[0:GP, 25, :], nat[0:GP, 23, :], ACT.Exp)
            act.activation(nat[0:GP, 26, :], nat[0:GP, 24, :], ACT.Sin)
            act.activation(nat[0:GP, 27, :], nat[0:GP, 24, :], ACT.Sin, scale=0.5).then_inc(aprep, 1)
            act.wait_ge(const_in, 16 * 11)
            copy(ident16[:, :], ident[:, :]).then_inc(mask_cut, 1)
            copy(cmask16[:, :], cmask[:, :]).then_inc(mask_cut, 1)
            act.wait_ge(vec_done, 1)
            copy(vecs[:, :], bank6[:, 0:VROWS]).then_inc(vec_sb, 1)
            for k in range(KT):
                act.wait_ge(tile_done, k + 1)
                copy(xT[:, k, 0:SEQ], pair[k % 2][:, 0, :])
                copy(xT[:, k, SEQ:N], pair[k % 2][:, 1, 0:NS]).then_inc(tile_free, 1)
                act.wait_ge(tile_free, k + 1)
                if k >= 2:
                    act.wait_ge(sq_used, k - 1)
                act.activation(sq[:, k % 2, :], xT[:, k, :], ACT.Square).then_inc(sq_ready, 1)

            act.wait_ge(c_done, 1)
            for half in range(2):
                for a in range(2):
                    copy(Cp[64 * half:64 * half + 64, a, :, :].rearrange("p (b q) o -> p b q o", b=2),
                               [bank23, bank45][a][0:ST, :, :].rearrange("p b (q h o) -> p h b q o", h=2, o=GS)[:, half])
                ins = copy(nCi[64 * half:64 * half + 64, :, :].rearrange("p (b q) o -> p b q o", b=2),
                           bank45[0:ST, :, :].rearrange("p b (q h o) -> p h b q o", h=2, o=GS)[:, half], -1.0)
            ins.then_inc(c_sb, 1)
            act.wait_ge(pw_done, 1)
            copy(PW[:, 0:16, :].rearrange("p a q -> p (a q)"), bank01[:, 0, :])
            copy(PW[:, 16:20, :].rearrange("p a q -> p (a q)"), bank01[:, 1, 0:4 * GP]).then_inc(pw_sb, 1)
            with act.Fori(0, GP // QC // 2) as i:
                for par in range(2):
                    c = i * 2 + par
                    kdc = kdcs[par]
                    act.wait_ge(yt_done, c + 1)
                    act.wait_ge(prep_left, c + (AHEAD - 1))
                    copy(bstcs[par].rearrange("p a q n -> p a (q n)"), y_banks[par][:, :, :]).then_inc(yt_sb, 1)
                    act.wait_ge(kd_done, c + (1 + AHEAD))
                    for half in range(2):
                        ins = copy(kdc[0:GS, :, half, :],
                                   kd_banks[par][half][0:GS, :].rearrange("p (q n) -> p q n", q=QC))
                    ins.then_inc(kd_sb, 1)

            def cut_block(n, raw=None, place=None):
                raw = n % RAW if raw is None else raw
                place = n % CUT if place is None else place
                q = n // RAW if isinstance(n, int) else None
                act.wait_ge(w_loaded[raw], loads(n, raw))
                if not (isinstance(n, int) and n < CUT):
                    act.wait_ge(blk_done, n - CUT + 1)
                act.activation(wR[:, place, HI, :, :], wraw[:, raw, :, :], ACT.Copy).then_inc(w_hi, 1)

            def cut_tokens(n0, ready, r0):
                for k in range(KT):
                    act.wait_ge(ready, r0 + k + 1 if r0 is not None else 1)
                    act.activation(hR[:, k, HI, :], hT[:, k, :], ACT.Copy).then_inc(h_hi, 1)

            cut_block(0)
            root(0)
            act.wait_ge(prep_left, GP // QC + AHEAD)
            cut_tokens(R_A, h_ready, H_MIX0)
            for m in range(6):
                n = Q_CQ + m
                cut_block(m + 1)
                act.wait_ge(blk_done, B_A + m + 1)
                act.wait_ge(sq_used, n - 1)
                src = pair[(T_A + m) % 2][:, :, 0:HALF]
                act.activation(halves(sq[:, n % 2, :]), src, ACT.Square).then_inc(sq_ready, 1)
                copy(halves(cqT[:, m, :] if m < 4 else ckvT[:, m - 4, :]), src).then_inc(tile_free, 1)
            root(1)
            root(2)
            def unit_exp(p, u):
                n = (UNITS[u][1] + 1) * P
                act.wait_ge(nm_ready, p * 8 + (u + 1))
                act.wait_ge(t_done, p * 8 + (before(u, 3) + CREDIT))
                act.activation(probs[u % 3][:, 0:n], score_banks[u % 3][:, 0:n], ACT.Exp,
                               bias=stat[:, u % 3:u % 3 + 1],
                               accum_out=stat[:, 3 + u % 3:4 + u % 3]).then_inc(p_exp, 1)

            def unit_turned(p, u):
                blk = UNITS[u][1]
                act.wait_ge(t_done, p * 8 + (u + 1 + CREDIT))
                act.wait_ge(pv_done, p * 8 + (before(u, 2) + CREDIT))
                copy(probT[:, u % 2, 0:blk + 1, :].rearrange("p t n -> p (t n)"), bank23[:, u % 2, 0:(blk + 1) * P])\
                    .then_inc(pt_sb, 1)

            def head_out(p, h):
                act.wait_ge(pv_done, p * 8 + (4 * h + 4) + CREDIT)
                copy(hT[64 * h:64 * h + 64, ds(p, 1), 0:SEQ].rearrange("p o n -> p (o n)"),
                     bank45[64 * h:64 * h + 64, 0, :]).then_inc(o_sb, 1)

            with act.Fori(0, PAIRS) as p:
                for h in range(2):
                    act.wait_ge(q_done, p * 2 + (h + 1))
                    copy(halves(qT[0:NOPE, h, :]), pair[h][0:NOPE, :, 0:HALF], SCALE).then_inc(qn_sb, 1)
                act.wait_ge(k_done, p + 1)
                copy(kT[0:NOPE, 0, :], bank45[0:NOPE, 0, :]).then_inc(k_sb, 1)
                copy(kT[0:NOPE, 1, :], bank45[NOPE:P, 0, :]).then_inc(k_sb, 1)
                act.wait_ge(uk_done, p + 1 + CREDIT)
                copy(ukT[0:NOPE, :, :].rearrange("p a n -> p (a n)"), bank6[0:NOPE, :]).then_inc(uk_sb, 1)
                unit_exp(p, 0)
                unit_exp(p, 1)
                for u in range(8):
                    unit_turned(p, u)
                    if u + 2 < 8:
                        unit_exp(p, u + 2)
                    if u == 5:
                        head_out(p, 0)
                head_out(p, 1)

            for j in range(BLK):
                act.wait_ge(nat_done, j + 1)
                copy(ckvNat[:, j // 2, j % 2, :], pair[j % 2][:, 0, 0:KV_D])
                copy(kpeNat[:, j, :], pair[j % 2][:, 0, KV_D:KV_D + ROPE]).then_inc(nat_sb, 1)
            act.wait_ge(nat_done, 5)
            copy(kpeNat[0:NS, BLK, :], pair[0][0:NS, 0, 0:ROPE]).then_inc(nat_sb, 1)
            for j, src in enumerate((bank45[:, 0, :], bank45[:, 1, :], bank6[:, :], bank7[:, :])):
                act.wait_ge(nat_done, 6 + j)
                copy(CN[0:DEC_Q, 2 * j:2 * j + 2, :].rearrange("p b n -> p (b n)"), src[0:DEC_Q]).then_inc(nat_sb, 1)

            def pages_turned(b, par, g):
                act.wait_ge(ct_done, b * 8 + (g + 1))
                act.wait_ge(sc_done, b * 9 + max(g - 1, 0) + CREDIT)
                copy(cT[:, g % 2, :, :].rearrange("p r n -> p (r n)"), bank01[:, g % 2, :]).then_inc(ct_sb, 1)

            def scores(b, par):
                for g in range(9):
                    if g == 0:
                        pages_turned(b, par, 0)
                        act.wait_ge(dt_done, b * 5 - 5 + CREDIT if not isinstance(b, int) else
                                    max(b - 1, 0) * 5 + CREDIT)
                    if g + 1 < 8:
                        pages_turned(b, par, g + 1)
                    n = DEC_Q if g == 8 else 256
                    act.wait_ge(sc_done, b * 9 + (g + 1) + CREDIT)
                    copy(S[:, par, g * 256:g * 256 + n], bank45[:, g % 2, 0:n]).then_inc(sc_sb, 1)

            def softmax(b, par):
                act.wait_ge(dm_ready, b + 1)
                act.activation(S[:, par, :], S[:, par, :], ACT.Exp, bias=stat[:, 24 + par:25 + par],
                               accum_out=stat[:, 26 + par:27 + par]).then_inc(d_exp, 1)

            def values(b, par):
                act.wait_ge(ov_done, b + CREDIT)
                for j in range(5):
                    act.wait_ge(dt_done, b * 5 + (j + 1) + CREDIT)
                    bank = [bank6, bank7][j % 2]
                    if j < 4:
                        copy(PT[:, 4 * j:4 * j + 4, :].rearrange("p g n -> p (g n)"), bank[:, :]).then_inc(dt_sb, 1)
                    else:
                        copy(PTN[0:DEC_Q, :], bank[0:DEC_Q, 0:P]).then_inc(dt_sb, 1)

            cut_block(B_B)
            scores(0, 0)
            softmax(0, 0)
            with act.Fori(0, DEC_B // 2 - 1) as i:
                scores(i * 2 + 1, 1)
                values(i * 2, 0)
                softmax(i * 2 + 1, 1)
                scores(i * 2 + 2, 0)
                values(i * 2 + 1, 1)
                softmax(i * 2 + 2, 0)
            scores(DEC_B - 1, 1)
            values(DEC_B - 2, 0)
            softmax(DEC_B - 1, 1)
            values(DEC_B - 1, 1)
            act.wait_ge(os_done, 1)
            copy(hT[:, :, SEQ:N], bank01[:, 0, :].rearrange("p (k n) -> p k n", k=KT)).then_inc(os_sb, 1)

            def mlp(i):
                for half in range(2):
                    n0, t0, z0 = B_MLP[i] + 32 * half, T_MLP[i] + 24 * half, 32 * i + 16 * half
                    act.wait_ge(tile_free, t0)
                    with act.Fori(0, 4) as it:
                        for s in range(4):
                            n = it * 4 + (n0 + s)
                            cut_block(n + 1, (n0 + s + 1) % RAW, (n0 + s + 1) % CUT)
                            act.wait_ge(blk_done, n + 1)
                            act.wait_ge(z_ready, it * 4 + max(z0 + s - 1, 0) + CREDIT)
                            act.activation(halves(tmpa[:, s % 2, :]), pair[(t0 + s) % 2][:, :, 0:HALF], ACT.Relu)\
                                .then_inc(tile_free, 1)
                            act.wait_ge(z_ready, it * 4 + (z0 + s + 1 + CREDIT))
                            act.activation(part_of(zR, it * 4 + s, HI), hid[:, s % 2, :], ACT.Copy).then_inc(z_hi, 1)
                    n0, t0 = n0 + 16, t0 + 16
                    q0 = (Q_MIX1, Q_FIN)[i]

                    def down(it):
                        for j in range(2):
                            for c in range(2):
                                n = it * 4 + (n0 + 2 * j + c)
                                if isinstance(n, int) and n + 1 == B_END:
                                    continue
                                cut_block(n + 1, (n0 + 2 * j + c + 1) % RAW, (n0 + 2 * j + c + 1) % CUT)
                            if half == 1:
                                act.wait_ge(tile_free, it * 2 + (t0 + j + 1))
                                act.wait_ge(sq_used, it * 2 + (q0 + j - 1))
                                act.activation(sq[:, j, :], row(xT, it * 2 + j), ACT.Square).then_inc(sq_ready, 1)

                    final = (i, half) == (1, 1)
                    with act.Fori(0, 4 - final) as it:
                        down(it)
                    if final:
                        down(3)

            cut_tokens(R_B, os_sb, None)
            act.wait_ge(out_sem, 16 * 5)
            for m in range(KT):
                cut_block(B_B + m + 1)
                act.wait_ge(tile_free, T_B + m + 1)
                act.wait_ge(sq_used, Q_MLP0 + m - 1)
                act.activation(sq[:, m % 2, :], xT[:, m, :], ACT.Square).then_inc(sq_ready, 1)
            root(3)
            cut_tokens(R_MLP[0], h_ready, H_MLP0)
            mlp(0)
            root(4)

            for j in range(11):
                n = min(3, GP - 3 * j)
                act.wait_ge(xs_done, j + 1)
                src = bank01[:, j % 2, 0:n * 2 * NC].rearrange("p (q a c) -> p q a c", q=n, a=2)
                copy(Z[:, 1:PC, :, 3 * j:3 * j + n].rearrange("p c a q -> p q a c"), src[:, :, :, 0:PC - 1])
                copy(XF[:, :, :, 3 * j:3 * j + n].rearrange("p c a q -> p q a c"), src[:, :, :, PC - 1:NC])\
                    .then_inc(xs_sb, 1)

            def chunk_outputs(k):
                act.wait_ge(yc_done, k + 1)
                if k >= 2:
                    act.wait_ge(yb_done, k - 1)
                for half in range(2):
                    ins = copy(yblk[0:NC, k % 2, :, :].rearrange("p t (q a o) -> p a q t o", a=2, o=GS)[:, half],
                               pair[k % 2][0:NC, half, :].rearrange("p (q t o) -> p q t o", q=4, o=GS))
                ins.then_inc(yc_sb, 1)

            chunk_outputs(0)
            act.wait_ge(f_done, 1)
            copy(tmpa[:, 1, 0:512], bank7[:, :]).then_inc(f_sb, 1)
            copy(sq[0:GP, 0, 0:2 * P], bank6[0:GP, 0:2 * P]).then_inc(f_sb, 1)
            for k in range(KT):
                if k + 1 < KT:
                    chunk_outputs(k + 1)
                act.wait_ge(yb_sb, k + 1)
                act.activation(hT[:, k, :], hT[:, k, :], ACT.Gelu_apprx_tanh).then_inc(g_sb, 1)
            act.wait_ge(yc_done, KT)
            cut_tokens(R_GLU, g_sb, 0)
            act.wait_ge(out_sem, 16 * 9)
            for m in range(KT):
                cut_block(B_GLU + 2 * m + 1)
                act.wait_ge(blk_done, B_GLU + 2 * m + 1)
                if m >= 2:
                    act.wait_ge(x_new, m - 1)
                act.activation(halves(tmpa[:, m % 2, :]), pair[T_GLU % 2][:, :, 0:HALF], ACT.Sigmoid)\
                    .then_inc(sig_ready, 1)
                cut_block(B_GLU + 2 * m + 2)
                act.wait_ge(x_new, m + 1)
                act.wait_ge(sq_used, Q_MLP1 + m - 1)
                act.activation(sq[:, m % 2, :], xT[:, m, :], ACT.Square).then_inc(sq_ready, 1)
            root(5)
            cut_tokens(R_MLP[1], h_ready, H_MLP1)
            mlp(1)
            root(6)
            for j in range(BLK + 1):
                rows = P if j < BLK else NS
                act.wait_ge(tile_done, 8 + j + 1)
                copy(arena[0:rows, j * D:(j + 1) * D].rearrange("p (a n) -> p a n", a=2), pair[j % 2][0:rows, :, :])\
                    .then_inc(tile_free, 1)

        @block.vector
        def _(dve):
            for s in (ql_sb, olt_sb, ca_ready, z_ready):
                dve.sem_inc(s, CREDIT)
            step = Tally(dstep)

            def own(ins):
                step.add()
                return ins.then_inc(dstep, 1)

            def settle():
                dve.wait_ge(dstep, step.now())

            tt = dve.tensor_tensor

            def clear_acc():
                own(dve.memset(acc[:, :], 0.0))
                settle()

            def add_square(n, place):
                dve.wait_ge(sq_ready, n + 1)
                dve.wait_ge(sq_used, n)
                tt(acc[:, :], acc[:, :], sq[:, place, :], ALU.add).then_inc(sq_used, 1)

            def norm(n, width, tiles, src, dst, v, by_token=False):
                dve.wait_ge(ss_done, n + 1)
                own(dve.tensor_scalar(halves(rstd[:, :]), bank45[:, :, 0:HALF], 1.0 / width, EPS, ALU.mult, ALU.add))
                settle()
                dve.reciprocal(rstd[:, :], rstd[:, :]).then_inc(var_ready, 1)
                dve.wait_ge(rstd_ready, n + 1)
                for k in range(tiles):
                    out, x, r = dst[:, k, :], src[:, k, :], rstd[:, :]
                    if by_token:
                        out = out.rearrange("p (s c) -> p s c", s=T)
                        x = x.rearrange("p (c s) -> p s c", s=T)
                        r = r.rearrange("p (c s) -> p s c", s=T)
                    dve.scalar_tensor_tensor(out=out, in0=x, scalar=vecs[:, v + k:v + k + 1], in1=r,
                                             op0=ALU.mult, op1=ALU.mult).then_inc(h_ready, 1)

            def rest_of(n0):
                for k in range(LOW_SPLIT, KT):
                    dve.wait_ge(h_hi, n0 + k + 1)
                    tt(hR[:, k, LO, :], hT[:, k, :], hR[:, k, HI, :].bitcast(F32), ALU.subtract).then_inc(h_lo_v, 1)

            def cut_rest(n, raw=None, place=None):
                raw = n % RAW if raw is None else raw
                place = n % CUT if place is None else place
                dve.wait_ge(w_hi, n + 1)
                tt(wR[:, place, LO, :, :], wraw[:, raw, :, :], wR[:, place, HI, :, :].bitcast(F32), ALU.subtract)\
                    .then_inc(w_lo, 1)

            nt = lambda a: nat[0:GP, a, :]
            ar, ai, dtr, th, er, sn, sh, t1, t2 = (nt(0), nt(1), nt(23), nt(24), nt(25), nt(26), nt(27), nt(28), nt(29))
            pr, pi = (lambda k: nt(3 + k)), (lambda k: nt(12 + k))
            dve.wait_ge(aprep, 1)
            dt_ = nat[0:GP, 2, 2:4].unsqueeze(2).to_broadcast([GP, 2, ST])
            two = lambda a: a.rearrange("p (a n) -> p a n", a=2)
            own(tt(two(dtr), two(ar), dt_, ALU.mult))
            own(tt(two(th), two(ai), dt_, ALU.mult))
            settle()
            magic = 1.5 * 2.0 ** 23
            own(dve.tensor_scalar(t1, th, 1.0 / (2 * math.pi), magic, ALU.mult, ALU.add))
            settle()
            own(dve.tensor_scalar(t1, t1, -magic, None, ALU.add))
            settle()
            c1, c2 = 6.28125, 2029.0 / 2 ** 20
            for part in (c1, c2, 2 * math.pi - c1 - c2):
                own(dve.scalar_tensor_tensor(out=th, in0=t1, scalar=-part, in1=th, op0=ALU.mult, op1=ALU.add))
                settle()
            lim = 3.1415925
            dve.tensor_scalar(th, th, lim, -lim, ALU.min, ALU.max).then_inc(dprep, 1)
            own(dve.memset(pr(0), 1.0))
            own(dve.memset(pi(0), 0.0))
            dve.wait_ge(aprep, 2)
            own(tt(t1, sh, sh, ALU.mult))
            own(tt(pi(1), er, sn, ALU.mult))
            settle()
            own(dve.tensor_scalar(t1, t1, -2.0, 1.0, ALU.mult, ALU.add))
            settle()
            own(tt(pr(1), er, t1, ALU.mult))
            settle()
            fr, fi = nt(21), nt(22)
            own(tt(t1, ar, ar, ALU.mult))
            own(tt(t2, ai, ai, ALU.mult))
            own(dve.tensor_scalar(er, pr(1), -1.0, None, ALU.add))
            settle()
            own(tt(t1, t1, t2, ALU.add))
            own(tt(sn, er, ar, ALU.mult))
            own(tt(sh, pi(1), ai, ALU.mult))
            settle()
            own(dve.reciprocal(t1, t1))
            own(tt(sn, sn, sh, ALU.add))
            settle()
            own(tt(fr, sn, t1, ALU.mult))
            own(tt(t2, pi(1), ar, ALU.mult))
            own(tt(th, er, ai, ALU.mult))
            settle()
            own(tt(t2, t2, th, ALU.subtract))
            settle()
            own(tt(fi, t2, t1, ALU.mult))
            settle()
            clear_acc()
            for k in range(KT):
                add_square(k, k % 2)
            for n in (1, 2, 4):
                many = lambda j, k: nat[0:GP, j + k:j + k + n, :]
                top = lambda j: nat[0:GP, j + n:j + n + 1, :].to_broadcast([GP, n, P])
                tv = [tm[0:GP, j, 0:n * P].rearrange("p (k n) -> p k n", n=P) for j in range(4)]
                re, im = 3, 12
                own(tt(tv[0], top(re), many(re, 1), ALU.mult))
                own(tt(tv[1], top(im), many(im, 1), ALU.mult))
                own(tt(tv[2], top(re), many(im, 1), ALU.mult))
                own(tt(tv[3], top(im), many(re, 1), ALU.mult))
                settle()
                own(tt(many(re, n + 1), tv[0], tv[1], ALU.subtract))
                own(tt(many(im, n + 1), tv[2], tv[3], ALU.add))
                settle()
            dve.tensor_copy(t1, pi(8)).then_inc(y_ready, 1)
            dve.wait_ge(pw_sb, 1)
            own(dve.tensor_copy(a8[:, 0, :], PW[:, 8, :]))
            own(dve.tensor_copy(a8[:, 1, :], PW[:, 8, :]))
            own(dve.tensor_copy(a8[:, 2, :], PW[:, 17, :]))
            dve.wait_ge(c_sb, 1)

            def complex_product(out_re, out_im, xr, xi, yr, yi, shape):
                n = 1
                for d in shape:
                    n *= d
                names = dict(zip("abc", shape[1:]))
                tv = lambda j: tm[:, j, 0:n].rearrange("p (z a b) -> p z a b", a=shape[1], b=shape[2]) \
                    if len(shape) == 3 else tm[:, j, 0:n].rearrange("p (z a) -> p z a", a=shape[1])
                own(tt(tv(0), xr, yr, ALU.mult))
                own(tt(tv(1), xi, yi, ALU.mult))
                own(tt(tv(2), xr, yi, ALU.mult))
                own(tt(tv(3), xi, yr, ALU.mult))
                settle()
                own(tt(out_re, tm[:, 0, 0:n], tm[:, 1, 0:n], ALU.subtract))
                return tt(out_im, tm[:, 2, 0:n], tm[:, 3, 0:n], ALU.add)

            flat = lambda a: a.rearrange("p q k o -> p (q k o)")
            with dve.Fori(0, GP // QC // 2) as i:
                step.enter(i, 28)
                for par in range(2):
                    c = i * 2 + par
                    bb, Y, CA = bbs[par], Ys[par], CAs[par]
                    chunk = lambda t, a: t[:, a, ds(c * QC, QC), :]
                    pw = lambda a, k, n: PW[:, 9 * a:9 * a + k, ds(c * QC, QC)].rearrange("p k q -> p q k")\
                        .unsqueeze(3).to_broadcast([P, QC, k, n])
                    f = lambda a: PW[:, 18 + a, ds(c * QC, QC)].unsqueeze(2).to_broadcast([P, QC, GS])
                    dve.wait_ge(kd_done, c + (AHEAD - 1))
                    dve.wait_ge(ca_ready, c + CREDIT)
                    dve.wait_ge(prep_left, c + (AHEAD - 1))
                    own(complex_product(bb[:, 0].rearrange("p q i -> p (q i)"), bb[:, 1].rearrange("p q i -> p (q i)"),
                                        f(0), f(1), chunk(Bn, 0), chunk(Bn, 1), (QC, GS)))
                    settle()
                    b_ = lambda a: bb[:, a].unsqueeze(2).to_broadcast([P, QC, T, GS])
                    own(complex_product(Y[:, 0].rearrange("p q n -> p (q n)"), Y[:, 1].rearrange("p q n -> p (q n)"),
                                        pw(0, T, GS), pw(1, T, GS), b_(0), b_(1), (QC, T, GS)))
                    settle()
                    c_ = lambda a: chunk(Cp, a).unsqueeze(2).to_broadcast([P, QC, 9, GS])
                    dve.tensor_scalar(bb[:, 1].rearrange("p q i -> p (q i)"), bb[:, 1].rearrange("p q i -> p (q i)"),
                                      1.0, None, ALU.mult).then_inc(y_ready, 1)
                    tv = lambda j: tm[:, j, 0:QC * 9 * GS].rearrange("p (z a b) -> p z a b", a=9, b=GS)
                    own(tt(tv(0), pw(0, 9, GS), c_(0), ALU.mult))
                    own(tt(tv(1), pw(1, 9, GS), c_(1), ALU.mult))
                    settle()
                    tt(flat(CA[:, 0]), tm[:, 0, :], tm[:, 1, :], ALU.subtract).then_inc(ca_ready, 1)
                step.leave(GP // QC // 2)

            cut_rest(0)
            norm(0, D, KT, xT, hT, V_MIX)
            rest_of(R_A)
            own(dve.memset(acc[:, :], 0.0))
            settle()
            for m in range(4):
                cut_rest(m + 1)
                add_square(Q_CQ + m, m % 2)
            dve.wait_ge(ss_done, 2)
            own(dve.memset(acc[:, :], 0.0))
            settle()
            for m in range(2):
                cut_rest(5 + m)
                add_square(Q_CKV + m, m % 2)
            norm(1, QL_D, 4, cqT, cqT, V_Q)
            dve.wait_ge(blk_done, B_B)
            bank = pair[(T_A + 6) % 2]
            own(tt(halves(tmpa[64:96, 0, :]), bank[64:96, :, 0:HALF], halves(ropek[64:96, :]), ALU.mult))
            tt(halves(tmpa[64:96, 1, :]), bank[96:128, :, 0:HALF], halves(ropek[96:128, :]), ALU.mult)\
                .then_inc(tile_free, 1)
            settle()
            dve.wait_ge(tile_free, T_B)
            own(tt(kpR[64:96, :], tmpa[64:96, 0, :], tmpa[64:96, 1, :], ALU.add))
            settle()
            for h in range(2):
                own(dve.tensor_copy(kT[64:96, h, :], kpR[64:96, 0:SEQ]))
            dve.tensor_copy(kpeN[0:ROPE, :], kpR[64:96, SEQ:N]).then_inc(kpe_raw, 1)
            norm(2, KV_D, 2, ckvT, ckvT, V_KV)


            def unit_max(p, u):
                n = (UNITS[u][1] + 1) * P
                dve.wait_ge(s_done, p * 8 + (u + 1))
                dve.wait_ge(p_exp, p * 8 + (before(u, 3) + CREDIT))
                dve.tensor_reduce(stat[:, u % 3:u % 3 + 1], score_banks[u % 3][:, 0:n], AX.X, ALU.max, negate=True)\
                    .then_inc(nm_ready, 1)

            def unit_scale(p, u):
                n = (UNITS[u][1] + 1) * P
                dve.wait_ge(p_exp, p * 8 + (u + 1 + CREDIT))
                c = u % 3
                own(dve.reciprocal(stat[:, 32 + c:33 + c], stat[:, 3 + c:4 + c]))
                settle()
                dve.tensor_scalar(probs[c][:, 0:n], probs[c][:, 0:n], stat[:, 32 + c:33 + c], None, ALU.mult)\
                    .then_inc(p_sb, 1)

            with dve.Fori(0, PAIRS) as p:
                step.enter(p, 4 + 8)
                for h in range(2):
                    dve.wait_ge(q_done, p * 2 + (h + 1))
                    own(tt(halves(tmpa[64:96, 0, :]), pair[h][64:96, :, 0:HALF], halves(ropeq[64:96, :]), ALU.mult))
                    own(tt(halves(tmpa[64:96, 1, :]), pair[h][96:128, :, 0:HALF], halves(ropeq[96:128, :]), ALU.mult))
                    settle()
                    tt(qT[64:96, h, :], tmpa[64:96, 0, :], tmpa[64:96, 1, :], ALU.add).then_inc(qr_sb, 1)
                    dve.wait_ge(qr_sb, p * 2 + (h + 1))
                dve.wait_ge(v_done, p + 1)
                dve.tensor_copy(V[:, :, :].rearrange("p t n -> p (t n)"), bank45[:, 1, :]).then_inc(v_sb, 1)
                for h in range(2):
                    dve.tensor_copy(QPE[0:ROPE, :].rearrange("p (t h) -> p t h", h=HEADS)[:, :, ds(p * 2 + h, 1)],
                                    qT[64:96, h, SEQ:N].unsqueeze(2)).then_inc(ql_sb, 1)
                dve.wait_ge(ql_done, p + 1)
                for h in range(2):
                    dve.tensor_copy(QL[:, :, :].rearrange("p r (t h) -> p r t h", h=HEADS)[:, :, :, ds(p * 2 + h, 1)],
                                    bank7[:, 2 * h * NS:(2 * h + 2) * NS].rearrange("p (r t o) -> p r t o", r=2, o=1))\
                        .then_inc(ql_sb, 1)
                unit_max(p, 0)
                unit_max(p, 1)
                for u in range(8):
                    unit_scale(p, u)
                    if u + 2 < 8:
                        unit_max(p, u + 2)
                step.leave(PAIRS)

            def keys_turned(b, par, g):
                dve.wait_ge(ct_done, b * 8 + (g + 1))
                dve.wait_ge(sc_done, b * 9 + max(g - 1, 0) + CREDIT)
                dve.tensor_copy(kpT[0:ROPE, g % 2, :], bank23[0:ROPE, g % 2, 0:256]).then_inc(kp_sb, 1)

            def scores(b, par):
                keys_turned(b, par, 0)
                for g in range(9):
                    if g + 1 < 8:
                        keys_turned(b, par, g + 1)
                    n = DEC_Q if g == 8 else 256
                    dve.wait_ge(sc_sb, b * 9 + (g + 1) + CREDIT)
                    dve.tensor_reduce(stat[:, 6 + 9 * par + g:7 + 9 * par + g], S[:, par, g * 256:g * 256 + n],
                                      AX.X, ALU.max).then_inc(gm_done, 1)
                dve.wait_ge(gm_done, b * 9 + 9)
                dve.tensor_reduce(stat[:, 24 + par:25 + par], stat[:, 6 + 9 * par:15 + 9 * par], AX.X, ALU.max,
                                  negate=True).then_inc(dm_ready, 1)

            def values(b, par):
                dve.wait_ge(d_exp, b + 1)
                dve.reciprocal(stat[:, 28 + par:29 + par], stat[:, 26 + par:27 + par]).then_inc(rl_ready, 1)
                dve.wait_ge(rl_ready, b + 1)
                dve.wait_ge(ov_done, b + 1 + CREDIT)
                dve.wait_ge(olt_done, b + CREDIT)
                dve.tensor_scalar(OLn[:, :], bank23[:, 0, 0:256], stat[:, 28 + par:29 + par], None, ALU.mult)\
                    .then_inc(ol_sb, 1)
                dve.wait_ge(olt_done, b + 1 + CREDIT)
                out = OLT[:, :, b, :] if isinstance(b, int) else OLT[:, :, ds(b, 1), :].rearrange("p r o n -> p r (o n)")
                dve.tensor_copy(out, bank23[:, 1, 0:256].rearrange("p (r n) -> p r n", r=2)).then_inc(olt_sb, 1)

            cut_rest(B_B)
            scores(0, 0)
            with dve.Fori(0, DEC_B // 2 - 1) as i:
                scores(i * 2 + 1, 1)
                values(i * 2, 0)
                scores(i * 2 + 2, 0)
                values(i * 2 + 1, 1)
            scores(DEC_B - 1, 1)
            values(DEC_B - 2, 0)
            values(DEC_B - 1, 1)

            def residual(m, j):
                x = row(xT, m)
                tt(halves(x), halves(x), pair[j][:, :, 0:HALF], ALU.add).then_inc(tile_free, 1)

            def mlp(i):
                for half in range(2):
                    n0, t0, z0 = B_MLP[i] + 32 * half, T_MLP[i] + 24 * half, 32 * i + 16 * half
                    with dve.Fori(0, 4) as it:
                        for s in range(4):
                            n = it * 4 + (n0 + s)
                            cut_rest(n + 1, (n0 + s + 1) % RAW, (n0 + s + 1) % CUT)
                            dve.wait_ge(tile_free, it * 4 + (t0 + s + 1))
                            dve.wait_ge(z_lo, it * 4 + max(z0 + s - 1, 0) + CREDIT)
                            tt(hid[:, s % 2, :], tmpa[:, s % 2, :], tmpa[:, s % 2, :], ALU.mult).then_inc(z_ready, 1)
                    n0, t0 = n0 + 16, t0 + 16
                    q0 = (Q_MIX1, Q_FIN)[i]
                    if half == 1:
                        clear_acc()

                    def down(it):
                        for j in range(2):
                            for c in range(2):
                                n = it * 4 + (n0 + 2 * j + c)
                                if isinstance(n, int) and n + 1 == B_END:
                                    continue
                                cut_rest(n + 1, (n0 + 2 * j + c + 1) % RAW, (n0 + 2 * j + c + 1) % CUT)
                            dve.wait_ge(blk_done, it * 4 + (n0 + 2 * j + 2))
                            residual(it * 2 + j, (t0 + j) % 2)
                            if half == 1:
                                add_square(it * 2 + (q0 + j), j)

                    final = (i, half) == (1, 1)
                    with dve.Fori(0, 4 - final) as it:
                        down(it)
                    if final:
                        down(3)

            clear_acc()
            rest_of(R_B)
            for m in range(KT):
                cut_rest(B_B + m + 1)
                dve.wait_ge(blk_done, B_B + m + 1)
                residual(m, (T_B + m) % 2)
                add_square(Q_MLP0 + m, m % 2)
            norm(3, D, KT, xT, hT, V_MLP)
            rest_of(R_MLP[0])
            mlp(0)
            norm(4, D, KT, xT, hT, V_MIX + 8, by_token=True)

            for a in range(2):
                own(dve.tensor_copy(E[:, a, 0, :], a8[:, 2 * a, :]))
            settle()
            for n in (1, 2, 4):
                shape = [P, n, GP]
                tv = [yblk[:, 1, j, 0:n * GP].rearrange("p (j q) -> p j q", q=GP) for j in range(4)]
                top = lambda a: E[:, a, n - 1:n, :].to_broadcast(shape)
                low = lambda a: E[:, a, 0:n, :]
                for j, (x, y) in enumerate(((0, 0), (1, 1), (0, 1), (1, 0))):
                    own(tt(tv[j], top(x), low(y), ALU.mult))
                settle()
                own(tt(E[:, 0, n:2 * n, :], tv[0], tv[1], ALU.subtract))
                own(tt(E[:, 1, n:2 * n, :], tv[2], tv[3], ALU.add))
                settle()
            own(dve.memset(Z[:, 0, :, :], 0.0))
            dve.wait_ge(h0_done, 1)
            dve.tensor_copy(Z[:, PC:NC, :, :].rearrange("p b a q -> p a b q"),
                            bank6[:, :].rearrange("p (a b q) -> p a b q", a=2, b=DEC_B)).then_inc(h0_sb, 1)
            dve.wait_ge(xs_sb, 11)
            settle()
            Z1 = Z[:, 1:PC + 1, :, :].rearrange("p (s j) a q -> p s j a q", j=SPAN)
            Z0 = Z[:, 0:PC, :, :].rearrange("p (s j) a q -> p s j a q", j=SPAN)
            temps = yblk[:, 1, :, :].rearrange("p t n -> p (t n)")

            def advance(z, nxt, power, spans):
                n = spans * 2 * GP
                shape = [P, spans, 2, GP]
                tv = lambda j: temps[:, j * 512:j * 512 + n].rearrange("p (s a q) -> p s a q", a=2, q=GP)
                e = lambda a: E[:, a, power - 1, :].unsqueeze(1).unsqueeze(1).to_broadcast(shape)
                own(tt(tv(0), e(0), z, ALU.mult))
                own(tt(tv(1), e(1), z, ALU.mult))
                settle()
                own(tt(tv(0), tv(0), nxt, ALU.add))
                settle()
                own(tt(nxt[:, :, 0, :], tv(0)[:, :, 0, :], tv(1)[:, :, 1, :], ALU.subtract))
                own(tt(nxt[:, :, 1, :], tv(0)[:, :, 1, :], tv(1)[:, :, 0, :], ALU.add))
                settle()

            at = lambda j: Z1[:, :, ds(j, 1), :, :].rearrange("p s o a q -> p s (o a) q")
            with dve.Fori(0, SPAN - 2) as j:
                step.enter(j, 5)
                advance(at(j), at(j + 1), 1, SPANS)
                step.leave(SPAN - 2)
            advance(Z1[:, 0:SPANS - 1, SPAN - 2], Z1[:, 0:SPANS - 1, SPAN - 1], 1, SPANS - 1)
            end = lambda s: Z[:, ds(s * SPAN, 1), :, :]
            with dve.Fori(0, SPANS - 2) as s:
                step.enter(s, 5)
                advance(end(s + 1), end(s + 2), SPAN, 1)
                step.leave(SPANS - 2)
            big = [tmpa.rearrange("p a n -> p (a n)"), sq.rearrange("p a n -> p (a n)"), temps]
            for q0, q1 in ((0, GP // 2), (GP // 2, GP)):
                shape = [P, SPANS - 1, SPAN - 1, q1 - q0]
                n = shape[1] * shape[2] * shape[3]
                tv = [t[:, 0:n].rearrange("p (s j q) -> p s j q", j=SPAN - 1, q=q1 - q0) for t in big]
                e = lambda a: E[:, a, 0:SPAN - 1, q0:q1].unsqueeze(1).to_broadcast(shape)
                carry = lambda a: Z0[:, 1:SPANS, 0:1, a, q0:q1].to_broadcast(shape)
                z = lambda a: Z1[:, 1:SPANS, 0:SPAN - 1, a, q0:q1]
                own(tt(tv[0], e(0), carry(0), ALU.mult))
                own(tt(tv[1], e(1), carry(1), ALU.mult))
                own(tt(tv[2], e(0), carry(1), ALU.mult))
                settle()
                own(tt(z(0), z(0), tv[0], ALU.add))
                own(tt(z(1), z(1), tv[2], ALU.add))
                settle()
                own(tt(z(0), z(0), tv[1], ALU.subtract))
                own(tt(tv[0], e(1), carry(0), ALU.mult))
                settle()
                own(tt(z(1), z(1), tv[0], ALU.add))
                settle()
            dve.tensor_copy(temps[:, 0:GP], a8[:, 0, :]).then_inc(z_state, 1)
            M = DEC_B + 1
            last = Z[:, PC - 1:NC, :, :]
            w = yblk[:, 1, 1:6, :].rearrange("p t n -> p (t n)")[:, 0:2 * M * GP].rearrange("p (a c q) -> p a c q", a=2, q=GP)
            bc = lambda a: a8[:, a, :].unsqueeze(1).to_broadcast([P, M, GP])
            for a in range(2):
                own(tt(XG[:, a], last[:, :, a, :], bc(0), ALU.mult))
                own(tt(w[:, a], last[:, :, 1 - a, :], bc(2), ALU.mult))
            settle()
            for a in range(2):
                own(tt(XG[:, a], XG[:, a], XF[:, :, a, :], ALU.add))
            settle()
            own(tt(XG[:, 0], XG[:, 0], w[:, 0], ALU.subtract))
            own(tt(XG[:, 1], XG[:, 1], w[:, 1], ALU.add))
            settle()
            dve.tensor_copy(rstd[:, 0:1], a8[:, 0, 0:1]).then_inc(f_ready, 1)
            for part in range(2):
                dve.wait_ge(hd_out[part], 16 * 4)
            for k in range(KT):
                dve.wait_ge(yb_done, k + 1)
                dve.scalar_tensor_tensor(out=halves(hT[:, k, :]), in0=halves(hT[:, k, :]),
                                         scalar=vecs[:, V_D + k:V_D + k + 1], in1=bank45[:, :, 0:HALF],
                                         op0=ALU.mult, op1=ALU.add).then_inc(yb_sb, 1)
            clear_acc()
            rest_of(R_GLU)
            for m in range(KT):
                g = tmpa[:, m % 2, :]
                cut_rest(B_GLU + 2 * m + 1)
                cut_rest(B_GLU + 2 * m + 2)
                dve.wait_ge(sig_ready, m + 1 + CREDIT)
                dve.wait_ge(blk_done, B_GLU + 2 * m + 2)
                tt(halves(g), halves(g), pair[(T_GLU + 1) % 2][:, :, 0:HALF], ALU.mult).then_inc(tile_free, 2)
                dve.wait_ge(tile_free, T_GLU + 2 * m + 2)
                x = xT[:, m, :].rearrange("p (c s) -> p s c", s=T)
                tt(x, x, g.rearrange("p (s c) -> p s c", s=T), ALU.add).then_inc(x_new, 1)
                add_square(Q_MLP1 + m, m % 2)
            norm(5, D, KT, xT, hT, V_MLP + 8)
            rest_of(R_MLP[1])
            mlp(1)
            norm(6, D, KT, xT, hT, V_FIN)


_INS = ["x_prompt", "x_sample", "cache_ckv", "cache_kpe", "state_ssm_re", "state_ssm_im", "page_table",
        "norm_mix", "norm_mlp", "norm_final", "mla_w_in", "mla_q_norm", "mla_kv_norm", "mla_w_q_up",
        "mla_w_kv_up", "mla_w_o", "ssm_a_re", "ssm_a_im", "ssm_log_dt", "ssm_b_re", "ssm_b_im", "ssm_c_re",
        "ssm_c_im", "ssm_d", "ssm_w_glu", "mlp_w1", "mlp_w2"]
_OUTS = [("y_prompt", (1, SEQ, D)), ("y_sample", (DEC_B, DEC_Q, D)),
         ("prompt_ckv", (1, 1, SEQ, KV_D)), ("prompt_kpe", (1, 1, SEQ, ROPE)),
         ("prompt_ssm_re", (1, 1, GROUPS, ST)), ("prompt_ssm_im", (1, 1, GROUPS, ST)),
         ("sample_ckv", (1, DEC_B, DEC_Q, KV_D)), ("sample_kpe", (1, DEC_B, DEC_Q, ROPE)),
         ("sample_ssm_re", (1, DEC_B, GROUPS, ST)), ("sample_ssm_im", (1, DEC_B, GROUPS, ST))]


def constants():
    import numpy as np
    half = ROPE // 2
    pos = np.concatenate([np.arange(SEQ), PAST + np.tile(np.arange(DEC_Q), DEC_B)]).astype(np.float32)
    inv = np.float32(10000.0) ** (-np.arange(half, dtype=np.float32) / np.float32(half))
    ang = inv[:, None] * pos[None, :]
    cos, sin = np.cos(ang), np.sin(ang)
    rope = np.concatenate([cos, cos, -sin, sin]).astype(np.float32)
    q, k = np.arange(P)[:, None], np.arange(P)[None, :]
    return {
        "c_ident": np.eye(P, dtype=np.float32),
        "c_ropeq": (rope * np.float32(SCALE)).astype(np.float32),
        "c_ropek": rope,
        "c_cmask": np.where(q >= k, 0.0, NEG).astype(np.float32),
        "c_nmask": np.where(q // HEADS >= np.arange(DEC_Q)[None, :], 0.0, NEG).astype(np.float32),
    }


def kernel(**inputs):
    import numpy as np
    import concourse.bacc as bacc
    from concourse.bass_utils import run_bass_kernel_spmd

    nc = bacc.Bacc("TRN2", target_bir_lowering=False, num_devices=1)
    arrays, ins, outs = {}, {}, {}
    for name, a in [(n, inputs[n]) for n in _INS] + list(constants().items()):
        a = np.ascontiguousarray(a)
        arrays[f"in_{name}"] = a
        ins[name] = nc.dram_tensor(f"in_{name}", a.shape, mybir.dt.from_np(a.dtype), kind="ExternalInput").ap()
    for name, shape in _OUTS:
        outs[name] = nc.dram_tensor(f"out_{name}", shape, F32, kind="ExternalOutput").ap()
    build(nc, ins, outs)
    r = run_bass_kernel_spmd(nc, [arrays], core_ids=[0])
    return tuple(r.results[0][f"out_{name}"] for name, _ in _OUTS)
```
